# Optimizing a Trainium2 kernel written in Bass

```python
import jax, jax.numpy as jnp
from jax import lax
import numpy as np

D_MODEL = 1024
BATCH = 1
SEQ = 1024
DEPTH = 1

MEM_LEN = 256
D_MIX = D_MODEL
GLA_WIDTH = D_MIX // 2
GLA_HEADS = 4
GLA_DV = GLA_WIDTH // GLA_HEADS
GLA_DK = GLA_DV // 2
GLA_KEY_WIDTH = GLA_HEADS * GLA_DK
GATE_RANK = 16
GATE_TAU = 16.0
CHUNK = 64
CONV_WIDTH = D_MIX - GLA_WIDTH
CONV_KERNEL = 31
IN_SIZES = (GLA_KEY_WIDTH, GLA_KEY_WIDTH, GLA_WIDTH, GLA_WIDTH, GATE_RANK, GATE_RANK, 2 * CONV_WIDTH)
IN_WIDTH = sum(IN_SIZES)
XATTN_HEADS = 4
XATTN_DH = D_MODEL // XATTN_HEADS
N_EXPERTS = 32
TOP_K = 4
D_FF_EXPERT = D_MODEL
SWIGLU_ALPHA = 1.702
SWIGLU_LIMIT = 7.0
MOE_BLOCK = 128
RMS_EPS = 1e-6
LN_EPS = 1e-5

kernel_name = "hybrid_gla_conformer_moe_encoder"

def rms_norm(x, g):
    xf = x.astype(jnp.float32)
    y = xf * lax.rsqrt(jnp.mean(xf * xf, axis=-1, keepdims=True) + RMS_EPS)
    return (y * g.astype(jnp.float32)).astype(x.dtype)

def layer_norm(x, g, b):
    xf = x.astype(jnp.float32)
    mu = jnp.mean(xf, axis=-1, keepdims=True)
    var = jnp.mean(jnp.square(xf - mu), axis=-1, keepdims=True)
    y = (xf - mu) * lax.rsqrt(var + LN_EPS)
    return (y * g.astype(jnp.float32) + b.astype(jnp.float32)).astype(x.dtype)

def gla_direction(q, k, v, log_a, strict):
    B, H, S, dk = q.shape
    dv = v.shape[-1]
    n = S // CHUNK
    qc = q.astype(jnp.float32).reshape(B, H, n, CHUNK, dk)
    kc = k.astype(jnp.float32).reshape(B, H, n, CHUNK, dk)
    vc = v.astype(jnp.float32).reshape(B, H, n, CHUNK, dv)
    bcum = jnp.cumsum(log_a.astype(jnp.float32).reshape(B, H, n, CHUNK, dk), axis=-2)
    b_last = bcum[..., -1:, :]
    idx = jnp.arange(CHUNK)
    mask = (idx[:, None] > idx[None, :]) if strict else (idx[:, None] >= idx[None, :])
    diff = bcum[..., :, None, :] - bcum[..., None, :, :]
    decay = jnp.exp(jnp.where(mask[:, :, None], diff, -jnp.inf))
    scores = jnp.einsum('bhnid,bhnjd,bhnijd->bhnij', qc, kc, decay)
    o_intra = jnp.einsum('bhnij,bhnjv->bhniv', scores, vc)
    u = jnp.einsum('bhncd,bhncv->bhndv', kc * jnp.exp(b_last - bcum), vc)
    a_chunk = jnp.exp(b_last[..., 0, :])

    def step(state, inp):
        a, uc = inp
        return a[..., None] * state + uc, state

    init = jnp.zeros((B, H, dk, dv), jnp.float32)
    _, s_in = lax.scan(step, init, (jnp.moveaxis(a_chunk, 2, 0), jnp.moveaxis(u, 2, 0)))
    s_in = jnp.moveaxis(s_in, 0, 2)
    o_inter = jnp.einsum('bhncd,bhndv->bhncv', qc * jnp.exp(bcum), s_in)
    return (o_intra + o_inter).reshape(B, H, S, dv)

def gla_group(q, k, v, r, gf, gb, w2_f, b_f, w2_b, b_b, norm_g):
    B, S, _ = q.shape

    def heads(t, d):
        return t.reshape(B, S, GLA_HEADS, d).transpose(0, 2, 1, 3)

    qh = heads(q, GLA_DK) * (GLA_DK ** -0.5)
    kh = heads(k, GLA_DK)
    vh = heads(v, GLA_DV)
    la_f = heads(jax.nn.log_sigmoid((gf @ w2_f + b_f).astype(jnp.float32)) / GATE_TAU, GLA_DK)
    la_b = heads(jax.nn.log_sigmoid((gb @ w2_b + b_b).astype(jnp.float32)) / GATE_TAU, GLA_DK)
    flip = lambda t: t[:, :, ::-1]
    o_f = gla_direction(qh, kh, vh, la_f, strict=False)
    o_b = flip(gla_direction(flip(qh), flip(kh), flip(vh), flip(la_b), strict=True))
    o = rms_norm(o_f + o_b, norm_g)
    o = o.transpose(0, 2, 1, 3).reshape(B, S, GLA_WIDTH)
    return (o * jax.nn.silu(r.astype(jnp.float32))).astype(q.dtype)

def conv_group(glu_in, conv_w, conv_b, ln_g, ln_b):
    a, g = jnp.split(glu_in, 2, axis=-1)
    u = a * jax.nn.sigmoid(g)
    pad = (CONV_KERNEL - 1) // 2
    y = lax.conv_general_dilated(
        u, conv_w[:, None, :].astype(u.dtype), window_strides=(1,), padding=[(pad, pad)],
        dimension_numbers=('NWC', 'WIO', 'NWC'), feature_group_count=CONV_WIDTH) + conv_b
    return jax.nn.silu(layer_norm(y, ln_g, ln_b))

def memory_cross_attention(h, m, wq, wk, wv, wo):
    B, S, _ = h.shape
    M = m.shape[1]
    q = (h @ wq).reshape(B, S, XATTN_HEADS, XATTN_DH)
    k = (m @ wk).reshape(B, M, XATTN_HEADS, XATTN_DH)
    v = (m @ wv).reshape(B, M, XATTN_HEADS, XATTN_DH)
    s = jnp.einsum('bqhd,bkhd->bhqk', q, k).astype(jnp.float32) * (XATTN_DH ** -0.5)
    p = jax.nn.softmax(s, axis=-1).astype(v.dtype)
    o = jnp.einsum('bhqk,bkhd->bqhd', p, v).reshape(B, S, D_MODEL)
    return o @ wo

def moe_ffn(h, router_w, router_b, w_up, b_up, w_down, b_down):
    B, S, D = h.shape
    T = B * S
    ht = h.reshape(T, D)
    logits = (ht @ router_w + router_b).astype(jnp.float32)
    top_vals, top_idx = lax.top_k(logits, TOP_K)
    gates = jax.nn.softmax(top_vals, axis=-1)
    A = T * TOP_K
    flat_e = top_idx.reshape(A)
    flat_tok = jnp.arange(A, dtype=jnp.int32) // TOP_K
    order = jnp.argsort(flat_e, stable=True)
    sorted_e = flat_e[order]
    sorted_tok = flat_tok[order]
    counts = jnp.bincount(flat_e, length=N_EXPERTS)
    padded = ((counts + MOE_BLOCK - 1) // MOE_BLOCK) * MOE_BLOCK
    starts = jnp.cumsum(counts) - counts
    pends = jnp.cumsum(padded)
    pstarts = pends - padded
    rank = jnp.arange(A, dtype=jnp.int32) - starts[sorted_e]
    dest = pstarts[sorted_e] + rank
    n_blocks = (A + N_EXPERTS * (MOE_BLOCK - 1) + MOE_BLOCK - 1) // MOE_BLOCK
    n_rows = n_blocks * MOE_BLOCK
    xs = jnp.zeros((n_rows, D), ht.dtype).at[dest].set(ht[sorted_tok])
    block_start = jnp.arange(n_blocks, dtype=pends.dtype) * MOE_BLOCK
    block_e = jnp.clip(jnp.searchsorted(pends, block_start, side='right'), 0, N_EXPERTS - 1)

    def expert_block(args):
        xb, e = args
        gu = xb @ w_up[e] + b_up[e]
        x_glu = jnp.minimum(gu[:, :D_FF_EXPERT], SWIGLU_LIMIT)
        x_lin = jnp.clip(gu[:, D_FF_EXPERT:], -SWIGLU_LIMIT, SWIGLU_LIMIT)
        hid = x_glu * jax.nn.sigmoid(SWIGLU_ALPHA * x_glu) * (x_lin + 1)
        return hid @ w_down[e] + b_down[e]

    ys = lax.map(expert_block, (xs.reshape(n_blocks, MOE_BLOCK, D), block_e)).reshape(n_rows, D)
    w_sorted = gates.reshape(A)[order].astype(ys.dtype)
    out = jax.ops.segment_sum(ys[dest] * w_sorted[:, None], sorted_tok, num_segments=T)
    return out.reshape(B, S, D).astype(h.dtype)

def setup_inputs(seed: int = 0) -> dict:
    key = jax.random.key(seed)
    ks = jax.random.split(key, 32)
    f32 = jnp.float32
    nrm = lambda k, shape, s: jax.random.normal(k, shape, f32) * s
    L = DEPTH
    return {
        "x": nrm(ks[0], (BATCH, SEQ, D_MODEL), 1.0),
        "mem": nrm(ks[1], (BATCH, MEM_LEN, D_MODEL), 1.0),
        "norm_mix_g": 1.0 + nrm(ks[2], (L, D_MODEL), 0.02),
        "w_in": nrm(ks[3], (L, D_MODEL, IN_WIDTH), D_MODEL ** -0.5),
        "gate_w2_fwd": nrm(ks[4], (L, GATE_RANK, GLA_KEY_WIDTH), GATE_RANK ** -0.5),
        "gate_b_fwd": nrm(ks[5], (L, GLA_KEY_WIDTH), 0.1),
        "gate_w2_bwd": nrm(ks[6], (L, GATE_RANK, GLA_KEY_WIDTH), GATE_RANK ** -0.5),
        "gate_b_bwd": nrm(ks[7], (L, GLA_KEY_WIDTH), 0.1),
        "gla_norm_g": 1.0 + nrm(ks[8], (L, GLA_DV), 0.02),
        "conv_w": nrm(ks[9], (L, CONV_KERNEL, CONV_WIDTH), CONV_KERNEL ** -0.5),
        "conv_b": nrm(ks[10], (L, CONV_WIDTH), 0.02),
        "conv_ln_g": 1.0 + nrm(ks[11], (L, CONV_WIDTH), 0.02),
        "conv_ln_b": nrm(ks[12], (L, CONV_WIDTH), 0.02),
        "w_out": nrm(ks[13], (L, D_MIX, D_MODEL), D_MIX ** -0.5),
        "norm_xattn_g": 1.0 + nrm(ks[14], (L, D_MODEL), 0.02),
        "norm_mem_g": 1.0 + nrm(ks[15], (L, D_MODEL), 0.02),
        "xattn_wq": nrm(ks[16], (L, D_MODEL, D_MODEL), D_MODEL ** -0.5),
        "xattn_wk": nrm(ks[17], (L, D_MODEL, D_MODEL), D_MODEL ** -0.5),
        "xattn_wv": nrm(ks[18], (L, D_MODEL, D_MODEL), D_MODEL ** -0.5),
        "xattn_wo": nrm(ks[19], (L, D_MODEL, D_MODEL), D_MODEL ** -0.5),
        "norm_ffn_g": 1.0 + nrm(ks[20], (L, D_MODEL), 0.02),
        "router_w": nrm(ks[21], (L, D_MODEL, N_EXPERTS), D_MODEL ** -0.5),
        "router_b": nrm(ks[22], (L, N_EXPERTS), 0.01),
        "exp_w_up": nrm(ks[23], (L, N_EXPERTS, D_MODEL, 2 * D_FF_EXPERT), D_MODEL ** -0.5),
        "exp_b_up": nrm(ks[24], (L, N_EXPERTS, 2 * D_FF_EXPERT), 0.02),
        "exp_w_down": nrm(ks[25], (L, N_EXPERTS, D_FF_EXPERT, D_MODEL), D_FF_EXPERT ** -0.5),
        "exp_b_down": nrm(ks[26], (L, N_EXPERTS, D_MODEL), 0.02),
        "final_norm_g": 1.0 + nrm(ks[27], (D_MODEL,), 0.02),
    }

def reference(x, mem, norm_mix_g, w_in, gate_w2_fwd, gate_b_fwd, gate_w2_bwd, gate_b_bwd,
              gla_norm_g, conv_w, conv_b, conv_ln_g, conv_ln_b, w_out, norm_xattn_g,
              norm_mem_g, xattn_wq, xattn_wk, xattn_wv, xattn_wo, norm_ffn_g, router_w,
              router_b, exp_w_up, exp_b_up, exp_w_down, exp_b_down, final_norm_g):
    splits = []
    off = 0
    for size in IN_SIZES[:-1]:
        off += size
        splits.append(off)
    for l in range(DEPTH):
        h = rms_norm(x, norm_mix_g[l])
        q, k, v, r, gf, gb, glu = jnp.split(h @ w_in[l], splits, axis=-1)
        a_out = gla_group(q, k, v, r, gf, gb, gate_w2_fwd[l], gate_b_fwd[l],
                          gate_w2_bwd[l], gate_b_bwd[l], gla_norm_g[l])
        b_out = conv_group(glu, conv_w[l], conv_b[l], conv_ln_g[l], conv_ln_b[l])
        x = x + (jnp.concatenate([a_out, b_out], axis=-1) @ w_out[l]).astype(x.dtype)
        h = rms_norm(x, norm_xattn_g[l])
        m = rms_norm(mem, norm_mem_g[l])
        x = x + memory_cross_attention(h, m, xattn_wq[l], xattn_wk[l], xattn_wv[l],
                                       xattn_wo[l]).astype(x.dtype)
        h = rms_norm(x, norm_ffn_g[l])
        x = x + moe_ffn(h, router_w[l], router_b[l], exp_w_up[l], exp_b_up[l],
                        exp_w_down[l], exp_b_down[l]).astype(x.dtype)
    return rms_norm(x, final_norm_g)


_drawn_inputs = setup_inputs


def setup_inputs(seed=0):
    import zlib

    import numpy as np

    out = dict(_drawn_inputs(seed))
    spreads = {}
    factors = {'norm_xattn_g': 4.807,
     'norm_mem_g': 3.534,
     'exp_b_up': 5.799,
     'exp_b_down': 17.812,
     'final_norm_g': 9.719,
     'norm_ffn_g': 3.727,
     'router_b': 6.42}
    for name, (base, spread) in spreads.items():
        noise = np.random.default_rng([zlib.crc32(name.encode()), seed]).standard_normal(out[name].shape)
        drawn = base * np.exp(spread * noise) if base else spread * noise
        out[name] = __import__('jax').numpy.asarray(drawn.astype(out[name].dtype))
    for name, factor in factors.items():
        out[name] = (out[name] * factor).astype(out[name].dtype)
    return out
```

```python
from contextlib import ExitStack

import concourse.bass as bass
from concourse import mybir

F = mybir.dt.float32
FR = mybir.dt.float32r
BF = mybir.dt.bfloat16
I32 = mybir.dt.int32
U32 = mybir.dt.uint32
U8 = mybir.dt.uint8
ALU = mybir.AluOpType
ACT = mybir.ActivationFunctionType
X = mybir.AxisListType.X

P = 128
S = 1024
D = 1024
KT = D // P
TT = S // P
MT = 2
GH, GDV, GDK = 4, 128, 64
GK = GH * GDK
GW = GH * GDV
CW_ = 512
CT = CW_ // P
TAPS = 31
PAD = TAPS // 2
RANK = 16
TAU = 16.0
XH = 4
XDH = D // XH
E = 32
TOPK = 4
FF = 1024
ALPHA, LIMIT = 1.702, 7.0
RMS_EPS, LN_EPS = 1e-6, 1e-5
Q0, K0, V0, R0 = 0, GK, 2 * GK, 2 * GK + GW
G0 = R0 + GW
A0 = G0 + 2 * RANK
B0 = A0 + CW_
NBLK = (S * TOPK + E * (P - 1) + P - 1) // P
NB = 72
RT_M, RT_GD = 9, 17
LEVELS = [64, 32, 16, 8, 4, 2, 1]
KIB = 1024
BASE = 16512


def build(nc, A):
    with ExitStack() as ctx:
        def sb(name, shape, dt, kib):
            return nc.alloc_sbuf_tensor_at(name, shape, dt, offset=BASE + int(kib * KIB))

        def sem(name):
            return ctx.enter_context(nc.semaphore(name))

        arena = ctx.enter_context(nc.sbuf_tensor("arena", [P, 212800], U8))
        assert arena is not None
        PS = ctx.enter_context(nc.psum_tensor("PS", [P, 8, 512], F))

        NR = 4
        ring = sb("ring", [P, NR, KT, 256], F, 0)
        hT = sb("hT", [P, KT, S], F, 32)
        o_gla = sb("o_gla", [P, TT, GW], F, 32)
        EX = sb("EX", [P, 2, S], F, 48)
        KQ = sb("KQ", [P, 2, S], F, 56)
        KEt = sb("KEt", [P, 4, 512], F, 48)
        SR = sb("SR", [P, TT, GW], F, 48)
        xres = sb("xres", [P, TT, D], F, 64)
        qT = sb("qT", [P, 2, S], F, 64)
        kT = sb("kT", [P, 2, S], F, 72)
        v_tm = sb("v_tm", [P, TT, GW], F, 80)
        r_tm = sb("r_tm", [P, TT, GW], F, 96)
        UW = S + 2 * PAD
        u_pad = sb("u_pad", [P, CT, UW], F, 112)
        qxT = sb("qxT", [P, KT, S], F, 96)
        mT = sb("mT", [P, KT, MT * P], F, 112)
        sig = sb("sig", [P, S], F, 129)
        yT = sb("yT", [P, CT, S], F, 133)
        mem_tm = sb("mem_tm", [P, MT, D], F, 133)
        Bf = sb("Bf", [P, S], F, 149)
        Rb = sb("Rb", [P, S], F, 153)
        Ssc = sb("Ssc", [P, 2, TT, P], F, 157)
        ST = sb("ST", [P, 2, TT, P], F, 165)
        aT = sb("aT", [P, CT, S], F, 149)
        kx = sb("kx", [P, KT, MT * P], F, 173)
        vx = sb("vx", [P, MT, D], F, 181)
        XN = sb("XN", [P, 2, D], F, 189)
        gT = sb("gT", [2 * RANK, S], F, 189)
        pr = sb("pr", [P, 2, MT * P], F, 130)
        pT = sb("pT", [P, 2, MT, S], F, 133)
        oxT = sb("oxT", [P, KT, S], F, 32)
        ident = sb("ident", [P, P], F, 197)
        ones = sb("ones", [P, P], F, 197.5)
        before = sb("before", [P, P], F, 198)
        masks = sb("masks", [P, 7, P], U8, 198.5)
        W2 = sb("W2", [2 * RANK, 2, GK], F, 199.5)
        PV = sb("PV", [P, 64], F, 201.5)
        CWT = sb("CWT", [P, TAPS * CT], F, 201.75)
        ngb = sb("ngb", [P, GDV], F, 202.25)
        st8 = sb("st8", [P, 4, 32], F, 202.75)
        TTd = sb("TTd", [P, 2, 2, TT], F, 203.25)
        smx = sb("smx", [P, 4, 4], F, 203.4375)
        xor = sb("xor", [P, P], I32, 203.5)
        mtmp = sb("mtmp", [P, P], F, 204)
        PVr = sb("PVr", [64, P], F, 204.5)
        CWr = sb("CWr", [TAPS * CT, P], F, 205)
        pid = sb("pid", [P, 8], F, 205.5)
        iot = sb("iot", [P, P], F, 206)

        h3T = sb("h3T", [P, 2, KT, P], F, 96)
        rw = sb("rw", [P, KT, E], F, 104)
        rbb = sb("rbb", [P, E], F, 105)
        LG = sb("LG", [P, TT, E], F, 106)
        MX = sb("MX", [P, TT, 8], F, 107)
        IX = sb("IX", [P, TT, 8], U32, 107.25)
        IXf = sb("IXf", [P, TT, 8], F, 107.5)
        gsum = sb("gsum", [P, 2, TT], F, 107.75)
        OH = sb("OH", [P, TT, TOPK, E], F, 108)
        M = sb("M", [P, TT, E], F, 112)
        slot0 = sb("slot0", [P, TT, E], F, 113)
        ex1 = sb("ex1", [P, 6, E], F, 114)
        exi = sb("exi", [P, 2, E], I32, 114.75)
        tmpA = sb("tmpA", [P, NB * E], F, 116)
        rowhot = sb("rowhot", [P, 2, TOPK, P], F, 125)
        blkhot = sb("blkhot", [P, 2, TOPK, NB], F, 129)
        GD = sb("GD", [P, TT, E], F, 132)
        GDT = sb("GDT", [E, S], F, 133)
        bdn = sb("bdn", [E, D], F, 137)
        di = sb("di", [P, 3, TT * TOPK], I32, 141)
        df = sb("df", [P, 3, TT * TOPK], F, 141.5)
        gfb = sb("gfb", [P, D], F, 184)
        bstage = sb("bstage", [P, 2 * FF], F, 152)
        Gt = sb("Gt", [P, TT, TOPK], F, 198.5)
        rowof = sb("rowof", [P, TT * TOPK], U32, 198.75)
        TM = sb("TM", [P, NB], U32, 199)
        EB = sb("EB", [P, NB], F, 199.5)
        BEI = sb("BEI", [P, NB], I32, 200)
        usedb = sb("usedb", [P, 1], I32, 200.5)
        idxc = sb("idxc", [P, 1], U32, 200.5625)
        pmod = sb("pmod", [P, 2], F, 200.625)
        pmi = sb("pmi", [P, 2], I32, 200.6875)
        SEL = sb("SEL", [P, P], BF, 200.75)
        BE = sb("BE", [P, NB], F, 201)
        NRAW, NSPL = 6, 4
        raw = sb("raw", [P, NRAW, 2 * FF], F, 0)
        whi = sb("whi", [P, NSPL, 2 * FF], FR, 96)
        wlo = sb("wlo", [P, NSPL, 2 * FF], FR, 128)
        xhi = sb("xhi", [P, KT, P], FR, 48)
        xlo = sb("xlo", [P, KT, P], FR, 52)
        hhi = sb("hhi", [P, KT, P], FR, 56)
        hlo = sb("hlo", [P, KT, P], FR, 60)
        xs = sb("xs", [P, D], F, 160)
        glu = sb("glu", [P, FF], F, 164)
        hid = sb("hid", [P, FF], F, 168)
        sgm = sb("sgm", [P, FF], F, 172)
        yb = sb("yb", [P, D], F, 176)
        bup = sb("bup", [P, 2 * FF], BF, 180)
        yg = sb("yg", [P, 8, D], F, 0)
        fo = sb("fo", [P, 2, D], F, 32)
        h3_dram = nc.dram_tensor("h3_scratch", (S, D), F, kind="Internal").ap()
        ys_dram = nc.dram_tensor("ys_scratch", (NBLK * P, D), F, kind="Internal").ap()

        s_par = sem("params_loaded")
        s_const = sem("constants_built")
        s_mask = sem("masks_built")
        s_w2z = sem("w2_zeroed")
        s_pvt = sem("vectors_transposed")
        s_pvc = sem("vectors_ready")
        s_ring = [sem(f"chunk_loaded{i}") for i in range(NR)]
        s_xld = [sem(f"x_loaded{i}") for i in range(4)]
        norms = {}
        for n in ("m", "x", "y", "z"):
            norms[n] = {k: sem(f"norm_{n}_{k}") for k in
                        ("stats_by_scalar", "stats_by_vector", "scaled", "turned") + ("drained",) * (n != "z")}
        norms["m"]["loaded"] = sem("memory_loaded")
        s_mm = {k: sem(f"{k}_product") for k in ("mem", "in", "out", "q", "o")}
        s_dr = {k: sem(f"{k}_drained") for k in ("mem", "in", "out", "q", "o")}
        s_pad = sem("margins_zeroed")
        s_u = sem("glu_ready")
        s_cv = sem("conv_tap")
        s_lnp, s_lna, s_lnv = sem("ln_by_tensor"), sem("ln_by_scalar"), sem("ln_by_vector")
        s_z, s_zabs, s_zln, s_zmin, s_la, s_scan, s_tot, s_rb, s_dec = (
            sem(n) for n in ("gate_product", "gate_abs", "gate_softplus", "gate_min", "log_decay", "scanned",
                             "totals", "suffix_ready", "window_decay"))
        s_sub, s_ex, s_kq, s_gram, s_sel = (
            sem(n) for n in ("exponent_ready", "decay_ready", "decayed_kq", "gram_product", "scores_selected"))
        s_ket, s_kev, s_U, s_st, s_st0, s_op, s_oe = (
            sem(n) for n in ("k_turned", "k_token_major", "window_update", "state_ready", "state_zero", "gla_product",
                             "gla_drained"))
        s_ov, s_oa, s_at, s_ae = (sem(n) for n in ("o_norm_by_vector", "o_norm_by_scalar", "a_turned", "a_ready"))
        s_sc, s_sv, s_pe, s_pt, s_pc, s_av, s_ax = (
            sem(n) for n in ("xscores", "softmax_by_vector", "xprob", "xprob_turned", "xprob_T", "xvalue", "xout"))
        s_xre = sem("x_reloaded")
        s_out = [sem(f"out_stored{i}") for i in range(2)]
        s_rpar, s_ffg, s_h3s = sem("router_loaded"), sem("final_gain_loaded"), [sem(f"h3_stored{i}") for i in range(2)]
        s_h3e, s_lgp, s_lg, s_top, s_rt = (sem(n) for n in ("h3_turned_out", "logit_product", "logits", "top8", "routing_step"))
        s_gx, s_rk, s_rkr, s_oh, s_tm, s_gdt, s_gde, s_bd, s_bdr = (
            sem(n) for n in ("gate_exp", "rank_product", "rank_read", "row_onehot", "token_map_product",
                             "gates_turned", "gates_turned_out", "bias_down_product", "bias_down_added"))
        s_bup, s_tab, s_rmi = sem("bias_parts"), sem("tables_ready"), sem("partition_ids")
        s_raw = [sem(f"expert_chunk_loaded{i}") for i in range(NRAW)]
        s_whi, s_wlv, s_wlp, s_wmm = (sem(n) for n in ("chunk_hi", "chunk_lo_by_vector", "chunk_lo_by_pool",
                                                       "chunk_multiplied"))
        s_idx, s_xsl, s_xt, s_xhi, s_xlo = (sem(n) for n in ("index_column", "tokens_gathered", "tokens_turned",
                                                             "tokens_hi", "tokens_lo"))
        s_bsel, s_g, s_upr, s_sg, s_hid, s_ht, s_hhi, s_hlo = (
            sem(n) for n in ("bias_selector", "glu_clamped", "up_banks_read", "expert_sigmoid", "hidden", "hidden_turned", "hidden_hi", "hidden_lo"))
        s_yev, s_yst = sem("rows_drained"), sem("rows_stored")
        s_yg = [sem(f"rows_gathered{i}") for i in range(8)]
        s_ac, s_fa, s_fv, s_fo = (sem(n) for n in ("row_added", "final_by_scalar", "final_by_vector",
                                                   "final_scaled"))

        w_in, w_out = A["w_in"][0], A["w_out"][0]
        wq, wk, wv, wo = (A[f"xattn_w{c}"][0] for c in "qkvo")
        x_in = A["x"][0].rearrange("(t p) d -> p t d", p=P)
        mem_in = A["mem"][0].rearrange("(t p) d -> p t d", p=P)
        out_v = A["out"][0].rearrange("(t p) d -> p t d", p=P)

        chunks = ([(wk, 256 * c) for c in range(4)] + [(wv, 256 * c) for c in range(4)]
                  + [(w_in, G0), (w_in, A0), (w_in, B0), (w_in, A0 + 256), (w_in, B0 + 256),
                     (w_in, Q0), (w_in, K0), (w_in, V0), (w_in, V0 + 256), (w_in, R0), (w_in, R0 + 256)]
                  + [(w_out, 256 * c) for c in range(4)] + [(wq, 256 * c) for c in range(4)]
                  + [(wo, 256 * c) for c in range(4)])
        used = ([("mem", 2 * (c + 1)) for c in range(8)]
                + [("in", n) for n in (2, 6, 10, 14, 18, 22, 26, 34, 42, 50, 58)]
                + [("out", 8 * (c + 1)) for c in range(4)] + [("q", 4 * (c + 1)) for c in range(4)]
                + [("o", 8 * (c + 1)) for c in range(4)])
        GX, GM, GA, ZB, CB, LG_, LB = 0, 8, 16, 24, 28, 32, 36
        NPV = 40

        def bank_groups(n, width=512):
            return PS[:, n % 8, 0:width]

        w_up, w_dn = A["exp_w_up"][0], A["exp_w_down"][0]

        def chunk_slot(c, n):
            return (c - 4) % n

        def wait_lo(eng, t, c):
            if c % 3 == 0:
                eng.wait_ge(s_wlp, 4 * t + (c - 3) // 3)
            else:
                eng.wait_ge(s_wlv, 8 * t + (c - 3) - (c - 3) // 3)

        def wait_raw(eng, t, c):
            eng.wait_ge(s_raw[chunk_slot(c, NRAW)], 32 * t + 16 * ((c - 4) // 6 + 1))

        def wait_multiplied(eng, t, c):
            eng.wait_ge(s_wmm, 12 * t + c - 3)

        block = ctx.enter_context(nc.Block())

        @block.sync
        def _(sp):
            sp.dma_start(mem_tm[:], mem_in).then_inc(norms["m"]["loaded"], 16)
            for i in range(4):
                sp.dma_start(xres[:, 2 * i:2 * i + 2, :], x_in[:, 2 * i:2 * i + 2, :]).then_inc(s_xld[i], 16)
            for g, (w, c0) in enumerate(chunks):
                if g >= NR:
                    sp.wait_ge(s_mm[used[g - NR][0]], used[g - NR][1])
                sp.dma_start(ring[:, g % NR], w[:, c0:c0 + 256].rearrange("(k p) n -> p k n", p=P)
                             ).then_inc(s_ring[g % NR], 16)
                if g == 18 + NR:
                    sp.wait_ge(s_oe, 2 * 16)
                    sp.dma_start(xres[:], x_in).then_inc(s_xre, 16)
            for t in range(TT):
                sp.wait_ge(norms["z"]["scaled"], t + 1)
                sp.dma_start(h3_dram[P * t:P * (t + 1), :], XN[:, t % 2, :]).then_inc(s_h3s[t % 2], 16)
            sp.wait_ge(norms["z"]["scaled"], TT)
            sp.dma_start(gfb[:], A["final_norm_g"].partition_broadcast(P)).then_inc(s_ffg, 16)

            def load_chunk(t, c, e_up, e_dn, fresh=False):
                if not fresh:
                    wait_lo(sp, t, c - NRAW)
                if e_dn is None or c < 8:
                    k = c - 4 if e_dn is None and c >= 4 else c
                    src = w_up[bass.ds(e_up, 1), P * k:P * (k + 1), :].rearrange("e p n -> p (e n)")
                    dst_ = raw[:, chunk_slot(c, NRAW), :]
                else:
                    src = w_dn[bass.ds(e_dn, 1), 256 * (c - 8):256 * (c - 7), :].rearrange(
                        "e (k p) n -> p (e k) n", p=P)
                    dst_ = raw[:, chunk_slot(c, NRAW), :].rearrange("p (k n) -> p k n", k=2)
                sp.dma_start(dst_, src).then_inc(s_raw[chunk_slot(c, NRAW)], 16)

            def expert(t):
                return sp.value_load(BEI[0:1, bass.ds(t, 1)], min_val=0, max_val=E - 1)

            sp.wait_ge(s_tab, 1)
            used_ = sp.value_load(usedb[0:1, 0:1], min_val=1, max_val=NBLK)
            e0, e1 = expert(0), expert(1)
            for c in range(4, 12):
                load_chunk(0, c, e0, None, fresh=c < 4 + NRAW)
            for c in range(3):
                load_chunk(1, c, e1, None)
            with sp.Fori(1, NBLK + 1) as t:
                with sp.If(t <= used_):
                    eu, ed, en = expert(t), expert(t - 1), expert(t + 1)
                    for c in range(3, 12):
                        load_chunk(t, c, eu, ed)
                    for c in range(3):
                        load_chunk(t + 1, c, en, ed)
            for t in range(TT):
                sp.wait_ge(s_fo, t + 1)
                sp.dma_start(out_v[:, t, :], fo[:, t % 2, :]).then_inc(s_out[t % 2], 16)
            for i in range(2):
                sp.wait_ge(s_out[i], 16 * TT // 2)

        @block.gpsimd
        def _(pool):
            nc.gpsimd.memset(ones[:], 1.0).then_inc(s_const, 1)
            nc.gpsimd.memset(W2[:], 0.0).then_inc(s_w2z, 1)
            pool.wait_ge(s_const, 1)
            nc.gpsimd.affine_select(out=ident[:], in_=ones[:], compare_op=ALU.is_equal, fill=0.0, base=0,
                                    pattern=[[-1, P]], channel_multiplier=1).then_inc(s_const, 1)
            nc.gpsimd.affine_select(out=before[:], in_=ones[:], compare_op=ALU.is_gt, fill=0.0, base=0,
                                    pattern=[[1, P]], channel_multiplier=-1).then_inc(s_const, 1)
            nc.gpsimd.iota(xor[:], pattern=[[1, P]], base=0, channel_multiplier=0).then_inc(s_const, 1)
            nc.gpsimd.iota(mtmp[:].bitcast(I32), pattern=[[0, P]], base=0, channel_multiplier=1).then_inc(s_const, 1)
            nc.gpsimd.iota(pid[:], pattern=[[P, 8]], base=0, channel_multiplier=1,
                           allow_small_or_imprecise_dtypes=True).then_inc(s_const, 1)
            nc.gpsimd.iota(iot[:], pattern=[[1, P]], base=0, channel_multiplier=0,
                           allow_small_or_imprecise_dtypes=True).then_inc(s_const, 1)
            pool.wait_ge(s_mm["mem"], 16)
            for c in range(CT):
                nc.gpsimd.memset(u_pad[:, c, 0:PAD], 0.0).then_inc(s_pad, 1)
                nc.gpsimd.memset(u_pad[:, c, PAD + S:UW], 0.0).then_inc(s_pad, 1)
            for c in range(CT):
                pool.wait_ge(s_dr["in"], 2 + 8 * (c // 2) + 4 + 2 * (c % 2 + 1))
                uc = u_pad[:, c, PAD:PAD + S]
                nc.gpsimd.tensor_tensor(uc, uc, sig[:], ALU.mult).then_inc(s_u, 1)

            pool.wait_ge(s_rt, 1)
            nc.gpsimd.iota(pmi[:], pattern=[[0, 2]], base=0, channel_multiplier=1).then_inc(s_rmi, 1)

            def index_column(n):
                nc.gpsimd.tensor_copy(idxc[:], TM[:, bass.ds(n, 1)]).then_inc(s_idx, 1)
                pool.wait_ge(s_idx, n + 1)

            def gather():
                nc.gpsimd.indirect_dma_start(xs[:], None, h3_dram, bass.IndirectOffsetOnAxis(ap=idxc[:], axis=0)
                                             ).then_inc(s_xsl, 16)

            def lo_by_pool(t, c):
                pool.wait_ge(s_whi, 12 * t + c - 3)
                nc.gpsimd.tensor_tensor(wlo[:, chunk_slot(c, NSPL), :], raw[:, chunk_slot(c, NRAW), :],
                                        whi[:, chunk_slot(c, NSPL), :].bitcast(F), ALU.subtract
                                        ).then_inc(s_wlp, 1)

            pool.wait_ge(s_tab, 1)
            for i in range(2):
                pool.wait_ge(s_h3s[i], 16 * TT // 2)
            used_ = pool.value_load(usedb[0:1, 0:1], min_val=1, max_val=NBLK)
            index_column(0)
            gather()
            lo_by_pool(0, 6)
            pool.wait_ge(s_xt, 2)
            index_column(1)
            gather()
            lo_by_pool(0, 9)
            pool.wait_ge(s_xt, 4)
            index_column(2)
            gather()
            lo_by_pool(1, 0)
            with pool.Fori(1, NBLK + 1) as t:
                with pool.If(t <= used_):
                    for c in (3, 6, 9):
                        lo_by_pool(t, c)
                    pool.wait_ge(s_xt, 2 * t + 4)
                    index_column(t + 2)
                    lo_by_pool(t + 1, 0)
                    gather()
            pool.wait_ge(s_yst, 16 * NBLK + 1)
            wait_lo(pool, used_ + 1, 0)
            wait_lo(pool, used_ + 1, 2)
            nc.gpsimd.tensor_tensor(pmod[:, 0:1], pmod[:, 0:1], pmod[:, 1:2], ALU.mult)
            for i in range(TT * TOPK):
                if i >= 8:
                    pool.wait_ge(s_ac, i - 7)
                nc.gpsimd.indirect_dma_start(yg[:, i % 8, :], None, ys_dram,
                                             bass.IndirectOffsetOnAxis(ap=rowof[:, i:i + 1], axis=0)
                                             ).then_inc(s_yg[i % 8], 16)

        @block.scalar
        def _(act):
            act.wait_ge(s_w2z, 1)
            act.dma_start(W2[0:RANK, 0, :], A["gate_w2_fwd"][0]).then_inc(s_par, 16)
            act.dma_start(W2[RANK:2 * RANK, 1, :], A["gate_w2_bwd"][0]).then_inc(s_par, 16)
            for row, name, n in ((GX, "norm_mix_g", 8), (GM, "norm_mem_g", 8), (GA, "norm_xattn_g", 8),
                                 (ZB, "gate_b_fwd", 2), (ZB + 2, "gate_b_bwd", 2), (CB, "conv_b", 4),
                                 (LG_, "conv_ln_g", 4), (LB, "conv_ln_b", 4)):
                act.dma_start(PVr[row:row + n, :], A[name][0].rearrange("(k p) -> k p", p=P)).then_inc(s_par, 16)
            act.dma_start(CWr[:], A["conv_w"][0].rearrange("j (c p) -> (j c) p", p=P)).then_inc(s_par, 16)
            act.dma_start(ngb[:], A["gla_norm_g"][0].partition_broadcast(P)).then_inc(s_par, 16)

            def norm_stats(n, src, tiles):
                N = norms[n]
                for t in range(tiles):
                    if n == "m":
                        act.wait_ge(N["loaded"], 16)
                    elif n == "x":
                        act.wait_ge(s_xld[t // 2], 16)
                    elif n == "y":
                        act.wait_ge(s_dr["out"], 24 + t + 1)
                    else:
                        act.wait_ge(s_dr["o"], 24 + t + 1)
                    if t:
                        act.wait_ge(N["stats_by_scalar"], t)
                    nc.scalar.activation(sig[:], src[:, t, :], ACT.Square,
                                         accum_out=st8[:, 0, t:t + 1]).then_inc(N["stats_by_scalar"], 1)
                act.wait_ge(N["stats_by_vector"], 1)
                nc.scalar.activation(st8[:, 2, 0:tiles], st8[:, 1, 0:tiles], ACT.Sqrt).then_inc(N["stats_by_scalar"], 1)

            norm_stats("m", mem_tm, MT)
            act.wait_ge(norms["m"]["stats_by_vector"], 2)
            act.wait_ge(norms["m"]["scaled"], MT)
            norm_stats("x", xres, TT)

            def drain(seg, n):
                act.wait_ge(s_mm[seg], n + 1)
                return s_dr[seg]

            for n in range(16):
                d = drain("mem", n)
                dst = kx[:, n, :] if n < 8 else vx[:, n % 2, 256 * ((n - 8) // 2):256 * ((n - 8) // 2 + 1)]
                nc.scalar.copy(dst, bank_groups(n, 256)).then_inc(d, 1)
            n = 0
            for th in range(2):
                d = drain("in", n)
                if n == 0:
                    act.wait_ge(norms["x"]["turned"], 2 * TT)
                nc.scalar.copy(gT[:, 512 * th:512 * (th + 1)], PS[0:2 * RANK, n % 8, :]).then_inc(d, 1)
                n += 1
            for c2 in range(2):
                for ft in range(2):
                    for th in range(2):
                        d = drain("in", n)
                        nc.scalar.copy(u_pad[:, 2 * c2 + ft, PAD + 512 * th:PAD + 512 * (th + 1)],
                                       bank_groups(n)).then_inc(d, 1)
                        n += 1
                for ft in range(2):
                    for th in range(2):
                        d = drain("in", n)
                        c = 2 * c2 + ft
                        if th == 0 and c:
                            act.wait_ge(s_u, c)
                        nc.scalar.activation(sig[:, 512 * th:512 * (th + 1)], bank_groups(n),
                                             ACT.Sigmoid).then_inc(d, 1)
                        n += 1
            for dst, sc in ((qT, GDK ** -0.5), (kT, 1.0)):
                for ft in range(2):
                    for th in range(2):
                        d = drain("in", n)
                        if n == 18:
                            act.wait_ge(norms["x"]["scaled"], TT)
                        nc.scalar.mul(dst[:, ft, 512 * th:512 * (th + 1)], bank_groups(n), sc).then_inc(d, 1)
                        n += 1
            for dst in (v_tm, r_tm):
                for c2 in range(2):
                    for t in range(TT):
                        d = drain("in", n)
                        nc.scalar.copy(dst[:, t, 256 * c2:256 * (c2 + 1)], bank_groups(n, 256)).then_inc(d, 1)
                        n += 1

            for c in range(CT):
                act.wait_ge(s_lnv, 2 * (c + 1))
                if c == 0:
                    act.wait_ge(s_mm["in"], 58)
                nc.scalar.activation(o_gla[:, 2 * c:2 * c + 2, :], yT[:, c, :].rearrange("p (a b) -> p a b", a=2),
                                     ACT.Square).then_inc(s_lna, 1)
            act.wait_ge(s_lnv, 10)
            nc.scalar.activation(sig[:], sig[:], ACT.Sqrt).then_inc(s_lna, 1)
            for c in range(CT):
                act.wait_ge(s_lnv, 12 + c)
                act.wait_ge(s_lnp, 4)
                nc.scalar.activation(o_gla[:, 2 * c:2 * c + 2, :], yT[:, c, :].rearrange("p (a b) -> p a b", a=2),
                                     ACT.Identity, bias=PV[:, LB + c:LB + c + 1],
                                     scale=PV[:, LG_ + c:LG_ + c + 1]).then_inc(s_lna, 1)
            for c in range(CT):
                act.wait_ge(s_lna, 6 + c)
                nc.scalar.activation(yT[:, c, :], yT[:, c, :], ACT.Sigmoid, bias=PV[:, LB + c:LB + c + 1],
                                     scale=PV[:, LG_ + c:LG_ + c + 1]).then_inc(s_lna, 1)

            for p in range(2):
                for n in range(4):
                    d, th = n // 2, n % 2
                    act.wait_ge(s_z, 4 * p + n + 1)
                    nc.scalar.activation(KQ[:, d, 512 * th:512 * (th + 1)], PS[:, n, :], ACT.Abs,
                                         bias=PV[:, ZB + 2 * d + p:ZB + 2 * d + p + 1]).then_inc(s_zabs, 1)
                act.wait_ge(s_zabs, 4 * (p + 1))
                nc.scalar.activation(KQ[:], KQ[:], ACT.Exp, scale=-1.0).then_inc(s_zln, 1)
                act.wait_ge(s_zln, 2 * p + 1)
                nc.scalar.activation(KQ[:], KQ[:], ACT.Ln, bias=1.0).then_inc(s_zln, 1)
                act.wait_ge(s_tot, 2 * (p + 1))
                nc.scalar.activation(TTd[:, 1], TTd[:, 0], ACT.Exp, scale=1.0 / TAU).then_inc(s_dec, 1)
                for l in range(8):
                    act.wait_ge(s_sub, 8 * p + l + 1)
                    nc.scalar.activation(EX[:], EX[:], ACT.Exp, scale=1.0 / TAU).then_inc(s_ex, 1)
                    if l == 7:
                        for b in range(4):
                            act.wait_ge(s_ket, 4 * p + b + 1)
                            nc.scalar.copy(KEt[:, b, :], PS[:, b, :]).then_inc(s_kev, 1)
                act.wait_ge(s_U, 14 * (p + 1))
                nc.scalar.activation(EX[:, 0, :], Bf[:], ACT.Exp, scale=1.0 / TAU)
                nc.scalar.activation(EX[:, 1, :], Rb[:], ACT.Exp, scale=1.0 / TAU).then_inc(s_ex, 1)
                for n in range(16):
                    act.wait_ge(s_op, 16 * p + n + 1)
                    w, hh = n // 2, n % 2
                    h = 2 * p + hh
                    nc.scalar.copy(o_gla[:, w, GDV * h:GDV * (h + 1)], PS[:, n % 4, 0:P]).then_inc(s_oe, 1)
            act.wait_ge(s_ov, 3)
            nc.scalar.activation(st8[:, 2, :], st8[:, 1, :], ACT.Sqrt).then_inc(s_oa, 1)
            nc.scalar.activation(SR[:], r_tm[:], ACT.Sigmoid).then_inc(s_oa, 1)
            for c in range(CT):
                for b in range(2):
                    n = 2 * c + b
                    act.wait_ge(s_at, n + 1)
                    nc.scalar.copy(aT[:, c, 512 * b:512 * (b + 1)], PS[:, n, :]).then_inc(s_ae, 1)
            norm_stats("y", xres, TT)
            for n in range(16):
                d = drain("q", n)
                nc.scalar.copy(qxT[:, n // 2, 512 * (n % 2):512 * (n % 2 + 1)], bank_groups(n)).then_inc(d, 1)
            def xprob_drain(h, t):
                i = TT * h + t
                act.wait_ge(s_pt, i + 1)
                nc.scalar.copy(pT[:, h % 2, :, P * t:P * (t + 1)],
                               PS[:, 2 + i % 2, 0:256].rearrange("p (m c) -> p m c", m=MT)).then_inc(s_pc, 1)

            for h in range(XH):
                for t in range(TT):
                    n = TT * h + t
                    act.wait_ge(s_sv, 4 * n + 2)
                    if n >= 2:
                        act.wait_ge(s_pt, n - 1)
                    nc.scalar.activation(pr[:, n % 2, :], PS[:, n % 2, 0:256], ACT.Exp, bias=smx[:, n % 4, 1:2],
                                         scale=XDH ** -0.5, accum_out=smx[:, n % 4, 2:3]).then_inc(s_pe, 1)
                    if t >= 1:
                        xprob_drain(h, t - 1)
                xprob_drain(h, TT - 1)
                for b in range(4):
                    m = 4 * h + b
                    act.wait_ge(s_av, m + 1)
                    nc.scalar.copy(oxT[:, 2 * h + b // 2, 512 * (b % 2):512 * (b % 2 + 1)],
                                   PS[:, 4 + b, :]).then_inc(s_ax, 1)
            act.wait_ge(s_mm["o"], 1)
            act.dma_start(gfb[:], A["norm_ffn_g"][0].partition_broadcast(P)).then_inc(s_rpar, 16)
            act.dma_start(rw[:], A["router_w"][0].rearrange("(k p) e -> p k e", p=P)).then_inc(s_rpar, 16)
            act.dma_start(rbb[:], A["router_b"][0].partition_broadcast(P)).then_inc(s_rpar, 16)
            act.wait_ge(s_mm["o"], 32)
            act.dma_start(bdn[:], A["exp_b_down"][0]).then_inc(s_rpar, 16)
            for i in range(3):
                act.dma_start(bstage[E * i:E * (i + 1), :], A["exp_b_up"][0]).then_inc(s_rpar, 16)
            norm_stats("z", xres, TT)
            for t in range(TT):
                for b in range(2):
                    act.wait_ge(norms["z"]["turned"], 2 * t + b + 1)
                    if t >= 2:
                        act.wait_ge(s_lgp, t - 1)
                    nc.scalar.copy(h3T[:, t % 2, 4 * b:4 * b + 4, :].rearrange("p k c -> p (k c)"),
                                   PS[:, 2 * (t % 2) + b, :]).then_inc(s_h3e, 1)
            act.wait_ge(s_rt, 2)
            nc.scalar.activation(Gt[:], Gt[:], ACT.Exp).then_inc(s_gx, 1)
            for b in range(2):
                act.wait_ge(s_gdt, b + 1)
                nc.scalar.copy(GDT[:, 512 * b:512 * (b + 1)], PS[0:E, b, :]).then_inc(s_gde, 1)

            def split_hi(t, c, first=False):
                wait_raw(act, t, c)
                if not first:
                    wait_multiplied(act, t, c - NSPL)
                nc.scalar.copy(whi[:, chunk_slot(c, NSPL), :], raw[:, chunk_slot(c, NRAW), :]).then_inc(s_whi, 1)

            def tokens_hi(t):
                for b in range(2):
                    act.wait_ge(s_xt, 2 * t + b + 1)
                    nc.scalar.copy(xhi[:, 4 * b:4 * b + 4, :].rearrange("p k c -> p (k c)"),
                                   PS[:, 6 + b, :]).then_inc(s_xhi, 1)

            def hidden_hi(t):
                for b in range(2):
                    act.wait_ge(s_ht, 2 * t + b + 1)
                    nc.scalar.copy(hhi[:, 4 * b:4 * b + 4, :].rearrange("p k c -> p (k c)"),
                                   PS[:, 6 + b, :]).then_inc(s_hhi, 1)

            def expert_sigmoid(t):
                act.wait_ge(s_g, 2 * t + 2)
                nc.scalar.activation(sgm[:], glu[:], ACT.Sigmoid, scale=ALPHA).then_inc(s_sg, 1)

            act.wait_ge(s_tab, 1)
            used_ = act.value_load(usedb[0:1, 0:1], min_val=1, max_val=NBLK)
            nc.scalar.copy(yb[:, 0:1], st8[:, 0, 0:1]).then_inc(s_yev, 1)
            nc.scalar.copy(yb[:, 1:2], st8[:, 0, 0:1]).then_inc(s_yst, 1)
            tokens_hi(0)
            for c in range(4, 12):
                split_hi(0, c, first=c < 4 + NSPL)
            tokens_hi(1)
            expert_sigmoid(0)
            for c in range(3):
                split_hi(1, c)
            hidden_hi(0)
            with act.Fori(1, NBLK + 1) as t:
                with act.If(t <= used_):
                    for c in range(3, 12):
                        split_hi(t, c)
                    tokens_hi(t + 1)
                    expert_sigmoid(t)
                    for c in range(3):
                        split_hi(t + 1, c)
                    wait_multiplied(act, t, 11)
                    act.wait_ge(s_yst, 16 * t - 15)
                    for b in range(2):
                        nc.scalar.copy(yb[:, 512 * b:512 * (b + 1)], PS[:, 4 + b, :]).then_inc(s_yev, 1)
                    act.wait_ge(s_yev, 2 * t + 1)
                    act.dma_start(ys_dram[bass.ds((t - 1) * P, P), :], yb[:]).then_inc(s_yst, 16)
                    hidden_hi(t)
                with act.Else():
                    act.dma_start(ys_dram[bass.ds((t - 1) * P, P), :], yb[:]).then_inc(s_yst, 16)
            for t in range(TT):
                act.wait_ge(s_ac, TOPK * (t + 1))
                nc.scalar.activation(sgm[:], xres[:, t, :], ACT.Square, accum_out=st8[:, 0, t:t + 1]
                                     ).then_inc(s_fa, 1)
                act.wait_ge(s_fv, 2 * t + 1)
                nc.scalar.activation(st8[:, 2, t:t + 1], st8[:, 1, t:t + 1], ACT.Sqrt).then_inc(s_fa, 1)

        @block.vector
        def _(dve):
            dve.wait_ge(s_const, 5)
            nc.vector.tensor_tensor(xor[:], xor[:], mtmp[:].bitcast(I32), ALU.bitwise_xor).then_inc(s_mask, 1)
            for l, s in enumerate(LEVELS):
                dve.wait_ge(s_mask, 2 * l + 1)
                nc.vector.tensor_scalar(mtmp[:], xor[:], float(2 * s), None, ALU.is_lt).then_inc(s_mask, 1)
                dve.wait_ge(s_mask, 2 * l + 2)
                nc.vector.scalar_tensor_tensor(out=masks[:, l, :], in0=xor[:], scalar=float(s), in1=mtmp[:],
                                               op0=ALU.is_ge, op1=ALU.mult).then_inc(s_mask, 1)
            dve.wait_ge(s_pvt, 2)
            nc.vector.tensor_copy(PV[:, 0:NPV], PS[:, 6, 0:NPV]).then_inc(s_pvc, 1)
            nc.vector.tensor_copy(CWT[:], PS[:, 7, 0:TAPS * CT]).then_inc(s_pvc, 1)
            dve.wait_ge(s_pvc, 2)

            def norm_scale(n, src, tiles, g, dst):
                N = norms[n]
                dve.wait_ge(N["stats_by_scalar"], tiles)
                nc.vector.tensor_scalar(st8[:, 1, 0:tiles], st8[:, 0, 0:tiles], 1.0 / D, RMS_EPS,
                                        ALU.mult, ALU.add).then_inc(N["stats_by_vector"], 1)
                dve.wait_ge(N["stats_by_scalar"], tiles + 1)
                nc.vector.reciprocal(st8[:, 3, 0:tiles], st8[:, 2, 0:tiles]).then_inc(N["stats_by_vector"], 1)
                dve.wait_ge(N["stats_by_vector"], 2)

                def evac(t):
                    for b in range(2):
                        dve.wait_ge(N["turned"], 2 * t + b + 1)
                        bank = 2 * (t % 4) + b
                        nc.vector.tensor_tensor(
                            dst[:, 4 * b:4 * b + 4, P * t:P * (t + 1)],
                            PS[:, bank, :].rearrange("p (k c) -> p k c", k=4),
                            PV[:, g + 4 * b:g + 4 * b + 4].unsqueeze(2).broadcast_to([P, 4, P]),
                            ALU.mult).then_inc(N["drained"], 1)

                for t in range(tiles):
                    if t >= 2:
                        dve.wait_ge(N["turned"], 2 * (t - 1))
                    nc.vector.tensor_scalar(XN[:, t % 2, :], src[:, t, :], st8[:, 3, t:t + 1], None,
                                            ALU.mult).then_inc(N["scaled"], 1)
                    if t >= 1:
                        evac(t - 1)
                evac(tiles - 1)

            norm_scale("m", mem_tm, MT, GM, mT)
            norm_scale("x", xres, TT, GX, hT)

            dve.wait_ge(s_pad, 2 * CT)
            cv = 0
            for c2 in range(2):
                dve.wait_ge(s_u, 2 * c2 + 2)
                for j in range(TAPS):
                    for c in (2 * c2, 2 * c2 + 1):
                        uc = u_pad[:, c, j:j + S]
                        w = CWT[:, j * CT + c:j * CT + c + 1]
                        if j == 0:
                            if c == 0:
                                dve.wait_ge(norms["m"]["scaled"], MT)
                            ins = nc.vector.tensor_scalar(yT[:, c, :], uc, w, PV[:, CB + c:CB + c + 1],
                                                          ALU.mult, ALU.add)
                        else:
                            dve.wait_ge(s_cv, cv - 1)
                            ins = nc.vector.scalar_tensor_tensor(out=yT[:, c, :], in0=uc, scalar=w,
                                                                 in1=yT[:, c, :], op0=ALU.mult, op1=ALU.add)
                        ins.then_inc(s_cv, 1)
                        cv += 1
            for th in range(2):
                dve.wait_ge(s_lnp, th + 1)
            for c in range(CT):
                for th in range(2):
                    yh = yT[:, c, 512 * th:512 * (th + 1)]
                    nc.vector.scalar_tensor_tensor(out=yh, in0=PS[:, th, :], scalar=-1.0 / CW_, in1=yh,
                                                   op0=ALU.mult, op1=ALU.add).then_inc(s_lnv, 1)
            for th in range(2):
                dve.wait_ge(s_lnp, th + 3)
                nc.vector.tensor_scalar(sig[:, 512 * th:512 * (th + 1)], PS[:, 2 + th, :], 1.0 / CW_, LN_EPS,
                                        ALU.mult, ALU.add).then_inc(s_lnv, 1)
            dve.wait_ge(s_lna, 5)
            nc.vector.reciprocal(sig[:], sig[:]).then_inc(s_lnv, 1)
            dve.wait_ge(s_lnv, 11)
            for c in range(CT):
                nc.vector.tensor_tensor(yT[:, c, :], yT[:, c, :], sig[:], ALU.mult).then_inc(s_lnv, 1)
            for c in range(CT):
                dve.wait_ge(s_lna, 10 + c)
                nc.vector.tensor_tensor(yT[:, c, :].rearrange("p (a b) -> p a b", a=2),
                                        yT[:, c, :].rearrange("p (a b) -> p a b", a=2),
                                        o_gla[:, 2 * c:2 * c + 2, :], ALU.mult).then_inc(s_lnv, 1)

            dve.wait_ge(s_par, 12 * 16)
            for p in range(2):
                if p:
                    dve.wait_ge(s_kq, 9 * p)
                for n in range(4):
                    d, th = n // 2, n % 2
                    dve.wait_ge(s_z, 4 * p + n + 1)
                    dve.wait_ge(s_zabs, 4 * p + n + 1)
                    nc.vector.tensor_scalar(EX[:, d, 512 * th:512 * (th + 1)], PS[:, n, :],
                                            PV[:, ZB + 2 * d + p:ZB + 2 * d + p + 1], 0.0,
                                            ALU.add, ALU.min).then_inc(s_zmin, 1)
                dve.wait_ge(s_zmin, 4 * (p + 1))
                dve.wait_ge(s_zln, 2 * (p + 1))
                nc.vector.tensor_tensor(EX[:], EX[:], KQ[:], ALU.subtract).then_inc(s_la, 1)
                dve.wait_ge(s_la, p + 1)
                for d, dst in ((0, Bf), (1, Rb)):
                    for w in range(TT):
                        nc.vector.tensor_tensor_scan(out=dst[:, P * w:P * (w + 1)], data0=ones[:],
                                                     data1=EX[:, d, P * w:P * (w + 1)], initial=0.0,
                                                     op0=ALU.mult, op1=ALU.add).then_inc(s_scan, 1)
                dve.wait_ge(s_scan, 16 * (p + 1))
                wins = lambda ap: ap.rearrange("p (w c) -> p w c", w=TT)
                ends = lambda ap: wins(ap)[:, :, P - 1:P].rearrange("p w c -> p (w c)")
                if p:
                    dve.wait_ge(s_st, 14 * p)
                nc.vector.tensor_copy(TTd[:, 0, 0, :], ends(Bf[:])).then_inc(s_tot, 1)
                nc.vector.tensor_copy(TTd[:, 0, 1, :], ends(Rb[:])).then_inc(s_tot, 1)
                dve.wait_ge(s_tot, 2 * (p + 1))
                nc.vector.tensor_tensor(Rb[:], EX[:, 1, :], Rb[:], ALU.subtract).then_inc(s_rb, 1)
                dve.wait_ge(s_rb, 2 * p + 1)
                tot = lambda d: TTd[:, 0, d, :].unsqueeze(2).broadcast_to([P, TT, P])
                nc.vector.tensor_tensor(wins(Rb[:]), wins(Rb[:]), tot(1), ALU.add).then_inc(s_rb, 1)
                dve.wait_ge(s_rb, 2 * p + 2)

                def exponents(l):
                    s = LEVELS[l]
                    v3 = lambda ap: ap.rearrange("p (g h c) -> p g h c", h=2, c=s)
                    bref = v3(Bf[:])[:, :, 0, s - 1:s].broadcast_to([P, S // (2 * s), s])
                    rref = v3(Rb[:])[:, :, 1, 0:1].broadcast_to([P, S // (2 * s), s])
                    B_, R_, K_, Q_ = v3(Bf[:]), v3(Rb[:]), v3(EX[:, 0, :]), v3(EX[:, 1, :])
                    nc.vector.tensor_tensor(K_[:, :, 0, :], bref, B_[:, :, 0, :], ALU.subtract)
                    nc.vector.tensor_tensor(K_[:, :, 1, :], rref, R_[:, :, 1, :], ALU.subtract)
                    nc.vector.tensor_tensor(Q_[:, :, 0, :], R_[:, :, 0, :], rref, ALU.subtract)
                    nc.vector.tensor_tensor(Q_[:, :, 1, :], B_[:, :, 1, :], bref, ALU.subtract).then_inc(s_sub, 1)

                exponents(0)
                for b in range(4):
                    hh, half = b // 2, b % 2
                    dve.wait_ge(s_gram, 32 * p + b + 1)
                    nc.vector.tensor_copy(Ssc[:, hh, 4 * half:4 * half + 4, :].rearrange("p w c -> p (w c)"),
                                          PS[:, b, :]).then_inc(s_sel, 1)
                for l in range(7):
                    dve.wait_ge(s_ex, 9 * p + l + 1)
                    if l:
                        dve.wait_ge(s_gram, 32 * p + 4 * (l + 1))
                    nc.vector.tensor_tensor(KQ[:, 0, :], EX[:, 0, :], kT[:, p, :], ALU.mult)
                    nc.vector.tensor_tensor(KQ[:, 1, :], EX[:, 1, :], qT[:, p, :], ALU.mult).then_inc(s_kq, 1)
                    dve.wait_ge(s_kq, 9 * p + l + 1)
                    if l < 6:
                        exponents(l + 1)
                    else:
                        nc.vector.tensor_tensor(wins(EX[:, 0, :]), tot(0), wins(Bf[:]), ALU.subtract)
                        nc.vector.tensor_tensor(wins(EX[:, 1, :]), tot(1), wins(Rb[:]),
                                                ALU.subtract).then_inc(s_sub, 1)
                    for b in range(4):
                        hh, half = b // 2, b % 2
                        L = 8 * p + l + 1
                        dve.wait_ge(s_gram, 4 * L + b + 1)
                        if b == 0:
                            dve.wait_ge(s_sel, 4 * L)
                        nc.vector.copy_predicated(
                            Ssc[:, hh, 4 * half:4 * half + 4, :],
                            masks[:, l:l + 1, :].broadcast_to([P, 4, P]),
                            PS[:, 4 * (L % 2) + b, :].rearrange("p (w c) -> p w c", w=4)).then_inc(s_sel, 1)
                dve.wait_ge(s_ex, 9 * p + 8)
                nc.vector.tensor_tensor(KQ[:, 0, :], EX[:, 0, :], kT[:, p, :], ALU.mult)
                nc.vector.tensor_tensor(KQ[:, 1, :], EX[:, 1, :], kT[:, p, :], ALU.mult).then_inc(s_kq, 1)
                nc.vector.memset(ST[:, 0, 0, :], 0.0).then_inc(s_st0, 1)
                nc.vector.memset(ST[:, 1, TT - 1, :], 0.0).then_inc(s_st0, 1)
                dve.wait_ge(s_st0, 2 * (p + 1))
                dve.wait_ge(s_dec, p + 1)
                for n in range(14):
                    d = n % 2
                    w = n // 2 if d == 0 else TT - 1 - n // 2
                    to = w + 1 if d == 0 else w - 1
                    dve.wait_ge(s_U, 14 * p + n + 1)
                    if n >= 2:
                        dve.wait_ge(s_st, 14 * p + n - 1)
                    for hh in range(2):
                        a, b = GDK * hh, GDK * (hh + 1)
                        ins = nc.vector.scalar_tensor_tensor(
                            out=ST[a:b, d, to, :], in0=ST[a:b, d, w, :], scalar=TTd[a:b, 1, d, w:w + 1],
                            in1=PS[a:b, 4 + n % 4, P * hh:P * (hh + 1)], op0=ALU.mult, op1=ALU.add)
                    ins.then_inc(s_st, 1)
                dve.wait_ge(s_ex, 9 * p + 9)
                dve.wait_ge(s_ket, 4 * (p + 1))
                nc.vector.tensor_tensor(KQ[:, 0, :], EX[:, 0, :], qT[:, p, :], ALU.mult)
                nc.vector.tensor_tensor(KQ[:, 1, :], EX[:, 1, :], qT[:, p, :], ALU.mult).then_inc(s_kq, 1)
            og = o_gla[:].rearrange("p w (h c) -> p (w h) c", h=GH)
            rg = r_tm[:].rearrange("p w (h c) -> p (w h) c", h=GH)
            sg = SR[:].rearrange("p w (h c) -> p (w h) c", h=GH)
            dve.wait_ge(s_oe, 32)
            dve.wait_ge(s_op, 32)
            nc.vector.tensor_tensor(sg, og, og, ALU.mult).then_inc(s_ov, 1)
            dve.wait_ge(s_ov, 1)
            nc.vector.tensor_reduce(st8[:, 0, :], sg, X, ALU.add).then_inc(s_ov, 1)
            dve.wait_ge(s_ov, 2)
            nc.vector.tensor_scalar(st8[:, 1, :], st8[:, 0, :], 1.0 / GDV, RMS_EPS, ALU.mult, ALU.add
                                    ).then_inc(s_ov, 1)
            dve.wait_ge(s_oa, 1)
            nc.vector.reciprocal(st8[:, 3, :], st8[:, 2, :]).then_inc(s_ov, 1)
            dve.wait_ge(s_ov, 4)
            nc.vector.tensor_tensor(og, og, st8[:, 3, :].unsqueeze(2).broadcast_to([P, 32, P]), ALU.mult
                                    ).then_inc(s_ov, 1)
            dve.wait_ge(s_ov, 5)
            nc.vector.tensor_tensor(og, og, ngb[:].unsqueeze(1).broadcast_to([P, 32, P]), ALU.mult
                                    ).then_inc(s_ov, 1)
            dve.wait_ge(s_oa, 2)
            nc.vector.tensor_tensor(rg, rg, sg, ALU.mult).then_inc(s_ov, 1)
            dve.wait_ge(s_ov, 7)
            nc.vector.tensor_tensor(og, og, rg, ALU.mult).then_inc(s_ov, 1)

            def add_residual(seg):
                for c in range(4):
                    for t in range(TT):
                        n = TT * c + t
                        dve.wait_ge(s_mm[seg], n + 1)
                        xs = xres[:, t, 256 * c:256 * (c + 1)]
                        nc.vector.tensor_tensor(xs, xs, bank_groups(n, 256), ALU.add).then_inc(s_dr[seg], 1)

            dve.wait_ge(s_xre, 16)
            add_residual("out")
            norm_scale("y", xres, TT, GA, hT)
            for h in range(XH):
                for t in range(TT):
                    n = TT * h + t
                    dve.wait_ge(s_sc, n + 1)
                    if n >= 4:
                        dve.wait_ge(s_sv, 4 * (n - 3))
                    m = smx[:, n % 4, :]
                    nc.vector.reduce_max(m[:, 0:1], PS[:, n % 2, 0:256], X).then_inc(s_sv, 1)
                    dve.wait_ge(s_sv, 4 * n + 1)
                    nc.vector.tensor_scalar(m[:, 1:2], m[:, 0:1], -(XDH ** -0.5), None, ALU.mult).then_inc(s_sv, 1)
                    dve.wait_ge(s_pe, n + 1)
                    nc.vector.reciprocal(m[:, 3:4], m[:, 2:3]).then_inc(s_sv, 1)
                    dve.wait_ge(s_sv, 4 * n + 3)
                    nc.vector.tensor_scalar(pr[:, n % 2, :], pr[:, n % 2, :], m[:, 3:4], None,
                                            ALU.mult).then_inc(s_sv, 1)
            add_residual("o")

            N = norms["z"]
            dve.wait_ge(N["stats_by_scalar"], TT)
            nc.vector.tensor_scalar(st8[:, 1, 0:TT], st8[:, 0, 0:TT], 1.0 / D, RMS_EPS, ALU.mult, ALU.add
                                    ).then_inc(N["stats_by_vector"], 1)
            dve.wait_ge(N["stats_by_scalar"], TT + 1)
            nc.vector.reciprocal(st8[:, 3, 0:TT], st8[:, 2, 0:TT]).then_inc(N["stats_by_vector"], 1)
            dve.wait_ge(N["stats_by_vector"], 2)
            dve.wait_ge(s_rpar, 7 * 16)

            def logits(t):
                dve.wait_ge(s_lgp, t + 1)
                nc.vector.tensor_tensor(LG[:, t, :], PS[:, 4 + t % 2, 0:E], rbb[:], ALU.add).then_inc(s_lg, 1)
                dve.wait_ge(s_lg, t + 1)
                nc.vector.max(MX[:, t, :], LG[:, t, :]).then_inc(s_top, 1)
                dve.wait_ge(s_top, 2 * t + 1)
                nc.vector.max_index(IX[:, t, :], MX[:, t, :], LG[:, t, :]).then_inc(s_top, 1)

            for t in range(TT):
                if t >= 2:
                    dve.wait_ge(N["turned"], 2 * (t - 1))
                    dve.wait_ge(s_h3s[t % 2], 16 * (t // 2))
                nc.vector.scalar_tensor_tensor(out=XN[:, t % 2, :], in0=xres[:, t, :], scalar=st8[:, 3, t:t + 1],
                                               in1=gfb[:], op0=ALU.mult, op1=ALU.mult).then_inc(N["scaled"], 1)
                if t:
                    logits(t - 1)
            logits(TT - 1)
            dve.wait_ge(s_top, 2 * TT)

            rt = 0

            def step(ins):
                nonlocal rt
                rt += 1
                ins.then_inc(s_rt, 1)
                dve.wait_ge(s_rt, rt)

            step(nc.vector.tensor_copy(IXf[:], IX[:]))
            step(nc.vector.tensor_tensor(Gt[:], MX[:, :, 0:TOPK], MX[:, :, 0:1].broadcast_to([P, TT, TOPK]),
                                         ALU.subtract))
            for k in range(TOPK):
                step(nc.vector.tensor_tensor(OH[:, :, k, :], iot[:, 0:E].unsqueeze(1).broadcast_to([P, TT, E]),
                                             IXf[:, :, k:k + 1].broadcast_to([P, TT, E]), ALU.is_equal))
            step(nc.vector.tensor_tensor(M[:], OH[:, :, 0, :], OH[:, :, 1, :], ALU.add))
            step(nc.vector.tensor_tensor(M[:], M[:], OH[:, :, 2, :], ALU.add))
            step(nc.vector.tensor_tensor(M[:], M[:], OH[:, :, 3, :], ALU.add))
            assert rt == RT_M
            dve.wait_ge(s_gx, 1)
            step(nc.vector.tensor_reduce(gsum[:, 0, :], Gt[:], X, ALU.add))
            step(nc.vector.reciprocal(gsum[:, 1, :], gsum[:, 0, :]))
            step(nc.vector.tensor_tensor(Gt[:], Gt[:], gsum[:, 1, :].unsqueeze(2).broadcast_to([P, TT, TOPK]),
                                         ALU.mult))
            tA = tmpA[:, 0:TT * TOPK * E].rearrange("p (t k e) -> p t k e", t=TT, k=TOPK)
            for k in range(TOPK):
                step(nc.vector.tensor_tensor(tA[:, :, k, :], OH[:, :, k, :],
                                             Gt[:, :, k:k + 1].broadcast_to([P, TT, E]), ALU.mult))
            step(nc.vector.tensor_reduce(GD[:], tA.rearrange("p t k e -> p t e k"), X, ALU.add))
            assert rt == RT_GD
            dve.wait_ge(s_rk, 2)
            cnt, nblk, pend, pst = (ex1[:, i, :] for i in range(4))
            step(nc.vector.tensor_scalar(exi[:, 0, :], PS[:, 7, 0:E], float(P - 1), None, ALU.add))
            step(nc.vector.tensor_scalar(exi[:, 1, :], exi[:, 0, :], 7, None, ALU.arith_shift_right))
            step(nc.vector.tensor_copy(nblk, exi[:, 1, :]))
            step(nc.vector.tensor_tensor_scan(out=pend, data0=ones[:, 0:E], data1=nblk, initial=0.0,
                                              op0=ALU.mult, op1=ALU.add))
            step(nc.vector.tensor_tensor(pst, pend, nblk, ALU.subtract))
            step(nc.vector.tensor_scalar(pst, pst, float(P), None, ALU.mult))
            step(nc.vector.tensor_tensor(slot0[:], PS[:, 6, 0:TT * E].rearrange("p (t e) -> p t e", e=E),
                                         pst.unsqueeze(1).broadcast_to([P, TT, E]), ALU.add))
            for k in range(TOPK):
                step(nc.vector.tensor_tensor(tA[:, :, k, :], OH[:, :, k, :], slot0[:], ALU.mult))
            step(nc.vector.tensor_reduce(df[:, 0, :], tA.rearrange("p t k e -> p (t k) e"), X, ALU.add))
            step(nc.vector.tensor_copy(rowof[:], df[:, 0, :]))
            step(nc.vector.tensor_copy(di[:, 0, :], df[:, 0, :]))
            step(nc.vector.tensor_scalar(di[:, 1, :], di[:, 0, :], 7, None, ALU.arith_shift_right))
            step(nc.vector.tensor_scalar(di[:, 2, :], di[:, 0, :], P - 1, None, ALU.bitwise_and))
            step(nc.vector.tensor_copy(df[:, 1:3, :], di[:, 1:3, :]))
            for t in range(TT):
                ks = slice(TOPK * t, TOPK * (t + 1))
                if t >= 2:
                    dve.wait_ge(s_tm, t - 1)
                nc.vector.tensor_tensor(rowhot[:, t % 2], iot[:].unsqueeze(1).broadcast_to([P, TOPK, P]),
                                        df[:, 2, ks].unsqueeze(2).broadcast_to([P, TOPK, P]),
                                        ALU.is_equal).then_inc(s_oh, 1)
                nc.vector.tensor_tensor(blkhot[:, t % 2], iot[:, 0:NB].unsqueeze(1).broadcast_to([P, TOPK, NB]),
                                        df[:, 1, ks].unsqueeze(2).broadcast_to([P, TOPK, NB]),
                                        ALU.is_equal).then_inc(s_oh, 1)
                dve.wait_ge(s_oh, 3 * t + 2)
                nc.vector.tensor_scalar(blkhot[:, t % 2], blkhot[:, t % 2], pid[:, t:t + 1], None,
                                        ALU.mult).then_inc(s_oh, 1)
            tB = tmpA[:].rearrange("p (b e) -> p b e", e=E)
            step(nc.vector.tensor_tensor(tB, pend.unsqueeze(1).broadcast_to([P, NB, E]),
                                         iot[:, 0:NB].unsqueeze(2).broadcast_to([P, NB, E]), ALU.is_le))
            step(nc.vector.tensor_reduce(BE[:], tB, X, ALU.add))
            step(nc.vector.tensor_scalar(BE[:], BE[:], float(E - 1), None, ALU.min))
            step(nc.vector.tensor_copy(BEI[:], BE[:]))
            step(nc.vector.tensor_copy(usedb[:], pend[:, E - 1:E]))
            dve.wait_ge(s_rmi, 1)
            step(nc.vector.tensor_scalar(pmi[:, 0:1], pmi[:, 0:1], E - 1, None, ALU.bitwise_and))
            step(nc.vector.tensor_copy(pmod[:, 0:1], pmi[:, 0:1]))
            step(nc.vector.tensor_scalar(EB[:], BE[:], pmod[:, 0:1], None, ALU.is_equal))
            b0, b1, b2 = (slice(E * i, E * (i + 1)) for i in range(3))
            step(nc.vector.memset(bup[:], 0.0))
            step(nc.vector.tensor_copy(bup[0:3 * E, :], bstage[0:3 * E, :]))
            for rows in (b1, b2):
                step(nc.vector.tensor_tensor(bstage[rows, :], bstage[rows, :], bup[rows, :], ALU.subtract))
            for rows in (b1, b2):
                step(nc.vector.tensor_copy(bup[rows, :], bstage[rows, :]))
            step(nc.vector.tensor_tensor(bstage[b2, :], bstage[b2, :], bup[b2, :], ALU.subtract))
            step(nc.vector.tensor_copy(bup[b2, :], bstage[b2, :]))
            dve.wait_ge(s_tm, TT)
            step(nc.vector.tensor_copy(TM[:], PS[:, 4, 0:NB]))

            def bias_selector(t):
                nc.vector.tensor_scalar(SEL[:], ones[:], EB[:, bass.ds(t, 1)], None, ALU.mult).then_inc(s_bsel, 1)

            for t in range(TT):
                for b in range(2):
                    n = 2 * t + b
                    dve.wait_ge(s_bd, n + 1)
                    xh = xres[:, t, 512 * b:512 * (b + 1)]
                    nc.vector.tensor_tensor(xh, xh, PS[:, n % 4, :], ALU.add).then_inc(s_bdr, 1)
            dve.wait_ge(s_bdr, 2 * TT)
            nc.vector.tensor_copy(pmod[:, 1:2], pmod[:, 0:1]).then_inc(s_tab, 1)

            def lo_by_vector(t, c):
                dve.wait_ge(s_whi, 12 * t + c - 3)
                nc.vector.tensor_tensor(wlo[:, chunk_slot(c, NSPL), :], raw[:, chunk_slot(c, NRAW), :],
                                        whi[:, chunk_slot(c, NSPL), :].bitcast(F), ALU.subtract
                                        ).then_inc(s_wlv, 1)

            def turned_lo(t, s_hi, s_lo, hi, lo):
                for b in range(2):
                    dve.wait_ge(s_hi, 2 * t + b + 1)
                    flat = lambda ap: ap[:, 4 * b:4 * b + 4, :].rearrange("p k c -> p (k c)")
                    nc.vector.tensor_tensor(flat(lo), PS[:, 6 + b, :], flat(hi).bitcast(F), ALU.subtract
                                            ).then_inc(s_lo, 1)

            def clamp_glu(t):
                for b in range(2):
                    nc.vector.tensor_scalar(glu[:, 512 * b:512 * (b + 1)], PS[:, b, :], LIMIT, None, ALU.min
                                            ).then_inc(s_g, 1)

            def hidden(t):
                for b in range(2):
                    nc.vector.tensor_scalar(hid[:, 512 * b:512 * (b + 1)], PS[:, 2 + b, :], LIMIT, -LIMIT,
                                            ALU.min, ALU.max).then_inc(s_upr, 1)
                dve.wait_ge(s_sg, t + 1)
                nc.vector.tensor_tensor(glu[:], glu[:], sgm[:], ALU.mult).then_inc(s_hid, 1)
                dve.wait_ge(s_hid, 2 * t + 1)
                dve.wait_ge(s_upr, 2 * t + 2)
                nc.vector.scalar_tensor_tensor(out=hid[:], in0=hid[:], scalar=1.0, in1=glu[:], op0=ALU.add,
                                               op1=ALU.mult).then_inc(s_hid, 1)

            used_ = dve.value_load(usedb[0:1, 0:1], min_val=1, max_val=NBLK)
            bias_selector(0)
            turned_lo(0, s_xhi, s_xlo, xhi, xlo)
            for c in (4, 5, 7, 8, 10, 11):
                lo_by_vector(0, c)
            wait_multiplied(dve, 0, 11)
            bias_selector(1)
            clamp_glu(0)
            turned_lo(1, s_xhi, s_xlo, xhi, xlo)
            hidden(0)
            for c in (1, 2):
                lo_by_vector(1, c)
            turned_lo(0, s_hhi, s_hlo, hhi, hlo)
            with dve.Fori(1, NBLK + 1) as t:
                with dve.If(t <= used_):
                    for c in (4, 5, 7, 8, 10):
                        lo_by_vector(t, c)
                    wait_multiplied(dve, t, 7)
                    bias_selector(t + 1)
                    clamp_glu(t)
                    lo_by_vector(t, 11)
                    turned_lo(t + 1, s_xhi, s_xlo, xhi, xlo)
                    hidden(t)
                    for c in (1, 2):
                        lo_by_vector(t + 1, c)
                    turned_lo(t, s_hhi, s_hlo, hhi, hlo)
            def final(t):
                dve.wait_ge(s_fv, 2 * t + 2)
                if t >= 2:
                    dve.wait_ge(s_out[t % 2], 16 * (t // 2))
                nc.vector.scalar_tensor_tensor(out=fo[:, t % 2, :], in0=xres[:, t, :], scalar=st8[:, 3, t:t + 1],
                                               in1=gfb[:], op0=ALU.mult, op1=ALU.mult).then_inc(s_fo, 1)

            def root(t):
                dve.wait_ge(s_fa, 2 * t + 1)
                nc.vector.tensor_scalar(st8[:, 1, t:t + 1], st8[:, 0, t:t + 1], 1.0 / D, RMS_EPS, ALU.mult,
                                        ALU.add).then_inc(s_fv, 1)
                dve.wait_ge(s_fa, 2 * t + 2)
                nc.vector.reciprocal(st8[:, 3, t:t + 1], st8[:, 2, t:t + 1]).then_inc(s_fv, 1)

            dve.wait_ge(s_ffg, 16)
            for t in range(TT):
                for k in range(TOPK):
                    i = TOPK * t + k
                    dve.wait_ge(s_yg[i % 8], 16 * (i // 8 + 1))
                    if k:
                        dve.wait_ge(s_ac, i)
                    nc.vector.scalar_tensor_tensor(out=xres[:, t, :], in0=yg[:, i % 8, :], scalar=Gt[:, t, k:k + 1],
                                                   in1=xres[:, t, :], op0=ALU.mult, op1=ALU.add).then_inc(s_ac, 1)
                if t:
                    root(t - 1)
                    final(t - 1)
            root(TT - 1)
            final(TT - 1)

        @block.tensor
        def _(pe):
            pe.wait_ge(s_const, 2)
            pe.wait_ge(s_par, 12 * 16)
            pe.transpose(PS[:, 6, 0:NPV], PVr[0:NPV, :], ident[0:NPV, 0:NPV]).then_inc(s_pvt, 1)
            pe.transpose(PS[:, 7, 0:TAPS * CT], CWr[:], ident[0:TAPS * CT, 0:TAPS * CT]).then_inc(s_pvt, 1)
            pe.wait_ge(s_pvc, 2)

            def norm_turn(n, tiles):
                N = norms[n]
                for t in range(tiles):
                    pe.wait_ge(N["scaled"], t + 1)
                    if t >= 4:
                        pe.wait_ge(N["drained"], 2 * (t - 3))
                    for b in range(2):
                        for k in range(4):
                            ins = pe.transpose(PS[:, 2 * (t % 4) + b, P * k:P * (k + 1)],
                                               XN[:, t % 2, P * (4 * b + k):P * (4 * b + k + 1)], ident[:])
                        ins.then_inc(N["turned"], 1)
                pe.wait_ge(N["drained"], 2 * tiles)

            g = 0
            n = 0

            def arrived():
                pe.wait_ge(s_ring[g % NR], 16 * (g // NR + 1))

            def group(seg, n, out, lhs, rhs):
                if n >= 8:
                    pe.wait_ge(s_dr[seg], n - 7)
                for k in range(KT):
                    ins = pe.matmul(out, lhs(k), rhs(k), start=(k == 0), stop=(k == KT - 1))
                ins.then_inc(s_mm[seg], 1)

            def chunk_T(seg, src, fts=2, width=512):
                nonlocal g, n
                arrived()
                halves = src.shape[2] // width
                for ft in range(fts):
                    for th in range(halves):
                        group(seg, n, bank_groups(n, width),
                              lambda k: ring[:, g % NR, k, P * ft:P * (ft + 1)],
                              lambda k: src[:, k, width * th:width * (th + 1)])
                        n += 1
                g += 1

            def chunk_tm(seg, src, tiles):
                nonlocal g, n
                arrived()
                for t in range(tiles):
                    group(seg, n, bank_groups(n, 256), lambda k: src(k)[:, P * t:P * (t + 1)],
                          lambda k: ring[:, g % NR, k, :])
                    n += 1
                g += 1

            norm_turn("m", MT)
            norm_turn("x", TT)
            for c in range(4):
                chunk_T("mem", mT, width=256)
            for c in range(4):
                chunk_tm("mem", lambda k: mT[:, k, :], MT)
            pe.wait_ge(s_dr["mem"], 16)
            n = 0
            chunk_T("in", hT, fts=1)
            for c in range(6):
                chunk_T("in", hT)
            for c in range(4):
                chunk_tm("in", lambda k: hT[:, k, :], TT)
            pe.wait_ge(s_dr["in"], 58)

            pe.wait_ge(s_cv, TAPS * CT)
            for th in range(2):
                for c in range(CT):
                    ins = pe.matmul(PS[:, th, :], ones[:], yT[:, c, 512 * th:512 * (th + 1)],
                                    start=(c == 0), stop=(c == CT - 1))
                ins.then_inc(s_lnp, 1)
            pe.wait_ge(s_lna, CT)
            for th in range(2):
                for c in range(CT):
                    ins = pe.matmul(PS[:, 2 + th, :], ones[:], o_gla[:, 2 * c + th, :],
                                    start=(c == 0), stop=(c == CT - 1))
                ins.then_inc(s_lnp, 1)
            pe.wait_ge(s_lnv, 10)

            for p in range(2):
                if p:
                    pe.wait_ge(s_oe, 16 * p)
                for i in range(4):
                    d, th = i // 2, i % 2
                    pe.matmul(PS[:, i, :], W2[:, d, P * p:P * (p + 1)], gT[:, 512 * th:512 * (th + 1)],
                              start=True, stop=True).then_inc(s_z, 1)
                for l in range(8):
                    L = 8 * p + l
                    if l == 0:
                        pe.wait_ge(s_zmin, 4 * (p + 1))
                        pe.wait_ge(s_zabs, 4 * (p + 1))
                        if p:
                            pe.wait_ge(s_st, 14 * p)
                    else:
                        pe.wait_ge(s_kq, 9 * p + l)
                        if l >= 2:
                            pe.wait_ge(s_sel, 4 * (L - 1))
                    K_, Q_ = (kT[:, p, :], qT[:, p, :]) if l == 0 else (KQ[:, 0, :], KQ[:, 1, :])
                    for b in range(4):
                        hh, half = b // 2, b % 2
                        for w in range(4):
                            a = slice(P * (4 * half + w), P * (4 * half + w + 1))
                            hp = slice(GDK * hh, GDK * (hh + 1))
                            ins = pe.matmul(PS[:, 4 * (L % 2) + b, P * w:P * (w + 1)], K_[hp, a], Q_[hp, a],
                                            start=True, stop=True)
                        ins.then_inc(s_gram, 1)
                pe.wait_ge(s_kq, 9 * p + 8)
                pe.wait_ge(s_sel, 32 * (p + 1))
                for b in range(4):
                    for i in range(4):
                        m = 4 * b + i
                        ins = pe.transpose(PS[:, b, P * i:P * (i + 1)],
                                           KQ[:, m // TT, P * (m % TT):P * (m % TT + 1)], ident[:])
                    ins.then_inc(s_ket, 1)
                pe.wait_ge(s_kev, 4 * (p + 1))
                for i in range(14):
                    d = i % 2
                    w = i // 2 if d == 0 else TT - 1 - i // 2
                    if i >= 4:
                        pe.wait_ge(s_st, 14 * p + i - 3)
                    m = TT * d + w
                    pe.matmul(PS[:, 4 + i % 4, 0:256], KEt[:, m // 4, P * (m % 4):P * (m % 4 + 1)],
                              v_tm[:, w, 256 * p:256 * (p + 1)], start=True, stop=True).then_inc(s_U, 1)
                pe.wait_ge(s_kq, 9 * p + 9)
                pe.wait_ge(s_st, 14 * (p + 1))
                for i in range(16):
                    w, hh = i // 2, i % 2
                    h = 2 * p + hh
                    if i >= 4:
                        pe.wait_ge(s_oe, 16 * p + i - 3)
                    o = PS[:, i % 4, 0:P]
                    hp = slice(GDK * hh, GDK * (hh + 1))
                    tw = slice(P * w, P * (w + 1))
                    pe.matmul(o, Ssc[:, hh, w, :], v_tm[:, w, P * h:P * (h + 1)], start=True, stop=False)
                    pe.matmul(o, KQ[hp, 0, tw], ST[hp, 0, w, :], start=False, stop=False)
                    pe.matmul(o, KQ[hp, 1, tw], ST[hp, 1, w, :], start=False, stop=True).then_inc(s_op, 1)
            pe.wait_ge(s_ov, 8)
            pe.wait_ge(s_oe, 32)
            for c in range(CT):
                for b in range(2):
                    for i in range(4):
                        ins = pe.transpose(PS[:, 2 * c + b, P * i:P * (i + 1)],
                                           o_gla[:, 4 * b + i, P * c:P * (c + 1)], ident[:])
                    ins.then_inc(s_at, 1)
            pe.wait_ge(s_ae, 8)
            pe.wait_ge(s_lnv, 19)
            n = 0
            for c in range(4):
                chunk_tm("out", lambda k: aT[:, k, :] if k < CT else yT[:, k - CT, :], TT)
            pe.wait_ge(s_dr["out"], 32)
            norm_turn("y", TT)
            n = 0
            for c in range(4):
                chunk_T("q", hT)
            pe.wait_ge(s_dr["q"], 16)
            for h in range(XH):
                def turn(t):
                    i = TT * h + t
                    pe.wait_ge(s_sv, 4 * (i + 1))
                    if i >= 2:
                        pe.wait_ge(s_pc, i - 1)
                    for m in range(MT):
                        ins = pe.transpose(PS[:, 2 + i % 2, P * m:P * (m + 1)], pr[:, i % 2, P * m:P * (m + 1)],
                                           ident[:])
                    ins.then_inc(s_pt, 1)

                for t in range(TT):
                    i = TT * h + t
                    if i >= 2:
                        pe.wait_ge(s_pe, i - 1)
                    for k in range(2):
                        ins = pe.matmul(PS[:, i % 2, 0:256], qxT[:, 2 * h + k, P * t:P * (t + 1)],
                                        kx[:, 2 * h + k, :], start=(k == 0), stop=(k == 1))
                    ins.then_inc(s_sc, 1)
                    if t:
                        turn(t - 1)
                turn(TT - 1)
                pe.wait_ge(s_pc, TT * (h + 1))
                if h:
                    pe.wait_ge(s_ax, 4 * h)
                for b in range(4):
                    ft, th = b // 2, b % 2
                    for m in range(MT):
                        ins = pe.matmul(PS[:, 4 + b, :], vx[:, m, XDH * h + P * ft:XDH * h + P * (ft + 1)],
                                        pT[:, h % 2, m, 512 * th:512 * (th + 1)], start=(m == 0), stop=(m == 1))
                    ins.then_inc(s_av, 1)
            pe.wait_ge(s_ax, 16)
            n = 0
            for c in range(4):
                chunk_tm("o", lambda k: oxT[:, k, :], TT)
            pe.wait_ge(s_dr["o"], 32)

            def router(t):
                pe.wait_ge(s_h3e, 2 * (t + 1))
                if t >= 2:
                    pe.wait_ge(s_lg, t - 1)
                if t == 0:
                    pe.wait_ge(s_rpar, 7 * 16)
                for k in range(KT):
                    ins = pe.matmul(PS[:, 4 + t % 2, 0:E], h3T[:, t % 2, k, :], rw[:, k, :],
                                    start=(k == 0), stop=(k == KT - 1))
                ins.then_inc(s_lgp, 1)

            for t in range(TT):
                pe.wait_ge(norms["z"]["scaled"], t + 1)
                if t >= 2:
                    pe.wait_ge(s_h3e, 2 * (t - 1))
                for b in range(2):
                    for k in range(4):
                        ins = pe.transpose(PS[:, 2 * (t % 2) + b, P * k:P * (k + 1)],
                                           XN[:, t % 2, P * (4 * b + k):P * (4 * b + k + 1)], ident[:])
                    ins.then_inc(norms["z"]["turned"], 1)
                if t:
                    router(t - 1)
            router(TT - 1)
            pe.wait_ge(s_rt, RT_M)
            for t in range(TT):
                o = PS[:, 6, E * t:E * (t + 1)]
                ins = pe.matmul(o, before[:], M[:, t, :], start=True, stop=(t == 0))
                for j in range(t):
                    ins = pe.matmul(o, ones[:], M[:, j, :], start=False, stop=(j == t - 1))
            ins.then_inc(s_rk, 1)
            for t in range(TT):
                ins = pe.matmul(PS[:, 7, 0:E], ones[:], M[:, t, :], start=(t == 0), stop=(t == TT - 1))
            ins.then_inc(s_rk, 1)
            pe.wait_ge(s_rt, RT_GD)
            pe.wait_ge(s_h3e, 2 * TT)
            for b in range(2):
                for i in range(4):
                    ins = pe.transpose(PS[0:E, b, P * i:P * (i + 1)], GD[:, 4 * b + i, :], ident[:])
                ins.then_inc(s_gdt, 1)
            pe.wait_ge(s_lg, TT)
            for t in range(TT):
                pe.wait_ge(s_oh, 3 * (t + 1))
                for k in range(TOPK):
                    ins = pe.matmul(PS[:, 4, 0:NB], rowhot[:, t % 2, k, :], blkhot[:, t % 2, k, :],
                                    start=(t == 0 and k == 0), stop=(t == TT - 1 and k == TOPK - 1))
                ins.then_inc(s_tm, 1)
            pe.wait_ge(s_gde, 2)
            for t in range(TT):
                for b in range(2):
                    i = 2 * t + b
                    if i >= 4:
                        pe.wait_ge(s_bdr, i - 3)
                    pe.matmul(PS[:, i % 4, :], GDT[:, P * t:P * (t + 1)], bdn[:, 512 * b:512 * (b + 1)],
                              start=True, stop=True).then_inc(s_bd, 1)
            pe.wait_ge(s_tab, 1)

            def turn_tokens(t):
                pe.wait_ge(s_xsl, 16 * (t + 1))
                for b in range(2):
                    for k in range(4):
                        ins = pe.transpose(PS[:, 6 + b, P * k:P * (k + 1)], xs[:, P * (4 * b + k):P * (4 * b + k + 1)],
                                           ident[:])
                    ins.then_inc(s_xt, 1)

            def turn_hidden(t):
                pe.wait_ge(s_hid, 2 * t + 2)
                pe.wait_ge(s_xlo, 2 * t + 4)
                for b in range(2):
                    for k in range(4):
                        ins = pe.transpose(PS[:, 6 + b, P * k:P * (k + 1)],
                                           hid[:, P * (4 * b + k):P * (4 * b + k + 1)], ident[:])
                    ins.then_inc(s_ht, 1)

            def split_products(bank, hi, lo, whi_, wlo_, stop):
                pe.matmul(PS[:, bank, :], hi, whi_, start=False, stop=False)
                pe.matmul(PS[:, bank, :], hi, wlo_, start=False, stop=False)
                return pe.matmul(PS[:, bank, :], lo, whi_, start=False, stop=stop)

            def up(t, c0):
                pe.wait_ge(s_xlo, 2 * t + 2)
                pe.wait_ge(s_bsel, t + 1)
                if c0 == 0:
                    pe.wait_ge(s_g, 2 * t)
                    pe.wait_ge(s_upr, 2 * t)
                for n in range(4):
                    pe.matmul(PS[:, n, :], SEL[:], bup[:, 512 * n:512 * (n + 1)], start=True, stop=False)
                for k in range(KT):
                    c = c0 + k
                    wait_lo(pe, t, c)
                    s_ = chunk_slot(c, NSPL)
                    for n in range(4):
                        cols = slice(512 * n, 512 * (n + 1))
                        ins = split_products(n, xhi[:, k, :], xlo[:, k, :], whi[:, s_, cols], wlo[:, s_, cols],
                                             k == KT - 1)
                    ins.then_inc(s_wmm, 1)

            def down(t):
                pe.wait_ge(s_hlo, 2 * t)
                pe.wait_ge(s_yev, 2 * t - 1)
                for c in range(8, 12):
                    wait_lo(pe, t, c)
                    s_ = chunk_slot(c, NSPL)
                    for kk in range(2):
                        k = 2 * (c - 8) + kk
                        for n in range(2):
                            cols = slice(FF * kk + 512 * n, FF * kk + 512 * (n + 1))
                            if k == 0:
                                pe.matmul(PS[:, 4 + n, :], hhi[:, k, :], whi[:, s_, cols], start=True, stop=False)
                                pe.matmul(PS[:, 4 + n, :], hhi[:, k, :], wlo[:, s_, cols], start=False, stop=False)
                                ins = pe.matmul(PS[:, 4 + n, :], hlo[:, k, :], whi[:, s_, cols], start=False,
                                                stop=False)
                            else:
                                ins = split_products(4 + n, hhi[:, k, :], hlo[:, k, :], whi[:, s_, cols],
                                                     wlo[:, s_, cols], k == KT - 1)
                    ins.then_inc(s_wmm, 1)

            used_ = pe.value_load(usedb[0:1, 0:1], min_val=1, max_val=NBLK)
            turn_tokens(0)
            up(0, 4)
            turn_tokens(1)
            turn_hidden(0)
            with pe.Fori(1, NBLK + 1) as t:
                with pe.If(t <= used_):
                    up(t, 0)
                    pe.wait_ge(s_hlo, 2 * t)
                    turn_tokens(t + 1)
                    down(t)
                    turn_hidden(t)


_INS = ["x", "mem", "norm_mix_g", "w_in", "gate_w2_fwd", "gate_b_fwd", "gate_w2_bwd", "gate_b_bwd",
        "gla_norm_g", "conv_w", "conv_b", "conv_ln_g", "conv_ln_b", "w_out", "norm_xattn_g", "norm_mem_g",
        "xattn_wq", "xattn_wk", "xattn_wv", "xattn_wo", "norm_ffn_g", "router_w", "router_b", "exp_w_up",
        "exp_b_up", "exp_w_down", "exp_b_down", "final_norm_g"]


def kernel(**inputs):
    import numpy as np
    from concourse import bacc
    from concourse.bass_utils import run_bass_kernel_spmd

    nc = bacc.Bacc("TRN2", target_bir_lowering=False, num_devices=1)
    arrays, aps = {}, {}
    for name in _INS:
        a = np.ascontiguousarray(inputs[name])
        arrays["in_" + name] = a
        aps[name] = nc.dram_tensor("in_" + name, a.shape, mybir.dt.from_np(a.dtype), kind="ExternalInput").ap()
    aps["out"] = nc.dram_tensor("out_y", (1, S, D), F, kind="ExternalOutput").ap()
    build(nc, aps)
    r = run_bass_kernel_spmd(nc, [arrays], core_ids=[0])
    return r.results[0]["out_y"]
```

```python
from contextlib import ExitStack

import concourse.bass as bass
from concourse import mybir

F = mybir.dt.float32
FR = mybir.dt.float32r
BF = mybir.dt.bfloat16
I32 = mybir.dt.int32
U32 = mybir.dt.uint32
U8 = mybir.dt.uint8
ALU = mybir.AluOpType
ACT = mybir.ActivationFunctionType
X = mybir.AxisListType.X

P = 128
S = 1024
D = 1024
KT = D // P
TT = S // P
MT = 2
GH, GDV, GDK = 4, 128, 64
GK = GH * GDK
GW = GH * GDV
CW_ = 512
CT = CW_ // P
TAPS = 31
PAD = TAPS // 2
RANK = 16
TAU = 16.0
XH = 4
XDH = D // XH
E = 32
TOPK = 4
FF = 1024
ALPHA, LIMIT = 1.702, 7.0
RMS_EPS, LN_EPS = 1e-6, 1e-5
Q0, K0, V0, R0 = 0, GK, 2 * GK, 2 * GK + GW
G0 = R0 + GW
A0 = G0 + 2 * RANK
B0 = A0 + CW_
NBLK = (S * TOPK + E * (P - 1) + P - 1) // P
NB = 66
NVIS = (S * TOPK + E * (2 * P - 1)) // (2 * P)
NV = NVIS + 3
RT_M, RT_GD = 9, 17
LEVELS = [64, 32, 16, 8, 4, 2, 1]
KIB = 1024
BASE = 16512


def build(nc, A):
    with ExitStack() as ctx:
        def sb(name, shape, dt, kib):
            return nc.alloc_sbuf_tensor_at(name, shape, dt, offset=BASE + int(kib * KIB))

        def sem(name):
            return ctx.enter_context(nc.semaphore(name))

        arena = ctx.enter_context(nc.sbuf_tensor("arena", [P, 212800], U8))
        assert arena is not None
        PS = ctx.enter_context(nc.psum_tensor("PS", [P, 8, 512], F))

        NR = 4
        ring = sb("ring", [P, NR, KT, 256], F, 0)
        hT = sb("hT", [P, KT, S], F, 32)
        o_gla = sb("o_gla", [P, TT, GW], F, 32)
        EX = sb("EX", [P, 2, S], F, 48)
        KQ = sb("KQ", [P, 2, S], F, 56)
        KQ2 = sb("KQ2", [P, 2, S], F, 120)
        KEt = sb("KEt", [P, 4, 512], F, 48)
        SR = sb("SR", [P, TT, GW], F, 48)
        xres = sb("xres", [P, TT, D], F, 64)
        qT = sb("qT", [P, 2, S], F, 64)
        kT = sb("kT", [P, 2, S], F, 72)
        v_tm = sb("v_tm", [P, TT, GW], F, 80)
        r_tm = sb("r_tm", [P, TT, GW], F, 96)
        UW = S + 2 * PAD
        u_pad = sb("u_pad", [P, CT, UW], F, 112)
        qxT = sb("qxT", [P, KT, S], F, 149)
        mT = sb("mT", [P, KT, MT * P], F, 173)
        sig = sb("sig", [P, S], F, 129)
        yT = sb("yT", [P, CT, S], F, 133)
        mem_tm = sb("mem_tm", [P, MT, D], F, 133)
        Bf = sb("Bf", [P, S], F, 149)
        Rb = sb("Rb", [P, S], F, 153)
        Ssc = sb("Ssc", [P, 2, TT, P], F, 157)
        ST = sb("ST", [P, 2, TT, P], F, 165)
        aT = sb("aT", [P, CT, S], F, 149)
        kx = sb("kx", [P, KT, MT * P], F, 181)
        vx = sb("vx", [P, MT, D], F, 112)
        XN = sb("XN", [P, 2, D], F, 189)
        gT = sb("gT", [2 * RANK, S], F, 189)
        pr = sb("pr", [P, 2, MT * P], F, 130)
        pT = sb("pT", [P, 2, MT, S], F, 133)
        oxT = sb("oxT", [P, KT, S], F, 32)
        ident = sb("ident", [P, P], F, 197)
        ones = sb("ones", [P, P], F, 197.5)
        before = sb("before", [P, P], F, 198)
        masks = sb("masks", [P, 7, P], U8, 198.5)
        W2 = sb("W2", [2 * RANK, 2, GK], F, 199.5)
        PV = sb("PV", [P, 64], F, 201.5)
        CWT = sb("CWT", [P, TAPS * CT], F, 201.75)
        ngb = sb("ngb", [P, GDV], F, 202.25)
        st8 = sb("st8", [P, 4, 32], F, 202.75)
        TTd = sb("TTd", [P, 2, 2, TT], F, 203.25)
        smx = sb("smx", [P, 4, 4], F, 203.4375)
        xor = sb("xor", [P, P], I32, 203.5)
        mtmp = sb("mtmp", [P, P], F, 204)
        PVr = sb("PVr", [64, P], F, 204.5)
        CWr = sb("CWr", [TAPS * CT, P], F, 205)
        pid = sb("pid", [P, 8], F, 205.5)
        iot = sb("iot", [P, P], F, 206)

        h3T = sb("h3T", [P, 2, KT, P], F, 96)
        rw = sb("rw", [P, KT, E], F, 104)
        h3 = sb("h3", [P, TT, D], F, 32)
        rbb = sb("rbb", [P, E], F, 105)
        LG = sb("LG", [P, TT, E], F, 106)
        MX = sb("MX", [P, TT, 8], F, 107)
        IX = sb("IX", [P, TT, 8], U32, 107.25)
        IXf = sb("IXf", [P, TT, 8], F, 107.5)
        gsum = sb("gsum", [P, 2, TT], F, 107.75)
        OH = sb("OH", [P, TT, TOPK, E], F, 108)
        M = sb("M", [P, TT, E], F, 112)
        slot0 = sb("slot0", [P, TT, E], F, 113)
        ex1 = sb("ex1", [P, 8, E], F, 114)
        exi = sb("exi", [P, 2, E], I32, 115)
        tmpA = sb("tmpA", [P, NB * E], F, 116)
        tmpC = sb("tmpC", [P, NV * E], F, 168)
        rowhot = sb("rowhot", [P, 2, TOPK, P], F, 125)
        blkhot = sb("blkhot", [P, TT * TOPK, NB], F, 175)
        GD = sb("GD", [P, TT, E], F, 132)
        GDT = sb("GDT", [E, S], F, 133)
        bdn = sb("bdn", [E, D], F, 137)
        di = sb("di", [P, 3, TT * TOPK], I32, 141)
        df = sb("df", [P, 3, TT * TOPK], F, 141.5)
        Mb = sb("Mb", [P, TT, E], BF, 142)
        onesb = sb("onesb", [P, P], BF, 142.5)
        beforeb = sb("beforeb", [P, P], BF, 142.75)
        gfb = sb("gfb", [P, D], F, 189)
        bstage = sb("bstage", [P, 2 * FF], F, 152)
        Gt = sb("Gt", [P, TT, TOPK], F, 198.5)
        rowof = sb("rowof", [P, TT * TOPK], U32, 198.75)
        TM = sb("TM", [P, NB], U32, 199)
        EB = sb("EB", [P, NV], F, 199.375)
        VT = sb("VT", [P, 3, NV], I32, 199.625)
        usedb = sb("usedb", [P, 1], I32, 200.5)
        idxc = sb("idxc", [P, 2], U32, 200.5625)
        pmod = sb("pmod", [P, 2], F, 200.625)
        pmi = sb("pmi", [P, 2], I32, 200.6875)
        SEL = sb("SEL", [P, P], BF, 200.75)
        vt = sb("vt", [P, 4, NV], F, 201)
        NRAW, NSPL = 4, 4
        raw = sb("raw", [P, NRAW, 4, 512], F, 0)
        whi = sb("whi", [P, NSPL, 4, 512], FR, 96)
        wlo = sb("wlo", [P, NSPL, 4, 512], FR, 32)
        xhi = sb("xhi", [P, 2, KT, P], FR, 128)
        xlo = sb("xlo", [P, 2, KT, P], FR, 136)
        hhi = sb("hhi", [P, 2, KT, P], FR, 144)
        hlo = sb("hlo", [P, 2, KT, P], FR, 152)
        xs = sb("xs", [P, 2, D], F, 160)
        glu = sb("glu", [P, 2, 512], F, 168)
        sgm = sb("sgm", [P, 2, 512], F, 172)
        hid = sb("hid", [P, 2, FF], F, 176)
        bup = sb("bup", [P, 2 * FF], BF, 184)
        yb = sb("yb", [P, 2, D], F, 189)
        yg = sb("yg", [P, 8, D], F, 0)
        fo = sb("fo", [P, 2, D], F, 32)
        fgb = sb("fgb", [P, D], F, 40)
        sqs = sb("sqs", [P, D], F, 44)
        h3_dram = nc.dram_tensor("h3_scratch", (S, D), F, kind="Internal").ap()
        ys_dram = nc.dram_tensor("ys_scratch", ((NBLK + 1) * P, D), F, kind="Internal").ap()

        s_par = sem("params_loaded")
        s_const = sem("constants_built")
        s_mask = sem("masks_built")
        s_w2z = sem("w2_zeroed")
        s_pvt = sem("vectors_transposed")
        s_pvc = sem("vectors_ready")
        s_ring = [sem(f"chunk_loaded{i}") for i in range(NR)]
        s_xld = [sem(f"x_loaded{i}") for i in range(4)]
        norms = {}
        for n in ("m", "x", "y", "z"):
            norms[n] = {k: sem(f"norm_{n}_{k}") for k in
                        ("stats_by_scalar", "stats_by_vector", "scaled", "turned") + ("drained",) * (n != "z")}
        norms["m"]["loaded"] = sem("memory_loaded")
        s_mm = {k: sem(f"{k}_product") for k in ("mem", "in", "out", "q", "o")}
        s_dr = {k: sem(f"{k}_drained") for k in ("mem", "in", "out", "q", "o")}
        s_pad = sem("margins_zeroed")
        s_u = sem("glu_ready")
        s_cv = sem("conv_tap")
        s_lnp, s_lna, s_lnv = sem("ln_by_tensor"), sem("ln_by_scalar"), sem("ln_by_vector")
        s_z, s_zabs, s_zln, s_zmin, s_la, s_scan, s_tot, s_rb, s_dec = (
            sem(n) for n in ("gate_product", "gate_abs", "gate_softplus", "gate_min", "log_decay", "scanned",
                             "totals", "suffix_ready", "window_decay"))
        s_sub, s_ex, s_kq, s_gram, s_sel = (
            sem(n) for n in ("exponent_ready", "decay_ready", "decayed_kq", "gram_product", "scores_selected"))
        s_ket, s_kev, s_U, s_st, s_st0, s_op, s_oe = (
            sem(n) for n in ("k_turned", "k_token_major", "window_update", "state_ready", "state_zero", "gla_product",
                             "gla_drained"))
        s_ov, s_oa, s_at, s_ae = (sem(n) for n in ("o_norm_by_vector", "o_norm_by_scalar", "a_turned", "a_ready"))
        s_sc, s_sv, s_pe, s_pt, s_pc, s_av, s_ax = (
            sem(n) for n in ("xscores", "softmax_by_vector", "xprob", "xprob_turned", "xprob_T", "xvalue", "xout"))
        s_xre = sem("x_reloaded_and_rows_filled")
        s_out = [sem(f"out_stored{i}") for i in range(2)]
        s_rpar, s_ffg, s_h3s = sem("router_loaded"), sem("final_gain_loaded"), [sem(f"h3_stored{i}") for i in range(2)]
        s_h3e, s_lgp, s_lg, s_top, s_rt = (sem(n) for n in ("h3_turned_out", "logit_product", "logits", "top8", "routing_step"))
        s_gx, s_rk, s_rkr, s_oh, s_tm, s_gdt, s_gde, s_bd, s_bdr = (
            sem(n) for n in ("gate_exp", "rank_product", "rank_read", "row_onehot", "token_map_product",
                             "gates_turned", "gates_turned_out", "bias_down_product", "bias_down_added"))
        s_bup, s_tab, s_rmi = sem("bias_parts"), sem("tables_ready"), sem("partition_ids")
        s_raw = [sem(f"expert_chunk_loaded{i}") for i in range(NRAW)]
        s_whi, s_wlv, s_wlp, s_wmm = (sem(n) for n in ("chunk_hi", "chunk_lo_by_vector", "chunk_lo_by_pool",
                                                       "chunk_multiplied"))
        s_idx, s_xsl, s_xt, s_xhi, s_xlo = (sem(n) for n in ("index_column", "tokens_gathered", "tokens_turned",
                                                             "tokens_hi", "tokens_lo"))
        s_bsel, s_g, s_upr, s_sg, s_hid, s_ht, s_hhi, s_hlo = (
            sem(n) for n in ("bias_selector", "glu_clamped", "up_banks_read", "expert_sigmoid", "hidden", "hidden_turned", "hidden_hi", "hidden_lo"))
        s_yev, s_yst = sem("rows_drained"), sem("rows_stored")
        s_yg = [sem(f"rows_gathered{i}") for i in range(8)]
        s_ac, s_fa, s_fv, s_fo = (sem(n) for n in ("row_added", "final_by_scalar", "final_by_vector",
                                                   "final_scaled"))

        w_in, w_out = A["w_in"][0], A["w_out"][0]
        wq, wk, wv, wo = (A[f"xattn_w{c}"][0] for c in "qkvo")
        x_in = A["x"][0].rearrange("(t p) d -> p t d", p=P)
        mem_in = A["mem"][0].rearrange("(t p) d -> p t d", p=P)
        out_v = A["out"][0].rearrange("(t p) d -> p t d", p=P)

        chunks = ([(w_in, G0), (w_in, A0), (w_in, B0), (w_in, A0 + 256), (w_in, B0 + 256),
                     (w_in, Q0), (w_in, K0), (w_in, V0), (w_in, V0 + 256), (w_in, R0), (w_in, R0 + 256)]
                  + [(wk, 256 * c) for c in range(4)] + [(wv, 256 * c) for c in range(4)]
                  + [(w_out, 256 * c) for c in range(4)] + [(wq, 256 * c) for c in range(4)]
                  + [(wo, 256 * c) for c in range(4)])
        used = ([("in", n) for n in (2, 6, 10, 14, 18, 22, 26, 34, 42, 50, 58)]
                + [("mem", 2 * (c + 1)) for c in range(8)]
                + [("out", 8 * (c + 1)) for c in range(4)] + [("q", 4 * (c + 1)) for c in range(4)]
                + [("o", 8 * (c + 1)) for c in range(4)])
        GX, GM, GA, ZB, CB, LG_, LB = 0, 8, 16, 24, 28, 32, 36
        NPV = 40

        def bank_groups(n, width=512):
            return PS[:, n % 8, 0:width]

        w_up, w_dn = A["exp_w_up"][0], A["exp_w_down"][0]

        UPCOL = [0, FF, 512, FF + 512]

        def chunk_slot(c, n):
            return (c - 4) % n

        def wait_lo(eng, t, c):
            if c % 3 == 0:
                eng.wait_ge(s_wlp, 4 * t + (c - 3) // 3)
            else:
                eng.wait_ge(s_wlv, 8 * t + (c - 3) - (c - 3) // 3)

        def wait_raw(eng, t, c):
            eng.wait_ge(s_raw[chunk_slot(c, NRAW)], 16 * 12 // NRAW * t + 16 * ((c - 4) // NRAW + 1))

        def wait_multiplied(eng, t, c):
            eng.wait_ge(s_wmm, 12 * t + c - 3)

        block = ctx.enter_context(nc.Block())

        @block.sync
        def _(sp):
            sp.dma_start(mem_tm[:], mem_in).then_inc(norms["m"]["loaded"], 16)
            for i in range(4):
                sp.dma_start(xres[:, 2 * i:2 * i + 2, :], x_in[:, 2 * i:2 * i + 2, :]).then_inc(s_xld[i], 16)
            for g, (w, c0) in enumerate(chunks):
                if g >= NR:
                    sp.wait_ge(s_mm[used[g - NR][0]], used[g - NR][1])
                sp.dma_start(ring[:, g % NR], w[:, c0:c0 + 256].rearrange("(k p) n -> p k n", p=P)
                             ).then_inc(s_ring[g % NR], 16)
                if g == 18 + NR:
                    sp.wait_ge(s_const, 1)
                    fresh_rows = ys_dram[S * TOPK:(NBLK + 1) * P, :].rearrange("(p b) (r c) -> p (b r) c", p=P, c=P)
                    sp.dma_start(fresh_rows, ones[:].unsqueeze(1).broadcast_to(
                        [P, fresh_rows.shape[1], P])).then_inc(s_xre, 16)
                    sp.wait_ge(s_oe, 2 * 16)
                    sp.dma_start(xres[:], x_in).then_inc(s_xre, 16)
            for t in range(TT):
                sp.wait_ge(norms["z"]["scaled"], t + 1)
                sp.dma_start(h3_dram[P * t:P * (t + 1), :], h3[:, t, :]).then_inc(s_h3s[0], 16)
            def load_chunk(t, c, e_up, e_dn, fresh=False):
                if not fresh:
                    wait_lo(sp, t, c - NRAW)
                if e_dn is None or c < 8:
                    j = c - 4 if e_dn is None and c >= 4 else c
                    w, e, col = w_up, e_up, UPCOL[j // 2]
                else:
                    j = c - 8
                    w, e, col = w_dn, e_dn, 512 * (j // 2)
                src = w[bass.ds(e, 1), 512 * (j % 2):512 * (j % 2 + 1), col:col + 512]
                sp.dma_start(raw[:, chunk_slot(c, NRAW)], src.rearrange("e (k p) n -> p (e k) n", p=P)
                             ).then_inc(s_raw[chunk_slot(c, NRAW)], 16)

            def expert(t):
                return sp.value_load(VT[0:1, 0, bass.ds(t, 1)], min_val=0, max_val=E - 1)

            sp.wait_ge(s_tab, 1)
            used_ = sp.value_load(usedb[0:1, 0:1], min_val=1, max_val=NVIS)
            e0, e1 = expert(0), expert(1)
            for c in range(4, 12):
                load_chunk(0, c, e0, None, fresh=c < 4 + NRAW)
            for c in range(3):
                load_chunk(1, c, e1, None)
            with sp.Fori(1, NVIS + 1) as t:
                with sp.If(t <= used_):
                    eu, ed, en = expert(t), expert(t - 1), expert(t + 1)
                    for c in range(3, 12):
                        load_chunk(t, c, eu, ed)
                    for c in range(3):
                        load_chunk(t + 1, c, en, ed)
            wait_lo(sp, used_ + 1, 1)
            wait_lo(sp, used_ + 1, 2)
            wait_lo(sp, used_ + 1, 0)
            sp.dma_start(fgb[:], A["final_norm_g"].partition_broadcast(P)).then_inc(s_ffg, 16)
            for t in range(TT):
                sp.wait_ge(s_fo, t + 1)
                sp.dma_start(out_v[:, t, :], fo[:, t % 2, :]).then_inc(s_out[t % 2], 16)
            for i in range(2):
                sp.wait_ge(s_out[i], 16 * TT // 2)

        @block.gpsimd
        def _(pool):
            nc.gpsimd.memset(ones[:], 1.0).then_inc(s_const, 1)
            nc.gpsimd.memset(W2[:], 0.0).then_inc(s_w2z, 1)
            pool.wait_ge(s_const, 1)
            nc.gpsimd.affine_select(out=ident[:], in_=ones[:], compare_op=ALU.is_equal, fill=0.0, base=0,
                                    pattern=[[-1, P]], channel_multiplier=1).then_inc(s_const, 1)
            nc.gpsimd.affine_select(out=before[:], in_=ones[:], compare_op=ALU.is_gt, fill=0.0, base=0,
                                    pattern=[[1, P]], channel_multiplier=-1).then_inc(s_const, 1)
            nc.gpsimd.iota(xor[:], pattern=[[1, P]], base=0, channel_multiplier=0).then_inc(s_const, 1)
            nc.gpsimd.iota(mtmp[:].bitcast(I32), pattern=[[0, P]], base=0, channel_multiplier=1).then_inc(s_const, 1)
            nc.gpsimd.iota(pid[:], pattern=[[P, 8]], base=0, channel_multiplier=1,
                           allow_small_or_imprecise_dtypes=True).then_inc(s_const, 1)
            nc.gpsimd.iota(iot[:], pattern=[[1, P]], base=0, channel_multiplier=0,
                           allow_small_or_imprecise_dtypes=True).then_inc(s_const, 1)
            for c in range(CT):
                nc.gpsimd.memset(u_pad[:, c, 0:PAD], 0.0).then_inc(s_pad, 1)
                nc.gpsimd.memset(u_pad[:, c, PAD + S:UW], 0.0).then_inc(s_pad, 1)
            for c in range(CT):
                pool.wait_ge(s_dr["in"], 2 + 8 * (c // 2) + 4 + 2 * (c % 2 + 1))
                uc = u_pad[:, c, PAD:PAD + S]
                nc.gpsimd.tensor_tensor(uc, uc, sig[:], ALU.mult).then_inc(s_u, 1)

            pool.wait_ge(s_mm["o"], 32)
            nc.gpsimd.memset(onesb[:], 1.0).then_inc(s_rmi, 1)
            nc.gpsimd.tensor_copy(beforeb[:], before[:]).then_inc(s_rmi, 1)
            pool.wait_ge(s_rpar, 7 * 16)
            b0, b1, b2 = (slice(E * i, E * (i + 1)) for i in range(3))
            bp = 0

            def part(ins):
                nonlocal bp
                bp += 1
                ins.then_inc(s_bup, 1)
                pool.wait_ge(s_bup, bp)

            part(nc.gpsimd.memset(bup[:], 0.0))
            part(nc.gpsimd.tensor_copy(bup[0:3 * E, :], bstage[0:3 * E, :]))
            for rows in (b1, b2):
                part(nc.gpsimd.tensor_tensor(bstage[rows, :], bstage[rows, :], bup[rows, :], ALU.subtract))
            for rows in (b1, b2):
                part(nc.gpsimd.tensor_copy(bup[rows, :], bstage[rows, :]))
            part(nc.gpsimd.tensor_tensor(bstage[b2, :], bstage[b2, :], bup[b2, :], ALU.subtract))
            part(nc.gpsimd.tensor_copy(bup[b2, :], bstage[b2, :]))

            pool.wait_ge(s_rt, 1)
            nc.gpsimd.iota(pmi[:], pattern=[[0, 2]], base=0, channel_multiplier=1).then_inc(s_rmi, 1)

            def index_columns(t):
                b0 = pool.value_load(VT[0:1, 1, bass.ds(t, 1)], min_val=0, max_val=NBLK - 1)
                nc.gpsimd.tensor_copy(idxc[:], TM[:, bass.ds(b0, 2)]).then_inc(s_idx, 1)
                pool.wait_ge(s_idx, t + 1)

            def gather():
                for b in range(2):
                    nc.gpsimd.indirect_dma_start(xs[:, b, :], None, h3_dram,
                                                 bass.IndirectOffsetOnAxis(ap=idxc[:, b:b + 1], axis=0)
                                                 ).then_inc(s_xsl, 16)

            def lo_by_pool(t, c):
                pool.wait_ge(s_whi, 12 * t + c - 3)
                nc.gpsimd.tensor_tensor(wlo[:, chunk_slot(c, NSPL), :], raw[:, chunk_slot(c, NRAW), :],
                                        whi[:, chunk_slot(c, NSPL), :].bitcast(F), ALU.subtract
                                        ).then_inc(s_wlp, 1)

            pool.wait_ge(s_tab, 1)
            pool.wait_ge(s_h3s[0], 16 * TT)
            used_ = pool.value_load(usedb[0:1, 0:1], min_val=1, max_val=NVIS)
            nc.gpsimd.memset(yb[:], 0.0).then_inc(s_yst, 1)
            index_columns(0)
            gather()
            lo_by_pool(0, 6)
            pool.wait_ge(s_xt, 1)
            index_columns(1)
            gather()
            lo_by_pool(0, 9)
            pool.wait_ge(s_xt, 2)
            index_columns(2)
            lo_by_pool(1, 0)
            gather()
            with pool.Fori(1, NVIS + 1) as t:
                with pool.If(t <= used_):
                    for c in (3, 6, 9):
                        lo_by_pool(t, c)
                    pool.wait_ge(s_xt, t + 2)
                    index_columns(t + 2)
                    lo_by_pool(t + 1, 0)
                    gather()
            pool.wait_ge(s_yst, 16 * used_ + 1)
            wait_lo(pool, used_ + 1, 0)
            wait_lo(pool, used_ + 1, 2)
            nc.gpsimd.tensor_tensor(pmod[:, 0:1], pmod[:, 0:1], pmod[:, 1:2], ALU.mult)
            for i in range(TT * TOPK):
                if i >= 8:
                    pool.wait_ge(s_ac, i - 7)
                nc.gpsimd.indirect_dma_start(yg[:, i % 8, :], None, ys_dram[0:NBLK * P, :],
                                             bass.IndirectOffsetOnAxis(ap=rowof[:, i:i + 1], axis=0)
                                             ).then_inc(s_yg[i % 8], 16)

        @block.scalar
        def _(act):
            act.wait_ge(s_w2z, 1)
            act.dma_start(W2[0:RANK, 0, :], A["gate_w2_fwd"][0]).then_inc(s_par, 16)
            act.dma_start(W2[RANK:2 * RANK, 1, :], A["gate_w2_bwd"][0]).then_inc(s_par, 16)
            for row, name, n in ((GX, "norm_mix_g", 8), (GM, "norm_mem_g", 8), (GA, "norm_xattn_g", 8),
                                 (ZB, "gate_b_fwd", 2), (ZB + 2, "gate_b_bwd", 2), (CB, "conv_b", 4),
                                 (LG_, "conv_ln_g", 4), (LB, "conv_ln_b", 4)):
                act.dma_start(PVr[row:row + n, :], A[name][0].rearrange("(k p) -> k p", p=P)).then_inc(s_par, 16)
            act.dma_start(CWr[:], A["conv_w"][0].rearrange("j (c p) -> (j c) p", p=P)).then_inc(s_par, 16)
            act.dma_start(ngb[:], A["gla_norm_g"][0].partition_broadcast(P)).then_inc(s_par, 16)

            def norm_stats(n, src, tiles):
                N = norms[n]
                for t in range(tiles):
                    if n == "m":
                        act.wait_ge(N["loaded"], 16)
                    elif n == "x":
                        act.wait_ge(s_xld[t // 2], 16)
                    elif n == "y":
                        act.wait_ge(s_dr["out"], 24 + t + 1)
                    else:
                        act.wait_ge(s_dr["o"], 24 + t + 1)
                    if t:
                        act.wait_ge(N["stats_by_scalar"], t)
                    nc.scalar.activation(sig[:], src[:, t, :], ACT.Square,
                                         accum_out=st8[:, 0, t:t + 1]).then_inc(N["stats_by_scalar"], 1)
                act.wait_ge(N["stats_by_vector"], 1)
                nc.scalar.activation(st8[:, 2, 0:tiles], st8[:, 1, 0:tiles], ACT.Sqrt).then_inc(N["stats_by_scalar"], 1)

            norm_stats("m", mem_tm, MT)
            act.wait_ge(norms["m"]["stats_by_vector"], 2)
            act.wait_ge(norms["m"]["scaled"], MT)
            norm_stats("x", xres, TT)

            def drain(seg, n):
                act.wait_ge(s_mm[seg], n + 1)
                return s_dr[seg]

            def drain_memory(groups):
                for n in groups:
                    d = drain("mem", n)
                    dst = kx[:, n, :] if n < 8 else vx[:, n % 2, 256 * ((n - 8) // 2):256 * ((n - 8) // 2 + 1)]
                    nc.scalar.copy(dst, PS[:, 4 + n % 4, 0:256]).then_inc(d, 1)

            n = 0
            for th in range(2):
                d = drain("in", n)
                if n == 0:
                    act.wait_ge(norms["x"]["turned"], 2 * TT)
                nc.scalar.copy(gT[:, 512 * th:512 * (th + 1)], PS[0:2 * RANK, n % 8, :]).then_inc(d, 1)
                n += 1
            for c2 in range(2):
                for ft in range(2):
                    for th in range(2):
                        d = drain("in", n)
                        nc.scalar.copy(u_pad[:, 2 * c2 + ft, PAD + 512 * th:PAD + 512 * (th + 1)],
                                       bank_groups(n)).then_inc(d, 1)
                        n += 1
                for ft in range(2):
                    for th in range(2):
                        d = drain("in", n)
                        c = 2 * c2 + ft
                        if th == 0 and c:
                            act.wait_ge(s_u, c)
                        nc.scalar.activation(sig[:, 512 * th:512 * (th + 1)], bank_groups(n),
                                             ACT.Sigmoid).then_inc(d, 1)
                        n += 1
            for dst, sc in ((qT, GDK ** -0.5), (kT, 1.0)):
                for ft in range(2):
                    for th in range(2):
                        d = drain("in", n)
                        if n == 18:
                            act.wait_ge(norms["x"]["scaled"], TT)
                        nc.scalar.mul(dst[:, ft, 512 * th:512 * (th + 1)], bank_groups(n), sc).then_inc(d, 1)
                        n += 1
            for dst in (v_tm, r_tm):
                for c2 in range(2):
                    for t in range(TT):
                        d = drain("in", n)
                        nc.scalar.copy(dst[:, t, 256 * c2:256 * (c2 + 1)], bank_groups(n, 256)).then_inc(d, 1)
                        n += 1

            for c in range(CT):
                act.wait_ge(s_lnv, 2 * (c + 1))
                if c == 0:
                    act.wait_ge(s_mm["in"], 58)
                nc.scalar.activation(o_gla[:, 2 * c:2 * c + 2, :], yT[:, c, :].rearrange("p (a b) -> p a b", a=2),
                                     ACT.Square).then_inc(s_lna, 1)
            act.wait_ge(s_lnv, 10)
            nc.scalar.activation(sig[:], sig[:], ACT.Sqrt).then_inc(s_lna, 1)
            for c in range(CT):
                act.wait_ge(s_lnv, 12 + c)
                act.wait_ge(s_lnp, 4)
                nc.scalar.activation(o_gla[:, 2 * c:2 * c + 2, :], yT[:, c, :].rearrange("p (a b) -> p a b", a=2),
                                     ACT.Identity, bias=PV[:, LB + c:LB + c + 1],
                                     scale=PV[:, LG_ + c:LG_ + c + 1]).then_inc(s_lna, 1)
            for c in range(CT):
                act.wait_ge(s_lna, 6 + c)
                nc.scalar.activation(yT[:, c, :], yT[:, c, :], ACT.Sigmoid, bias=PV[:, LB + c:LB + c + 1],
                                     scale=PV[:, LG_ + c:LG_ + c + 1]).then_inc(s_lna, 1)

            for p in range(2):
                for n in range(4):
                    d, th = n // 2, n % 2
                    act.wait_ge(s_z, 4 * p + n + 1)
                    nc.scalar.activation(KQ[:, d, 512 * th:512 * (th + 1)], PS[:, n, :], ACT.Abs,
                                         bias=PV[:, ZB + 2 * d + p:ZB + 2 * d + p + 1]).then_inc(s_zabs, 1)
                act.wait_ge(s_zabs, 4 * (p + 1))
                nc.scalar.activation(KQ[:], KQ[:], ACT.Exp, scale=-1.0).then_inc(s_zln, 1)
                act.wait_ge(s_zln, 2 * p + 1)
                nc.scalar.activation(KQ[:], KQ[:], ACT.Ln, bias=1.0).then_inc(s_zln, 1)
                drain_memory(range(8 * p, 8 * p + 4))
                act.wait_ge(s_tot, 2 * (p + 1))
                nc.scalar.activation(TTd[:, 1], TTd[:, 0], ACT.Exp, scale=1.0 / TAU).then_inc(s_dec, 1)
                for l in range(8):
                    act.wait_ge(s_sub, 8 * p + l + 1)
                    nc.scalar.activation(EX[:], EX[:], ACT.Exp, scale=1.0 / TAU).then_inc(s_ex, 1)
                    if l == 0:
                        drain_memory(range(8 * p + 4, 8 * p + 8))
                    if l == 7:
                        for b in range(4):
                            act.wait_ge(s_ket, 4 * p + b + 1)
                            nc.scalar.copy(KEt[:, b, :], PS[:, b, :]).then_inc(s_kev, 1)
                act.wait_ge(s_U, 14 * (p + 1))
                nc.scalar.activation(EX[:, 0, :], Bf[:], ACT.Exp, scale=1.0 / TAU)
                nc.scalar.activation(EX[:, 1, :], Rb[:], ACT.Exp, scale=1.0 / TAU).then_inc(s_ex, 1)
                for n in range(16):
                    act.wait_ge(s_op, 16 * p + n + 1)
                    w, hh = n // 2, n % 2
                    h = 2 * p + hh
                    nc.scalar.copy(o_gla[:, w, GDV * h:GDV * (h + 1)], PS[:, n % 4, 0:P]).then_inc(s_oe, 1)
            act.wait_ge(s_ov, 3)
            nc.scalar.activation(st8[:, 2, :], st8[:, 1, :], ACT.Sqrt).then_inc(s_oa, 1)
            nc.scalar.activation(SR[:], r_tm[:], ACT.Sigmoid).then_inc(s_oa, 1)
            for c in range(CT):
                for b in range(2):
                    n = 2 * c + b
                    act.wait_ge(s_at, n + 1)
                    nc.scalar.copy(aT[:, c, 512 * b:512 * (b + 1)], PS[:, n, :]).then_inc(s_ae, 1)
            norm_stats("y", xres, TT)
            for n in range(16):
                d = drain("q", n)
                nc.scalar.copy(qxT[:, n // 2, 512 * (n % 2):512 * (n % 2 + 1)], bank_groups(n)).then_inc(d, 1)
            def xprob_drain(h, t):
                i = TT * h + t
                act.wait_ge(s_pt, i + 1)
                nc.scalar.copy(pT[:, h % 2, :, P * t:P * (t + 1)],
                               PS[:, 2 + i % 2, 0:256].rearrange("p (m c) -> p m c", m=MT)).then_inc(s_pc, 1)

            for h in range(XH):
                for t in range(TT):
                    n = TT * h + t
                    act.wait_ge(s_sv, 4 * n + 2)
                    if n >= 2:
                        act.wait_ge(s_pt, n - 1)
                    nc.scalar.activation(pr[:, n % 2, :], PS[:, n % 2, 0:256], ACT.Exp, bias=smx[:, n % 4, 1:2],
                                         scale=XDH ** -0.5, accum_out=smx[:, n % 4, 2:3]).then_inc(s_pe, 1)
                    if t >= 1:
                        xprob_drain(h, t - 1)
                xprob_drain(h, TT - 1)
                for b in range(4):
                    m = 4 * h + b
                    act.wait_ge(s_av, m + 1)
                    nc.scalar.copy(oxT[:, 2 * h + b // 2, 512 * (b % 2):512 * (b % 2 + 1)],
                                   PS[:, 4 + b, :]).then_inc(s_ax, 1)
            act.wait_ge(s_mm["o"], 1)
            act.dma_start(gfb[:], A["norm_ffn_g"][0].partition_broadcast(P)).then_inc(s_rpar, 16)
            act.dma_start(rw[:], A["router_w"][0].rearrange("(k p) e -> p k e", p=P)).then_inc(s_rpar, 16)
            act.dma_start(rbb[:], A["router_b"][0].partition_broadcast(P)).then_inc(s_rpar, 16)
            act.dma_start(bdn[:], A["exp_b_down"][0]).then_inc(s_rpar, 16)
            for i in range(3):
                act.dma_start(bstage[E * i:E * (i + 1), :], A["exp_b_up"][0]).then_inc(s_rpar, 16)
            norm_stats("z", xres, TT)
            for t in range(TT):
                for b in range(2):
                    act.wait_ge(norms["z"]["turned"], 2 * t + b + 1)
                    if t >= 2:
                        act.wait_ge(s_lgp, t - 1)
                    nc.scalar.copy(h3T[:, t % 2, 4 * b:4 * b + 4, :].rearrange("p k c -> p (k c)"),
                                   PS[:, 2 * (t % 2) + b, :]).then_inc(s_h3e, 1)
            act.wait_ge(s_rt, 2)
            nc.scalar.activation(Gt[:], Gt[:], ACT.Exp).then_inc(s_gx, 1)
            for b in range(2):
                act.wait_ge(s_gdt, b + 1)
                nc.scalar.copy(GDT[:, 512 * b:512 * (b + 1)], PS[0:E, b, :]).then_inc(s_gde, 1)

            def split_hi(t, c, first=False):
                wait_raw(act, t, c)
                if not first:
                    wait_multiplied(act, t, c - NSPL)
                nc.scalar.copy(whi[:, chunk_slot(c, NSPL), :], raw[:, chunk_slot(c, NRAW), :]).then_inc(s_whi, 1)

            def two_blocks(t):
                return act.value_load(VT[0:1, 2, bass.ds(t, 1)], min_val=0, max_val=1)

            def turned_hi(turned, t, hi, blocks, done):
                act.wait_ge(turned, t + 1)
                for b in range(blocks):
                    for i in range(2):
                        ins = nc.scalar.copy(hi[:, b, 4 * i:4 * i + 4, :].rearrange("p k c -> p (k c)"),
                                             PS[:, 4 + 2 * b + i, :])
                ins.then_inc(done, 1)

            def tokens_hi(t):
                both = two_blocks(t)
                with act.If(both >= 1):
                    turned_hi(s_xt, t, xhi, 2, s_xhi)
                with act.Else():
                    turned_hi(s_xt, t, xhi, 1, s_xhi)

            def hidden_hi(t, both):
                with act.If(both >= 1):
                    turned_hi(s_ht, t, hhi, 2, s_hhi)
                with act.Else():
                    turned_hi(s_ht, t, hhi, 1, s_hhi)

            def expert_sigmoid(t, i, both):
                def one(blocks):
                    act.wait_ge(s_g, 2 * t + i + 1)
                    nc.scalar.activation(sgm[:, 0:blocks, :], glu[:, 0:blocks, :], ACT.Sigmoid, scale=ALPHA
                                         ).then_inc(s_sg, 1)
                with act.If(both >= 1):
                    one(2)
                with act.Else():
                    one(1)

            def drain_rows(t, i, both):
                def one(blocks):
                    wait_multiplied(act, t, 9 + 2 * i)
                    act.wait_ge(s_yst, 16 * t - 15)
                    for b in range(blocks):
                        ins = nc.scalar.copy(yb[:, b, 512 * i:512 * (i + 1)], PS[:, 2 * i + b, :])
                    ins.then_inc(s_yev, 1)
                with act.If(both >= 1):
                    one(2)
                with act.Else():
                    one(1)

            def store_rows(t):
                b0 = act.value_load(VT[0:1, 1, bass.ds(t, 1)], min_val=0, max_val=NBLK - 1)
                act.dma_start(ys_dram[bass.ds(b0 * P, 2 * P), :].rearrange("(b p) d -> p b d", p=P), yb[:]
                              ).then_inc(s_yst, 16)

            act.wait_ge(s_tab, 1)
            used_ = act.value_load(usedb[0:1, 0:1], min_val=1, max_val=NVIS)
            nc.scalar.copy(smx[:, 0, 0:1], st8[:, 0, 0:1]).then_inc(s_yev, 1)
            nc.scalar.copy(smx[:, 0, 1:2], st8[:, 0, 0:1]).then_inc(s_yev, 1)
            tokens_hi(0)
            both0 = two_blocks(0)
            for c in range(4, 9):
                split_hi(0, c, first=c < 4 + NSPL)
            expert_sigmoid(0, 0, both0)
            for c in (9, 10, 11):
                split_hi(0, c)
            split_hi(1, 0)
            expert_sigmoid(0, 1, both0)
            split_hi(1, 1)
            split_hi(1, 2)
            tokens_hi(1)
            hidden_hi(0, both0)
            with act.Fori(1, NVIS + 1) as t:
                with act.If(t <= used_):
                    both, both_last = two_blocks(t), two_blocks(t - 1)
                    split_hi(t, 3)
                    split_hi(t, 4)
                    split_hi(t, 5)
                    expert_sigmoid(t, 0, both)
                    split_hi(t, 6)
                    split_hi(t, 7)
                    split_hi(t, 8)
                    split_hi(t, 9)
                    expert_sigmoid(t, 1, both)
                    split_hi(t, 10)
                    split_hi(t, 11)
                    tokens_hi(t + 1)
                    split_hi(t + 1, 0)
                    drain_rows(t, 0, both_last)
                    split_hi(t + 1, 1)
                    drain_rows(t, 1, both_last)
                    hidden_hi(t, both)
                    split_hi(t + 1, 2)
                    act.wait_ge(s_yev, 2 * t + 2)
                    store_rows(t - 1)
            for t in range(TT):
                act.wait_ge(s_ac, TOPK * (t + 1))
                nc.scalar.activation(sqs[:], xres[:, t, :], ACT.Square, accum_out=st8[:, 0, t:t + 1]
                                     ).then_inc(s_fa, 1)
                act.wait_ge(s_fv, 2 * t + 1)
                nc.scalar.activation(st8[:, 2, t:t + 1], st8[:, 1, t:t + 1], ACT.Sqrt).then_inc(s_fa, 1)

        @block.vector
        def _(dve):
            dve.wait_ge(s_const, 5)
            nc.vector.tensor_tensor(xor[:], xor[:], mtmp[:].bitcast(I32), ALU.bitwise_xor).then_inc(s_mask, 1)
            for l, s in enumerate(LEVELS):
                dve.wait_ge(s_mask, 2 * l + 1)
                nc.vector.tensor_scalar(mtmp[:], xor[:], float(2 * s), None, ALU.is_lt).then_inc(s_mask, 1)
                dve.wait_ge(s_mask, 2 * l + 2)
                nc.vector.scalar_tensor_tensor(out=masks[:, l, :], in0=xor[:], scalar=float(s), in1=mtmp[:],
                                               op0=ALU.is_ge, op1=ALU.mult).then_inc(s_mask, 1)
            dve.wait_ge(s_pvt, 2)
            nc.vector.tensor_copy(PV[:, 0:NPV], PS[:, 6, 0:NPV]).then_inc(s_pvc, 1)
            nc.vector.tensor_copy(CWT[:], PS[:, 7, 0:TAPS * CT]).then_inc(s_pvc, 1)
            dve.wait_ge(s_pvc, 2)

            def norm_scale(n, src, tiles, g, dst):
                N = norms[n]
                dve.wait_ge(N["stats_by_scalar"], tiles)
                nc.vector.tensor_scalar(st8[:, 1, 0:tiles], st8[:, 0, 0:tiles], 1.0 / D, RMS_EPS,
                                        ALU.mult, ALU.add).then_inc(N["stats_by_vector"], 1)
                dve.wait_ge(N["stats_by_scalar"], tiles + 1)
                nc.vector.reciprocal(st8[:, 3, 0:tiles], st8[:, 2, 0:tiles]).then_inc(N["stats_by_vector"], 1)
                dve.wait_ge(N["stats_by_vector"], 2)

                def evac(t):
                    for b in range(2):
                        dve.wait_ge(N["turned"], 2 * t + b + 1)
                        bank = 2 * (t % 4) + b
                        nc.vector.tensor_tensor(
                            dst[:, 4 * b:4 * b + 4, P * t:P * (t + 1)],
                            PS[:, bank, :].rearrange("p (k c) -> p k c", k=4),
                            PV[:, g + 4 * b:g + 4 * b + 4].unsqueeze(2).broadcast_to([P, 4, P]),
                            ALU.mult).then_inc(N["drained"], 1)

                for t in range(tiles):
                    if t >= 2:
                        dve.wait_ge(N["turned"], 2 * (t - 1))
                    nc.vector.tensor_scalar(XN[:, t % 2, :], src[:, t, :], st8[:, 3, t:t + 1], None,
                                            ALU.mult).then_inc(N["scaled"], 1)
                    if t >= 1:
                        evac(t - 1)
                evac(tiles - 1)

            norm_scale("m", mem_tm, MT, GM, mT)
            norm_scale("x", xres, TT, GX, hT)

            dve.wait_ge(s_pad, 2 * CT)
            cv = 0
            for c2 in range(2):
                dve.wait_ge(s_u, 2 * c2 + 2)
                for j in range(TAPS):
                    for c in (2 * c2, 2 * c2 + 1):
                        uc = u_pad[:, c, j:j + S]
                        w = CWT[:, j * CT + c:j * CT + c + 1]
                        if j == 0:
                            if c == 0:
                                dve.wait_ge(norms["m"]["scaled"], MT)
                            ins = nc.vector.tensor_scalar(yT[:, c, :], uc, w, PV[:, CB + c:CB + c + 1],
                                                          ALU.mult, ALU.add)
                        else:
                            dve.wait_ge(s_cv, cv - 1)
                            ins = nc.vector.scalar_tensor_tensor(out=yT[:, c, :], in0=uc, scalar=w,
                                                                 in1=yT[:, c, :], op0=ALU.mult, op1=ALU.add)
                        ins.then_inc(s_cv, 1)
                        cv += 1
            for th in range(2):
                dve.wait_ge(s_lnp, th + 1)
            for c in range(CT):
                for th in range(2):
                    yh = yT[:, c, 512 * th:512 * (th + 1)]
                    nc.vector.scalar_tensor_tensor(out=yh, in0=PS[:, th, :], scalar=-1.0 / CW_, in1=yh,
                                                   op0=ALU.mult, op1=ALU.add).then_inc(s_lnv, 1)
            for th in range(2):
                dve.wait_ge(s_lnp, th + 3)
                nc.vector.tensor_scalar(sig[:, 512 * th:512 * (th + 1)], PS[:, 2 + th, :], 1.0 / CW_, LN_EPS,
                                        ALU.mult, ALU.add).then_inc(s_lnv, 1)
            dve.wait_ge(s_lna, 5)
            nc.vector.reciprocal(sig[:], sig[:]).then_inc(s_lnv, 1)
            dve.wait_ge(s_lnv, 11)
            for c in range(CT):
                nc.vector.tensor_tensor(yT[:, c, :], yT[:, c, :], sig[:], ALU.mult).then_inc(s_lnv, 1)
            for c in range(CT):
                dve.wait_ge(s_lna, 10 + c)
                nc.vector.tensor_tensor(yT[:, c, :].rearrange("p (a b) -> p a b", a=2),
                                        yT[:, c, :].rearrange("p (a b) -> p a b", a=2),
                                        o_gla[:, 2 * c:2 * c + 2, :], ALU.mult).then_inc(s_lnv, 1)

            dve.wait_ge(s_par, 12 * 16)
            for p in range(2):
                if p:
                    dve.wait_ge(s_kq, 9 * p)
                for n in range(4):
                    d, th = n // 2, n % 2
                    dve.wait_ge(s_z, 4 * p + n + 1)
                    dve.wait_ge(s_zabs, 4 * p + n + 1)
                    nc.vector.tensor_scalar(EX[:, d, 512 * th:512 * (th + 1)], PS[:, n, :],
                                            PV[:, ZB + 2 * d + p:ZB + 2 * d + p + 1], 0.0,
                                            ALU.add, ALU.min).then_inc(s_zmin, 1)
                dve.wait_ge(s_zmin, 4 * (p + 1))
                dve.wait_ge(s_zln, 2 * (p + 1))
                nc.vector.tensor_tensor(EX[:], EX[:], KQ[:], ALU.subtract).then_inc(s_la, 1)
                dve.wait_ge(s_la, p + 1)
                for d, dst in ((0, Bf), (1, Rb)):
                    for w in range(TT):
                        nc.vector.tensor_tensor_scan(out=dst[:, P * w:P * (w + 1)], data0=ones[:],
                                                     data1=EX[:, d, P * w:P * (w + 1)], initial=0.0,
                                                     op0=ALU.mult, op1=ALU.add).then_inc(s_scan, 1)
                dve.wait_ge(s_scan, 16 * (p + 1))
                wins = lambda ap: ap.rearrange("p (w c) -> p w c", w=TT)
                ends = lambda ap: wins(ap)[:, :, P - 1:P].rearrange("p w c -> p (w c)")
                if p:
                    dve.wait_ge(s_st, 14 * p)
                nc.vector.tensor_copy(TTd[:, 0, 0, :], ends(Bf[:])).then_inc(s_tot, 1)
                nc.vector.tensor_copy(TTd[:, 0, 1, :], ends(Rb[:])).then_inc(s_tot, 1)
                dve.wait_ge(s_tot, 2 * (p + 1))
                nc.vector.tensor_tensor(Rb[:], EX[:, 1, :], Rb[:], ALU.subtract).then_inc(s_rb, 1)
                dve.wait_ge(s_rb, 2 * p + 1)
                tot = lambda d: TTd[:, 0, d, :].unsqueeze(2).broadcast_to([P, TT, P])
                nc.vector.tensor_tensor(wins(Rb[:]), wins(Rb[:]), tot(1), ALU.add).then_inc(s_rb, 1)
                dve.wait_ge(s_rb, 2 * p + 2)

                def exponents(l):
                    s = LEVELS[l]
                    v3 = lambda ap: ap.rearrange("p (g h c) -> p g h c", h=2, c=s)
                    bref = v3(Bf[:])[:, :, 0, s - 1:s].broadcast_to([P, S // (2 * s), s])
                    rref = v3(Rb[:])[:, :, 1, 0:1].broadcast_to([P, S // (2 * s), s])
                    B_, R_, K_, Q_ = v3(Bf[:]), v3(Rb[:]), v3(EX[:, 0, :]), v3(EX[:, 1, :])
                    nc.vector.tensor_tensor(K_[:, :, 0, :], bref, B_[:, :, 0, :], ALU.subtract)
                    nc.vector.tensor_tensor(K_[:, :, 1, :], rref, R_[:, :, 1, :], ALU.subtract)
                    nc.vector.tensor_tensor(Q_[:, :, 0, :], R_[:, :, 0, :], rref, ALU.subtract)
                    nc.vector.tensor_tensor(Q_[:, :, 1, :], B_[:, :, 1, :], bref, ALU.subtract).then_inc(s_sub, 1)

                def select(l):
                    for b in range(4):
                        hh, half = b // 2, b % 2
                        L = 8 * p + l
                        dve.wait_ge(s_gram, 4 * L + b + 1)
                        if l and b == 0:
                            dve.wait_ge(s_sel, 4 * L)
                        scores = Ssc[:, hh, 4 * half:4 * half + 4, :]
                        products = PS[:, 4 * (L % 2) + b, :].rearrange("p (w c) -> p w c", w=4)
                        if l == 0:
                            ins = nc.vector.tensor_copy(scores, products)
                        else:
                            ins = nc.vector.copy_predicated(
                                scores, masks[:, l - 1:l, :].broadcast_to([P, 4, P]), products)
                        ins.then_inc(s_sel, 1)

                exponents(0)
                for l in range(7):
                    dve.wait_ge(s_ex, 9 * p + l + 1)
                    if l >= 2:
                        dve.wait_ge(s_gram, 32 * p + 4 * l)
                    dst = (KQ, KQ2)[l % 2]
                    nc.vector.tensor_tensor(dst[:, 0, :], EX[:, 0, :], kT[:, p, :], ALU.mult)
                    nc.vector.tensor_tensor(dst[:, 1, :], EX[:, 1, :], qT[:, p, :], ALU.mult).then_inc(s_kq, 1)
                    dve.wait_ge(s_kq, 9 * p + l + 1)
                    if l < 6:
                        exponents(l + 1)
                    else:
                        nc.vector.tensor_tensor(wins(EX[:, 0, :]), tot(0), wins(Bf[:]), ALU.subtract)
                        nc.vector.tensor_tensor(wins(EX[:, 1, :]), tot(1), wins(Rb[:]),
                                                ALU.subtract).then_inc(s_sub, 1)
                    select(l)
                dve.wait_ge(s_ex, 9 * p + 8)
                nc.vector.tensor_tensor(KQ2[:, 0, :], EX[:, 0, :], kT[:, p, :], ALU.mult)
                nc.vector.tensor_tensor(KQ2[:, 1, :], EX[:, 1, :], kT[:, p, :], ALU.mult).then_inc(s_kq, 1)
                select(7)
                nc.vector.memset(ST[:, 0, 0, :], 0.0).then_inc(s_st0, 1)
                nc.vector.memset(ST[:, 1, TT - 1, :], 0.0).then_inc(s_st0, 1)
                dve.wait_ge(s_st0, 2 * (p + 1))
                dve.wait_ge(s_dec, p + 1)
                for n in range(14):
                    d = n % 2
                    w = n // 2 if d == 0 else TT - 1 - n // 2
                    to = w + 1 if d == 0 else w - 1
                    dve.wait_ge(s_U, 14 * p + n + 1)
                    if n >= 2:
                        dve.wait_ge(s_st, 14 * p + n - 1)
                    for hh in range(2):
                        a, b = GDK * hh, GDK * (hh + 1)
                        ins = nc.vector.scalar_tensor_tensor(
                            out=ST[a:b, d, to, :], in0=ST[a:b, d, w, :], scalar=TTd[a:b, 1, d, w:w + 1],
                            in1=PS[a:b, 4 + n % 4, P * hh:P * (hh + 1)], op0=ALU.mult, op1=ALU.add)
                    ins.then_inc(s_st, 1)
                dve.wait_ge(s_ex, 9 * p + 9)
                nc.vector.tensor_tensor(KQ[:, 0, :], EX[:, 0, :], qT[:, p, :], ALU.mult)
                nc.vector.tensor_tensor(KQ[:, 1, :], EX[:, 1, :], qT[:, p, :], ALU.mult).then_inc(s_kq, 1)
            og = o_gla[:].rearrange("p w (h c) -> p (w h) c", h=GH)
            rg = r_tm[:].rearrange("p w (h c) -> p (w h) c", h=GH)
            sg = SR[:].rearrange("p w (h c) -> p (w h) c", h=GH)
            dve.wait_ge(s_oe, 32)
            dve.wait_ge(s_op, 32)
            nc.vector.tensor_tensor(sg, og, og, ALU.mult).then_inc(s_ov, 1)
            dve.wait_ge(s_ov, 1)
            nc.vector.tensor_reduce(st8[:, 0, :], sg, X, ALU.add).then_inc(s_ov, 1)
            dve.wait_ge(s_ov, 2)
            nc.vector.tensor_scalar(st8[:, 1, :], st8[:, 0, :], 1.0 / GDV, RMS_EPS, ALU.mult, ALU.add
                                    ).then_inc(s_ov, 1)
            dve.wait_ge(s_oa, 1)
            nc.vector.reciprocal(st8[:, 3, :], st8[:, 2, :]).then_inc(s_ov, 1)
            dve.wait_ge(s_ov, 4)
            nc.vector.tensor_tensor(og, og, st8[:, 3, :].unsqueeze(2).broadcast_to([P, 32, P]), ALU.mult
                                    ).then_inc(s_ov, 1)
            dve.wait_ge(s_ov, 5)
            nc.vector.tensor_tensor(og, og, ngb[:].unsqueeze(1).broadcast_to([P, 32, P]), ALU.mult
                                    ).then_inc(s_ov, 1)
            dve.wait_ge(s_oa, 2)
            nc.vector.tensor_tensor(rg, rg, sg, ALU.mult).then_inc(s_ov, 1)
            dve.wait_ge(s_ov, 7)
            nc.vector.tensor_tensor(og, og, rg, ALU.mult).then_inc(s_ov, 1)

            def add_residual(seg):
                for c in range(4):
                    for t in range(TT):
                        n = TT * c + t
                        dve.wait_ge(s_mm[seg], n + 1)
                        xs = xres[:, t, 256 * c:256 * (c + 1)]
                        nc.vector.tensor_tensor(xs, xs, bank_groups(n, 256), ALU.add).then_inc(s_dr[seg], 1)

            dve.wait_ge(s_xre, 32)
            add_residual("out")
            norm_scale("y", xres, TT, GA, hT)
            for h in range(XH):
                for t in range(TT):
                    n = TT * h + t
                    dve.wait_ge(s_sc, n + 1)
                    if n >= 4:
                        dve.wait_ge(s_sv, 4 * (n - 3))
                    m = smx[:, n % 4, :]
                    nc.vector.reduce_max(m[:, 0:1], PS[:, n % 2, 0:256], X).then_inc(s_sv, 1)
                    dve.wait_ge(s_sv, 4 * n + 1)
                    nc.vector.tensor_scalar(m[:, 1:2], m[:, 0:1], -(XDH ** -0.5), None, ALU.mult).then_inc(s_sv, 1)
                    dve.wait_ge(s_pe, n + 1)
                    nc.vector.reciprocal(m[:, 3:4], m[:, 2:3]).then_inc(s_sv, 1)
                    dve.wait_ge(s_sv, 4 * n + 3)
                    nc.vector.tensor_scalar(pr[:, n % 2, :], pr[:, n % 2, :], m[:, 3:4], None,
                                            ALU.mult).then_inc(s_sv, 1)
            add_residual("o")

            N = norms["z"]
            dve.wait_ge(N["stats_by_scalar"], TT)
            nc.vector.tensor_scalar(st8[:, 1, 0:TT], st8[:, 0, 0:TT], 1.0 / D, RMS_EPS, ALU.mult, ALU.add
                                    ).then_inc(N["stats_by_vector"], 1)
            dve.wait_ge(N["stats_by_scalar"], TT + 1)
            nc.vector.reciprocal(st8[:, 3, 0:TT], st8[:, 2, 0:TT]).then_inc(N["stats_by_vector"], 1)
            dve.wait_ge(N["stats_by_vector"], 2)
            dve.wait_ge(s_rpar, 7 * 16)

            def logits(t):
                dve.wait_ge(s_lgp, t + 1)
                nc.vector.tensor_tensor(LG[:, t, :], PS[:, 4 + t % 2, 0:E], rbb[:], ALU.add).then_inc(s_lg, 1)
                dve.wait_ge(s_lg, t + 1)
                nc.vector.max(MX[:, t, :], LG[:, t, :]).then_inc(s_top, 1)
                dve.wait_ge(s_top, 2 * t + 1)
                nc.vector.max_index(IX[:, t, :], MX[:, t, :], LG[:, t, :]).then_inc(s_top, 1)

            for t in range(TT):
                if t == 0:
                    dve.wait_ge(s_mm["o"], 32)
                nc.vector.scalar_tensor_tensor(out=h3[:, t, :], in0=xres[:, t, :], scalar=st8[:, 3, t:t + 1],
                                               in1=gfb[:], op0=ALU.mult, op1=ALU.mult).then_inc(N["scaled"], 1)
                if t >= 2:
                    logits(t - 2)
            logits(TT - 2)
            logits(TT - 1)
            dve.wait_ge(s_top, 2 * TT)

            rt = 0

            def step(ins):
                nonlocal rt
                rt += 1
                ins.then_inc(s_rt, 1)
                dve.wait_ge(s_rt, rt)

            step(nc.vector.tensor_copy(IXf[:], IX[:]))
            step(nc.vector.tensor_tensor(Gt[:], MX[:, :, 0:TOPK], MX[:, :, 0:1].broadcast_to([P, TT, TOPK]),
                                         ALU.subtract))
            for k in range(TOPK):
                step(nc.vector.tensor_tensor(OH[:, :, k, :], iot[:, 0:E].unsqueeze(1).broadcast_to([P, TT, E]),
                                             IXf[:, :, k:k + 1].broadcast_to([P, TT, E]), ALU.is_equal))
            step(nc.vector.tensor_tensor(M[:], OH[:, :, 0, :], OH[:, :, 1, :], ALU.add))
            step(nc.vector.tensor_tensor(M[:], M[:], OH[:, :, 2, :], ALU.add))
            step(nc.vector.tensor_tensor(Mb[:], M[:], OH[:, :, 3, :], ALU.add))
            assert rt == RT_M
            dve.wait_ge(s_gx, 1)
            step(nc.vector.tensor_reduce(gsum[:, 0, :], Gt[:], X, ALU.add))
            step(nc.vector.reciprocal(gsum[:, 1, :], gsum[:, 0, :]))
            step(nc.vector.tensor_tensor(Gt[:], Gt[:], gsum[:, 1, :].unsqueeze(2).broadcast_to([P, TT, TOPK]),
                                         ALU.mult))
            tA = tmpA[:, 0:TT * TOPK * E].rearrange("p (t k e) -> p t k e", t=TT, k=TOPK)
            for k in range(TOPK):
                step(nc.vector.tensor_tensor(tA[:, :, k, :], OH[:, :, k, :],
                                             Gt[:, :, k:k + 1].broadcast_to([P, TT, E]), ALU.mult))
            step(nc.vector.tensor_reduce(GD[:], tA.rearrange("p t k e -> p t e k"), X, ALU.add))
            assert rt == RT_GD
            dve.wait_ge(s_rk, 2)
            nblk, pend, pstb, pst, nvis, vend, vst, first = (ex1[:, i, :] for i in range(8))
            step(nc.vector.tensor_scalar(exi[:, 0, :], PS[:, 7, 0:E], float(P - 1), None, ALU.add))
            step(nc.vector.tensor_scalar(exi[:, 1, :], exi[:, 0, :], 7, None, ALU.arith_shift_right))
            step(nc.vector.tensor_copy(nblk, exi[:, 1, :]))
            step(nc.vector.tensor_tensor_scan(out=pend, data0=ones[:, 0:E], data1=nblk, initial=0.0,
                                              op0=ALU.mult, op1=ALU.add))
            step(nc.vector.tensor_tensor(pstb, pend, nblk, ALU.subtract))
            step(nc.vector.tensor_scalar(pst, pstb, float(P), None, ALU.mult))
            step(nc.vector.tensor_scalar(exi[:, 0, :], exi[:, 1, :], 1.0, None, ALU.add))
            step(nc.vector.tensor_scalar(exi[:, 1, :], exi[:, 0, :], 1, None, ALU.arith_shift_right))
            step(nc.vector.tensor_copy(nvis, exi[:, 1, :]))
            step(nc.vector.tensor_tensor_scan(out=vend, data0=ones[:, 0:E], data1=nvis, initial=0.0,
                                              op0=ALU.mult, op1=ALU.add))
            step(nc.vector.tensor_tensor(vst, vend, nvis, ALU.subtract))
            step(nc.vector.scalar_tensor_tensor(out=first, in0=vst, scalar=-2.0, in1=pstb, op0=ALU.mult,
                                                op1=ALU.add))
            step(nc.vector.tensor_tensor(slot0[:], PS[:, 6, 0:TT * E].rearrange("p (t e) -> p t e", e=E),
                                         pst.unsqueeze(1).broadcast_to([P, TT, E]), ALU.add))
            for k in range(TOPK):
                step(nc.vector.tensor_tensor(tA[:, :, k, :], OH[:, :, k, :], slot0[:], ALU.mult))
            step(nc.vector.tensor_reduce(df[:, 0, :], tA.rearrange("p t k e -> p (t k) e"), X, ALU.add))
            step(nc.vector.tensor_copy(rowof[:], df[:, 0, :]))
            step(nc.vector.tensor_copy(di[:, 0, :], df[:, 0, :]))
            step(nc.vector.tensor_scalar(di[:, 1, :], di[:, 0, :], 7, None, ALU.arith_shift_right))
            step(nc.vector.tensor_scalar(di[:, 2, :], di[:, 0, :], P - 1, None, ALU.bitwise_and))
            step(nc.vector.tensor_copy(df[:, 1:3, :], di[:, 1:3, :]))
            step(nc.vector.tensor_tensor(blkhot[:], iot[:, 0:NB].unsqueeze(1).broadcast_to([P, TT * TOPK, NB]),
                                         df[:, 1, :].unsqueeze(2).broadcast_to([P, TT * TOPK, NB]), ALU.is_equal))
            nc.vector.tensor_tensor(blkhot[:].rearrange("p (t k) b -> p t (k b)", t=TT),
                                    blkhot[:].rearrange("p (t k) b -> p t (k b)", t=TT),
                                    pid[:].unsqueeze(2).broadcast_to([P, TT, TOPK * NB]), ALU.mult
                                    ).then_inc(s_oh, 1)
            for t in range(TT):
                ks = slice(TOPK * t, TOPK * (t + 1))
                if t >= 2:
                    dve.wait_ge(s_tm, t - 1)
                nc.vector.tensor_tensor(rowhot[:, t % 2], iot[:].unsqueeze(1).broadcast_to([P, TOPK, P]),
                                        df[:, 2, ks].unsqueeze(2).broadcast_to([P, TOPK, P]),
                                        ALU.is_equal).then_inc(s_oh, 1)
            tB = tmpA[:, 0:NV * E].rearrange("p (v e) -> p v e", e=E)
            visit = iot[:, 0:NV]
            over_v = lambda ap: ap.unsqueeze(1).broadcast_to([P, NV, E])
            over_e = lambda ap: ap.unsqueeze(2).broadcast_to([P, NV, E])
            ve, vb, vp, v2 = (vt[:, i, :] for i in range(4))
            step(nc.vector.tensor_tensor(tB, over_v(vend), over_e(visit), ALU.is_le))
            step(nc.vector.tensor_reduce(ve, tB, X, ALU.add))
            step(nc.vector.tensor_scalar(ve, ve, float(E - 1), None, ALU.min))
            tC = tmpC[:, 0:NV * E].rearrange("p (v e) -> p v e", e=E)
            step(nc.vector.tensor_tensor(tC, over_v(iot[:, 0:E]), over_e(ve), ALU.is_equal))
            for src, dst_ in ((first, vb), (pend, vp)):
                step(nc.vector.tensor_tensor(tB, tC, over_v(src), ALU.mult))
                step(nc.vector.tensor_reduce(dst_, tB, X, ALU.add))
            step(nc.vector.scalar_tensor_tensor(out=vb, in0=visit, scalar=2.0, in1=vb, op0=ALU.mult, op1=ALU.add))
            step(nc.vector.scalar_tensor_tensor(out=v2, in0=vb, scalar=1.0, in1=vp, op0=ALU.add, op1=ALU.is_lt))
            step(nc.vector.tensor_scalar(vb, vb, float(NBLK - 1), None, ALU.min))
            step(nc.vector.tensor_copy(VT[:, 0:2, :], vt[:, 0:2, :]))
            step(nc.vector.tensor_copy(VT[:, 2, :], v2))
            step(nc.vector.tensor_copy(usedb[:], vend[:, E - 1:E]))
            dve.wait_ge(s_rmi, 3)
            step(nc.vector.tensor_scalar(pmi[:, 0:1], pmi[:, 0:1], E - 1, None, ALU.bitwise_and))
            step(nc.vector.tensor_copy(pmod[:, 0:1], pmi[:, 0:1]))
            step(nc.vector.tensor_scalar(EB[:], ve, pmod[:, 0:1], None, ALU.is_equal))
            dve.wait_ge(s_tm, TT)
            step(nc.vector.tensor_copy(TM[:], PS[:, 4, 0:NB]))

            def bias_selector(t):
                nc.vector.tensor_scalar(SEL[:], ones[:], EB[:, bass.ds(t, 1)], None, ALU.mult).then_inc(s_bsel, 1)

            nc.vector.tensor_copy(pmod[:, 1:2], pmod[:, 0:1]).then_inc(s_tab, 1)
            for t in range(TT):
                for b in range(2):
                    n = 2 * t + b
                    dve.wait_ge(s_bd, n + 1)
                    xh = xres[:, t, 512 * b:512 * (b + 1)]
                    nc.vector.tensor_tensor(xh, xh, PS[:, n % 4, :], ALU.add).then_inc(s_bdr, 1)
            dve.wait_ge(s_bdr, 2 * TT)

            def lo_by_vector(t, c):
                dve.wait_ge(s_whi, 12 * t + c - 3)
                nc.vector.tensor_tensor(wlo[:, chunk_slot(c, NSPL), :], raw[:, chunk_slot(c, NRAW), :],
                                        whi[:, chunk_slot(c, NSPL), :].bitcast(F), ALU.subtract
                                        ).then_inc(s_wlv, 1)

            def two_blocks(t):
                return dve.value_load(VT[0:1, 2, bass.ds(t, 1)], min_val=0, max_val=1)

            def turned_lo(t, split, hi, lo, blocks, done):
                dve.wait_ge(split, t + 1)
                flat = lambda ap, b, i: ap[:, b, 4 * i:4 * i + 4, :].rearrange("p k c -> p (k c)")
                for b in range(blocks):
                    for i in range(2):
                        ins = nc.vector.tensor_tensor(flat(lo, b, i), PS[:, 4 + 2 * b + i, :],
                                                      flat(hi, b, i).bitcast(F), ALU.subtract)
                ins.then_inc(done, 1)

            def tokens_lo(t):
                both = two_blocks(t)
                with dve.If(both >= 1):
                    turned_lo(t, s_xhi, xhi, xlo, 2, s_xlo)
                with dve.Else():
                    turned_lo(t, s_xhi, xhi, xlo, 1, s_xlo)

            def hidden_lo(t, both):
                with dve.If(both >= 1):
                    turned_lo(t, s_hhi, hhi, hlo, 2, s_hlo)
                with dve.Else():
                    turned_lo(t, s_hhi, hhi, hlo, 1, s_hlo)

            def clamp_glu(t, c, i, both, first=False):
                def one(blocks):
                    wait_multiplied(dve, t, c)
                    if not first:
                        dve.wait_ge(s_hid, 4 * t + 2 * i)
                    for b in range(blocks):
                        ins = nc.vector.tensor_scalar(glu[:, b, :], PS[:, b, :], LIMIT, None, ALU.min)
                    ins.then_inc(s_g, 1)
                with dve.If(both >= 1):
                    one(2)
                with dve.Else():
                    one(1)

            def hidden(t, c, i, both):
                cols = slice(512 * i, 512 * (i + 1))

                def one(blocks):
                    wait_multiplied(dve, t, c)
                    if not (isinstance(t, int) and t == 0):
                        dve.wait_ge(s_ht, t)
                    for b in range(blocks):
                        ins = nc.vector.tensor_scalar(hid[:, b, cols], PS[:, 2 + b, :], LIMIT, -LIMIT,
                                                      ALU.min, ALU.max)
                    ins.then_inc(s_upr, 1)
                    dve.wait_ge(s_sg, 2 * t + i + 1)
                    nc.vector.tensor_tensor(glu[:, 0:blocks, :], glu[:, 0:blocks, :], sgm[:, 0:blocks, :],
                                            ALU.mult).then_inc(s_hid, 1)
                    dve.wait_ge(s_hid, 4 * t + 2 * i + 1)
                    dve.wait_ge(s_upr, 2 * t + i + 1)
                    nc.vector.scalar_tensor_tensor(out=hid[:, 0:blocks, cols], in0=hid[:, 0:blocks, cols],
                                                   scalar=1.0, in1=glu[:, 0:blocks, :], op0=ALU.add,
                                                   op1=ALU.mult).then_inc(s_hid, 1)
                with dve.If(both >= 1):
                    one(2)
                with dve.Else():
                    one(1)

            used_ = dve.value_load(usedb[0:1, 0:1], min_val=1, max_val=NVIS)
            bias_selector(0)
            nc.vector.memset(glu[:, 1, 0:1], 0.0)
            tokens_lo(0)
            both0 = two_blocks(0)
            for c in (4, 5, 7, 8):
                lo_by_vector(0, c)
            clamp_glu(0, 5, 0, both0, first=True)
            lo_by_vector(0, 10)
            hidden(0, 7, 0, both0)
            lo_by_vector(0, 11)
            clamp_glu(0, 9, 1, both0)
            lo_by_vector(1, 1)
            lo_by_vector(1, 2)
            wait_multiplied(dve, 0, 11)
            bias_selector(1)
            hidden(0, 11, 1, both0)
            tokens_lo(1)
            hidden_lo(0, both0)
            with dve.Fori(1, NVIS + 1) as t:
                with dve.If(t <= used_):
                    both = two_blocks(t)
                    lo_by_vector(t, 4)
                    clamp_glu(t, 1, 0, both)
                    lo_by_vector(t, 5)
                    hidden(t, 3, 0, both)
                    lo_by_vector(t, 7)
                    lo_by_vector(t, 8)
                    clamp_glu(t, 5, 1, both)
                    lo_by_vector(t, 10)
                    wait_multiplied(dve, t, 7)
                    bias_selector(t + 1)
                    hidden(t, 7, 1, both)
                    lo_by_vector(t, 11)
                    tokens_lo(t + 1)
                    lo_by_vector(t + 1, 1)
                    hidden_lo(t, both)
                    lo_by_vector(t + 1, 2)
            def final(t):
                dve.wait_ge(s_fv, 2 * t + 2)
                if t >= 2:
                    dve.wait_ge(s_out[t % 2], 16 * (t // 2))
                nc.vector.scalar_tensor_tensor(out=fo[:, t % 2, :], in0=xres[:, t, :], scalar=st8[:, 3, t:t + 1],
                                               in1=fgb[:], op0=ALU.mult, op1=ALU.mult).then_inc(s_fo, 1)

            def root(t):
                dve.wait_ge(s_fa, 2 * t + 1)
                nc.vector.tensor_scalar(st8[:, 1, t:t + 1], st8[:, 0, t:t + 1], 1.0 / D, RMS_EPS, ALU.mult,
                                        ALU.add).then_inc(s_fv, 1)
                dve.wait_ge(s_fa, 2 * t + 2)
                nc.vector.reciprocal(st8[:, 3, t:t + 1], st8[:, 2, t:t + 1]).then_inc(s_fv, 1)

            dve.wait_ge(s_ffg, 16)
            for t in range(TT):
                for k in range(TOPK):
                    i = TOPK * t + k
                    dve.wait_ge(s_yg[i % 8], 16 * (i // 8 + 1))
                    if k:
                        dve.wait_ge(s_ac, i)
                    nc.vector.scalar_tensor_tensor(out=xres[:, t, :], in0=yg[:, i % 8, :], scalar=Gt[:, t, k:k + 1],
                                                   in1=xres[:, t, :], op0=ALU.mult, op1=ALU.add).then_inc(s_ac, 1)
                if t:
                    root(t - 1)
                    final(t - 1)
            root(TT - 1)
            final(TT - 1)

        @block.tensor
        def _(pe):
            pe.wait_ge(s_const, 2)
            pe.wait_ge(s_par, 12 * 16)
            pe.transpose(PS[:, 6, 0:NPV], PVr[0:NPV, :], ident[0:NPV, 0:NPV]).then_inc(s_pvt, 1)
            pe.transpose(PS[:, 7, 0:TAPS * CT], CWr[:], ident[0:TAPS * CT, 0:TAPS * CT]).then_inc(s_pvt, 1)
            pe.wait_ge(s_pvc, 2)

            def norm_turn(n, tiles):
                N = norms[n]
                for t in range(tiles):
                    pe.wait_ge(N["scaled"], t + 1)
                    if t >= 4:
                        pe.wait_ge(N["drained"], 2 * (t - 3))
                    for b in range(2):
                        for k in range(4):
                            ins = pe.transpose(PS[:, 2 * (t % 4) + b, P * k:P * (k + 1)],
                                               XN[:, t % 2, P * (4 * b + k):P * (4 * b + k + 1)], ident[:])
                        ins.then_inc(N["turned"], 1)
                pe.wait_ge(N["drained"], 2 * tiles)

            g = 0
            n = 0

            def arrived():
                pe.wait_ge(s_ring[g % NR], 16 * (g // NR + 1))

            def group(seg, n, out, lhs, rhs):
                if n >= 8:
                    pe.wait_ge(s_dr[seg], n - 7)
                for k in range(KT):
                    ins = pe.matmul(out, lhs(k), rhs(k), start=(k == 0), stop=(k == KT - 1))
                ins.then_inc(s_mm[seg], 1)

            def chunk_T(seg, src, fts=2, width=512):
                nonlocal g, n
                arrived()
                halves = src.shape[2] // width
                for ft in range(fts):
                    for th in range(halves):
                        group(seg, n, bank_groups(n, width),
                              lambda k: ring[:, g % NR, k, P * ft:P * (ft + 1)],
                              lambda k: src[:, k, width * th:width * (th + 1)])
                        n += 1
                g += 1

            def chunk_tm(seg, src, tiles):
                nonlocal g, n
                arrived()
                for t in range(tiles):
                    group(seg, n, bank_groups(n, 256), lambda k: src(k)[:, P * t:P * (t + 1)],
                          lambda k: ring[:, g % NR, k, :])
                    n += 1
                g += 1

            norm_turn("m", MT)
            norm_turn("x", TT)

            def memory_chunk(c):
                nonlocal g
                arrived()
                for i in range(2):
                    m = 2 * c + i
                    if m >= 4:
                        pe.wait_ge(s_dr["mem"], m - 3)
                    for k in range(KT):
                        w = ring[:, g % NR, k, :]
                        if c < 4:
                            lhs, rhs = w[:, P * i:P * (i + 1)], mT[:, k, :]
                        else:
                            lhs, rhs = mT[:, k, P * i:P * (i + 1)], w
                        ins = pe.matmul(PS[:, 4 + m % 4, 0:256], lhs, rhs, start=(k == 0), stop=(k == KT - 1))
                    ins.then_inc(s_mm["mem"], 1)
                g += 1

            n = 0
            chunk_T("in", hT, fts=1)
            for c in range(6):
                chunk_T("in", hT)
            for c in range(4):
                chunk_tm("in", lambda k: hT[:, k, :], TT)
            pe.wait_ge(s_dr["in"], 58)

            pe.wait_ge(s_cv, TAPS * CT)
            for th in range(2):
                for c in range(CT):
                    ins = pe.matmul(PS[:, th, :], ones[:], yT[:, c, 512 * th:512 * (th + 1)],
                                    start=(c == 0), stop=(c == CT - 1))
                ins.then_inc(s_lnp, 1)
            pe.wait_ge(s_lna, CT)
            for th in range(2):
                for c in range(CT):
                    ins = pe.matmul(PS[:, 2 + th, :], ones[:], o_gla[:, 2 * c + th, :],
                                    start=(c == 0), stop=(c == CT - 1))
                ins.then_inc(s_lnp, 1)
            pe.wait_ge(s_lnv, 10)

            for p in range(2):
                if p:
                    pe.wait_ge(s_oe, 16 * p)
                for i in range(4):
                    d, th = i // 2, i % 2
                    pe.matmul(PS[:, i, :], W2[:, d, P * p:P * (p + 1)], gT[:, 512 * th:512 * (th + 1)],
                              start=True, stop=True).then_inc(s_z, 1)
                if p:
                    pe.wait_ge(s_st, 14 * p)
                memory_chunk(4 * p)
                memory_chunk(4 * p + 1)
                for l in range(8):
                    L = 8 * p + l
                    if l == 0:
                        pe.wait_ge(s_zmin, 4 * (p + 1))
                        pe.wait_ge(s_zabs, 4 * (p + 1))
                    else:
                        pe.wait_ge(s_kq, 9 * p + l)
                        if l >= 2:
                            pe.wait_ge(s_sel, 4 * (L - 1))
                    K_, Q_ = (kT[:, p, :], qT[:, p, :]) if l == 0 else (
                        (KQ, KQ2)[(l - 1) % 2][:, i, :] for i in range(2))
                    for b in range(4):
                        hh, half = b // 2, b % 2
                        for w in range(4):
                            a = slice(P * (4 * half + w), P * (4 * half + w + 1))
                            hp = slice(GDK * hh, GDK * (hh + 1))
                            ins = pe.matmul(PS[:, 4 * (L % 2) + b, P * w:P * (w + 1)], K_[hp, a], Q_[hp, a],
                                            start=True, stop=True)
                        ins.then_inc(s_gram, 1)
                    if l == 0:
                        memory_chunk(4 * p + 2)
                        memory_chunk(4 * p + 3)
                        pe.wait_ge(s_dr["mem"], 8 * (p + 1))
                pe.wait_ge(s_kq, 9 * p + 8)
                pe.wait_ge(s_sel, 32 * (p + 1))
                for b in range(4):
                    for i in range(4):
                        m = 4 * b + i
                        ins = pe.transpose(PS[:, b, P * i:P * (i + 1)],
                                           KQ2[:, m // TT, P * (m % TT):P * (m % TT + 1)], ident[:])
                    ins.then_inc(s_ket, 1)
                pe.wait_ge(s_kev, 4 * (p + 1))
                for i in range(14):
                    d = i % 2
                    w = i // 2 if d == 0 else TT - 1 - i // 2
                    if i >= 4:
                        pe.wait_ge(s_st, 14 * p + i - 3)
                    m = TT * d + w
                    pe.matmul(PS[:, 4 + i % 4, 0:256], KEt[:, m // 4, P * (m % 4):P * (m % 4 + 1)],
                              v_tm[:, w, 256 * p:256 * (p + 1)], start=True, stop=True).then_inc(s_U, 1)
                pe.wait_ge(s_kq, 9 * p + 9)
                pe.wait_ge(s_st, 14 * (p + 1))
                for i in range(16):
                    w, hh = i // 2, i % 2
                    h = 2 * p + hh
                    if i >= 4:
                        pe.wait_ge(s_oe, 16 * p + i - 3)
                    o = PS[:, i % 4, 0:P]
                    hp = slice(GDK * hh, GDK * (hh + 1))
                    tw = slice(P * w, P * (w + 1))
                    pe.matmul(o, Ssc[:, hh, w, :], v_tm[:, w, P * h:P * (h + 1)], start=True, stop=False)
                    pe.matmul(o, KQ[hp, 0, tw], ST[hp, 0, w, :], start=False, stop=False)
                    pe.matmul(o, KQ[hp, 1, tw], ST[hp, 1, w, :], start=False, stop=True).then_inc(s_op, 1)
            pe.wait_ge(s_ov, 8)
            pe.wait_ge(s_oe, 32)
            for c in range(CT):
                for b in range(2):
                    for i in range(4):
                        ins = pe.transpose(PS[:, 2 * c + b, P * i:P * (i + 1)],
                                           o_gla[:, 4 * b + i, P * c:P * (c + 1)], ident[:])
                    ins.then_inc(s_at, 1)
            pe.wait_ge(s_ae, 8)
            pe.wait_ge(s_lnv, 19)
            n = 0
            for c in range(4):
                chunk_tm("out", lambda k: aT[:, k, :] if k < CT else yT[:, k - CT, :], TT)
            pe.wait_ge(s_dr["out"], 32)
            norm_turn("y", TT)
            n = 0
            for c in range(4):
                chunk_T("q", hT)
            pe.wait_ge(s_dr["q"], 16)
            for h in range(XH):
                def turn(t):
                    i = TT * h + t
                    pe.wait_ge(s_sv, 4 * (i + 1))
                    if i >= 2:
                        pe.wait_ge(s_pc, i - 1)
                    for m in range(MT):
                        ins = pe.transpose(PS[:, 2 + i % 2, P * m:P * (m + 1)], pr[:, i % 2, P * m:P * (m + 1)],
                                           ident[:])
                    ins.then_inc(s_pt, 1)

                for t in range(TT):
                    i = TT * h + t
                    if i >= 2:
                        pe.wait_ge(s_pe, i - 1)
                    for k in range(2):
                        ins = pe.matmul(PS[:, i % 2, 0:256], qxT[:, 2 * h + k, P * t:P * (t + 1)],
                                        kx[:, 2 * h + k, :], start=(k == 0), stop=(k == 1))
                    ins.then_inc(s_sc, 1)
                    if t:
                        turn(t - 1)
                turn(TT - 1)
                pe.wait_ge(s_pc, TT * (h + 1))
                if h:
                    pe.wait_ge(s_ax, 4 * h)
                for b in range(4):
                    ft, th = b // 2, b % 2
                    for m in range(MT):
                        ins = pe.matmul(PS[:, 4 + b, :], vx[:, m, XDH * h + P * ft:XDH * h + P * (ft + 1)],
                                        pT[:, h % 2, m, 512 * th:512 * (th + 1)], start=(m == 0), stop=(m == 1))
                    ins.then_inc(s_av, 1)
            pe.wait_ge(s_ax, 16)
            n = 0
            for c in range(4):
                chunk_tm("o", lambda k: oxT[:, k, :], TT)
            pe.wait_ge(s_dr["o"], 32)

            def router(t):
                pe.wait_ge(s_h3e, 2 * (t + 1))
                if t >= 2:
                    pe.wait_ge(s_lg, t - 1)
                if t == 0:
                    pe.wait_ge(s_rpar, 7 * 16)
                for k in range(KT):
                    ins = pe.matmul(PS[:, 4 + t % 2, 0:E], h3T[:, t % 2, k, :], rw[:, k, :],
                                    start=(k == 0), stop=(k == KT - 1))
                ins.then_inc(s_lgp, 1)

            for t in range(TT):
                pe.wait_ge(norms["z"]["scaled"], t + 1)
                if t >= 2:
                    pe.wait_ge(s_h3e, 2 * (t - 1))
                for b in range(2):
                    for k in range(4):
                        ins = pe.transpose(PS[:, 2 * (t % 2) + b, P * k:P * (k + 1)],
                                           h3[:, t, P * (4 * b + k):P * (4 * b + k + 1)], ident[:])
                    ins.then_inc(norms["z"]["turned"], 1)
                if t:
                    router(t - 1)
            router(TT - 1)
            pe.wait_ge(s_rt, RT_M)
            pe.wait_ge(s_rmi, 2)
            for t in range(TT):
                o = PS[:, 6, E * t:E * (t + 1)]
                ins = pe.matmul(o, beforeb[:], Mb[:, t, :], start=True, stop=(t == 0))
                for j in range(t):
                    ins = pe.matmul(o, onesb[:], Mb[:, j, :], start=False, stop=(j == t - 1))
            ins.then_inc(s_rk, 1)
            for t in range(TT):
                ins = pe.matmul(PS[:, 7, 0:E], onesb[:], Mb[:, t, :], start=(t == 0), stop=(t == TT - 1))
            ins.then_inc(s_rk, 1)
            pe.wait_ge(s_rt, RT_GD)
            pe.wait_ge(s_h3e, 2 * TT)
            for b in range(2):
                for i in range(4):
                    ins = pe.transpose(PS[0:E, b, P * i:P * (i + 1)], GD[:, 4 * b + i, :], ident[:])
                ins.then_inc(s_gdt, 1)
            def down_bias(i):
                if i >= 4:
                    pe.wait_ge(s_bdr, i - 3)
                t, b = i // 2, i % 2
                pe.matmul(PS[:, i % 4, :], GDT[:, P * t:P * (t + 1)], bdn[:, 512 * b:512 * (b + 1)],
                          start=True, stop=True).then_inc(s_bd, 1)

            pe.wait_ge(s_gde, 2)
            for i in range(4):
                down_bias(i)
            pe.wait_ge(s_lg, TT)
            for t in range(TT):
                pe.wait_ge(s_oh, t + 2)
                for k in range(TOPK):
                    ins = pe.matmul(PS[:, 4, 0:NB], rowhot[:, t % 2, k, :], blkhot[:, TOPK * t + k, :],
                                    start=(t == 0 and k == 0), stop=(t == TT - 1 and k == TOPK - 1))
                ins.then_inc(s_tm, 1)
            for i in range(4, 2 * TT):
                down_bias(i)
            pe.wait_ge(s_tab, 1)
            pe.wait_ge(s_bup, 8)

            def two_blocks(t):
                return pe.value_load(VT[0:1, 2, bass.ds(t, 1)], min_val=0, max_val=1)

            def turn(src, blocks, done):
                for b in range(blocks):
                    for k in range(KT):
                        ins = pe.transpose(PS[:, 4 + 2 * b + k // 4, P * (k % 4):P * (k % 4 + 1)],
                                           src[:, b, P * k:P * (k + 1)], ident[:])
                ins.then_inc(done, 1)

            def turn_tokens(t, both):
                pe.wait_ge(s_xsl, 32 * (t + 1))
                with pe.If(both >= 1):
                    turn(xs, 2, s_xt)
                with pe.Else():
                    turn(xs, 1, s_xt)

            def turn_hidden(t, both):
                pe.wait_ge(s_hid, 4 * t + 4)
                pe.wait_ge(s_xlo, t + 2)
                with pe.If(both >= 1):
                    turn(hid, 2, s_ht)
                with pe.Else():
                    turn(hid, 1, s_ht)

            def products(i, blocks, hi, lo, k0, slot, start, stop):
                for kk in range(4):
                    k = k0 + kk
                    for b in range(blocks):
                        o = PS[:, 2 * (i % 2) + b, :]
                        pe.matmul(o, hi[:, b, k, :], whi[:, slot, kk, :], start=start and kk == 0, stop=False)
                        pe.matmul(o, hi[:, b, k, :], wlo[:, slot, kk, :], start=False, stop=False)
                        ins = pe.matmul(o, lo[:, b, k, :], whi[:, slot, kk, :], start=False,
                                        stop=stop and kk == 3)
                ins.then_inc(s_wmm, 1)

            def up(t, both, c0):
                def all_groups(blocks):
                    for i in range(4):
                        if i < 2:
                            if c0 == 0:
                                pe.wait_ge(s_yev, 2 * t - 1 + i)
                        elif i == 2:
                            pe.wait_ge(s_g, 2 * t + 1)
                        else:
                            pe.wait_ge(s_upr, 2 * t + 1)
                        for b in range(blocks):
                            pe.matmul(PS[:, 2 * (i % 2) + b, :], SEL[:], bup[:, UPCOL[i]:UPCOL[i] + 512],
                                      start=True, stop=False)
                        for half in range(2):
                            c = c0 + 2 * i + half
                            wait_lo(pe, t, c)
                            products(i, blocks, xhi, xlo, 4 * half, chunk_slot(c, NSPL), False, half == 1)
                pe.wait_ge(s_xlo, t + 1)
                pe.wait_ge(s_bsel, t + 1)
                with pe.If(both >= 1):
                    all_groups(2)
                with pe.Else():
                    all_groups(1)

            def down(t, both):
                def all_groups(blocks):
                    for i in range(2):
                        pe.wait_ge(s_g if i == 0 else s_upr, 2 * t + 2)
                        for half in range(2):
                            c = 8 + 2 * i + half
                            wait_lo(pe, t, c)
                            products(i, blocks, hhi, hlo, 4 * half, chunk_slot(c, NSPL), half == 0, half == 1)
                pe.wait_ge(s_hlo, t)
                with pe.If(both >= 1):
                    all_groups(2)
                with pe.Else():
                    all_groups(1)

            used_ = pe.value_load(usedb[0:1, 0:1], min_val=1, max_val=NVIS)
            both0 = two_blocks(0)
            turn_tokens(0, both0)
            up(0, both0, 4)
            pe.wait_ge(s_xlo, 1)
            turn_tokens(1, two_blocks(1))
            turn_hidden(0, both0)
            with pe.Fori(1, NVIS + 1) as t:
                with pe.If(t <= used_):
                    both, both_last, both_next = two_blocks(t), two_blocks(t - 1), two_blocks(t + 1)
                    up(t, both, 0)
                    pe.wait_ge(s_hlo, t)
                    turn_tokens(t + 1, both_next)
                    down(t, both_last)
                    turn_hidden(t, both)
                    pe.wait_ge(s_hlo, t)


_INS = ["x", "mem", "norm_mix_g", "w_in", "gate_w2_fwd", "gate_b_fwd", "gate_w2_bwd", "gate_b_bwd",
        "gla_norm_g", "conv_w", "conv_b", "conv_ln_g", "conv_ln_b", "w_out", "norm_xattn_g", "norm_mem_g",
        "xattn_wq", "xattn_wk", "xattn_wv", "xattn_wo", "norm_ffn_g", "router_w", "router_b", "exp_w_up",
        "exp_b_up", "exp_w_down", "exp_b_down", "final_norm_g"]


def kernel(**inputs):
    import numpy as np
    from concourse import bacc
    from concourse.bass_utils import run_bass_kernel_spmd

    nc = bacc.Bacc("TRN2", target_bir_lowering=False, num_devices=1)
    arrays, aps = {}, {}
    for name in _INS:
        a = np.ascontiguousarray(inputs[name])
        arrays["in_" + name] = a
        aps[name] = nc.dram_tensor("in_" + name, a.shape, mybir.dt.from_np(a.dtype), kind="ExternalInput").ap()
    aps["out"] = nc.dram_tensor("out_y", (1, S, D), F, kind="ExternalOutput").ap()
    build(nc, aps)
    r = run_bass_kernel_spmd(nc, [arrays], core_ids=[0])
    return r.results[0]["out_y"]
```

```python
from contextlib import ExitStack

import concourse.bass as bass
from concourse import mybir

F = mybir.dt.float32
FR = mybir.dt.float32r
BF = mybir.dt.bfloat16
I32 = mybir.dt.int32
U32 = mybir.dt.uint32
U8 = mybir.dt.uint8
ALU = mybir.AluOpType
ACT = mybir.ActivationFunctionType
X = mybir.AxisListType.X

P = 128
S = 1024
D = 1024
KT = D // P
TT = S // P
MT = 2
GH, GDV, GDK = 4, 128, 64
GK = GH * GDK
GW = GH * GDV
CW_ = 512
CT = CW_ // P
TAPS = 31
PAD = TAPS // 2
RANK = 16
TAU = 16.0
XH = 4
XDH = D // XH
E = 32
TOPK = 4
FF = 1024
ALPHA, LIMIT = 1.702, 7.0
RMS_EPS, LN_EPS = 1e-6, 1e-5
Q0, K0, V0, R0 = 0, GK, 2 * GK, 2 * GK + GW
G0 = R0 + GW
A0 = G0 + 2 * RANK
B0 = A0 + CW_
NBLK = (S * TOPK + E * (P - 1) + P - 1) // P
NB = 66
NVIS = (S * TOPK + E * (2 * P - 1)) // (2 * P)
NV = NVIS + 3
RT_M, RT_GD = 9, 17
LEVELS = [64, 32, 16, 8, 4, 2, 1]
KIB = 1024
BASE = 16512


def build(nc, A):
    with ExitStack() as ctx:
        def sb(name, shape, dt, kib):
            return nc.alloc_sbuf_tensor_at(name, shape, dt, offset=BASE + int(kib * KIB))

        def sem(name):
            return ctx.enter_context(nc.semaphore(name))

        arena = ctx.enter_context(nc.sbuf_tensor("arena", [P, 212800], U8))
        assert arena is not None
        PS = ctx.enter_context(nc.psum_tensor("PS", [P, 8, 512], F))

        NR = 4
        ring = sb("ring", [P, NR, KT, 256], F, 0)
        xH = sb("xH", [P, KT, S], FR, 32)
        xL = [sb("xL0", [P, 6, S], FR, 149), sb("xL1", [P, 2, S], FR, 181)]
        wiH = [sb(f"wiH{i}", [P, KT, 256], FR, 16 + 8 * i) for i in range(2)]
        wiL = sb("wiL", [P, 2, KT, 256], FR, 0)
        gmb = sb("gmb", [P, D], F, 141)
        o_gla = sb("o_gla", [P, TT, GW], F, 32)
        EX = sb("EX", [P, 2, S], F, 48)
        KQ = sb("KQ", [P, 2, S], F, 56)
        KQ2 = sb("KQ2", [P, 2, S], F, 120)
        KEt = sb("KEt", [P, 4, 512], F, 48)
        SR = sb("SR", [P, TT, GW], F, 157)
        xres = sb("xres", [P, TT, D], F, 64)
        qT = sb("qT", [P, 2, S], F, 64)
        kT = sb("kT", [P, 2, S], F, 72)
        v_tm = sb("v_tm", [P, TT, GW], F, 80)
        r_tm = sb("r_tm", [P, TT, GW], F, 96)
        UW = S + 2 * PAD
        u_pad = sb("u_pad", [P, CT, UW], F, 112)
        qxT = sb("qxT", [P, KT, S], F, 149)
        mT = sb("mT", [P, KT, MT * P], F, 173)
        sig = sb("sig", [P, S], F, 129)
        yT = sb("yT", [P, CT, S], F, 133)
        mem_tm = sb("mem_tm", [P, MT, D], F, 133)
        Bf = sb("Bf", [P, S], F, 149)
        Rb = sb("Rb", [P, S], F, 153)
        Ssc = sb("Ssc", [P, 2, TT, P], F, 157)
        ST = sb("ST", [P, 2, TT, P], F, 165)
        aH = sb("aH", [P, CT, S], FR, 149)
        aL = sb("aL", [P, CT, S], FR, 48)
        yH = [sb(f"yH{i}", [P, 2, S], FR, 165 + 24 * i) for i in range(2)]
        yL = sb("yL", [P, CT, S], FR, 133)
        wuH = [sb(f"wuH{i}", [P, KT, 256], FR, 120 - 24 * i) for i in range(2)]
        kx = sb("kx", [P, KT, MT * P], F, 181)
        vx = sb("vx", [P, MT, D], F, 112)
        XN = sb("XN", [P, 2, D], F, 189)
        gT = sb("gT", [2 * RANK, S], F, 189)
        pr = sb("pr", [P, 4, MT * P], F, 129)
        pT = sb("pT", [P, 2, MT, S], F, 133)
        gxb = sb("gxb", [P, D], F, 173)
        hH = sb("hH", [P, KT, S], FR, 32)
        hL = [sb(f"hL{i}", [P, 4, S], FR, 96 + 37 * i) for i in range(2)]
        wqH = [sb(f"wqH{i}", [P, KT, 256], FR, 120 + 69 * i) for i in range(2)]
        ringL = sb("ringL", [P, NR, KT, 256], FR, 0)
        oxH = sb("oxH", [P, KT, S], FR, 32)
        oxL = sb("oxL", [P, KT, S], FR, 149)
        woH = [sb(f"woH{i}", [P, KT, 256], FR, 96 + 16 * i) for i in range(2)]
        woL = [sb(f"woL{i}", [P, KT, 256], FR, 104 + 16 * i) for i in range(2)]
        ident = sb("ident", [P, P], F, 197)
        ones = sb("ones", [P, P], F, 197.5)
        before = sb("before", [P, P], F, 198)
        masks = sb("masks", [P, 7, P], U8, 198.5)
        W2 = sb("W2", [2 * RANK, 2, GK], F, 199.5)
        PV = sb("PV", [P, 64], F, 201.5)
        CWT = sb("CWT", [P, TAPS * CT], F, 201.75)
        ngb = sb("ngb", [P, GDV], F, 202.25)
        st8 = sb("st8", [P, 4, 32], F, 202.75)
        TTd = sb("TTd", [P, 2, 2, TT], F, 203.25)
        smx = sb("smx", [P, 4, 4], F, 203.4375)
        xor = sb("xor", [P, P], I32, 203.5)
        mtmp = sb("mtmp", [P, P], F, 204)
        PVr = sb("PVr", [64, P], F, 204.5)
        CWr = sb("CWr", [TAPS * CT, P], F, 205)
        pid = sb("pid", [P, 8], F, 205.5)
        iot = sb("iot", [P, P], F, 206)

        h3T = sb("h3T", [P, 2, KT, P], F, 96)
        rw = sb("rw", [P, KT, E], F, 104)
        h3 = sb("h3", [P, TT, D], F, 32)
        rbb = sb("rbb", [P, E], F, 105)
        LG = sb("LG", [P, TT, E], F, 106)
        MX = sb("MX", [P, TT, 8], F, 107)
        IX = sb("IX", [P, TT, 8], U32, 107.25)
        IXf = sb("IXf", [P, TT, 8], F, 107.5)
        gsum = sb("gsum", [P, 2, TT], F, 107.75)
        OH = sb("OH", [P, TT, TOPK, E], F, 108)
        M = sb("M", [P, TT, E], F, 112)
        slot0 = sb("slot0", [P, TT, E], F, 113)
        ex1 = sb("ex1", [P, 8, E], F, 114)
        exi = sb("exi", [P, 2, E], I32, 115)
        tmpA = sb("tmpA", [P, NB * E], F, 116)
        tmpC = sb("tmpC", [P, NV * E], F, 168)
        rowhot = sb("rowhot", [P, 2, TOPK, P], F, 125)
        blkhot = sb("blkhot", [P, TT * TOPK, NB], F, 175)
        GD = sb("GD", [P, TT, E], F, 132)
        GDT = sb("GDT", [E, S], F, 133)
        bdn = sb("bdn", [E, D], F, 137)
        di = sb("di", [P, 3, TT * TOPK], I32, 141)
        df = sb("df", [P, 3, TT * TOPK], F, 141.5)
        Mb = sb("Mb", [P, TT, E], BF, 142)
        onesb = sb("onesb", [P, P], BF, 142.5)
        beforeb = sb("beforeb", [P, P], BF, 142.75)
        gfb = sb("gfb", [P, D], F, 189)
        bstage = sb("bstage", [P, 2 * FF], F, 152)
        Gt = sb("Gt", [P, TT, TOPK], F, 198.5)
        rowof = sb("rowof", [P, TT * TOPK], U32, 198.75)
        TM = sb("TM", [P, NB], U32, 199)
        EB = sb("EB", [P, NV], F, 199.375)
        VT = sb("VT", [P, 3, NV], I32, 199.625)
        usedb = sb("usedb", [P, 1], I32, 200.5)
        idxc = sb("idxc", [P, 2], U32, 200.5625)
        pmod = sb("pmod", [P, 2], F, 200.625)
        pmi = sb("pmi", [P, 2], I32, 200.6875)
        SEL = sb("SEL", [P, P], BF, 200.75)
        vt = sb("vt", [P, 4, NV], F, 201)
        NRAW, NSPL = 4, 4
        raw = sb("raw", [P, NRAW, 4, 512], F, 0)
        whi = sb("whi", [P, NSPL, 4, 512], FR, 96)
        wlo = sb("wlo", [P, NSPL, 4, 512], FR, 32)
        xhi = sb("xhi", [P, 2, KT, P], FR, 128)
        xlo = sb("xlo", [P, 2, KT, P], FR, 136)
        hhi = sb("hhi", [P, 2, KT, P], FR, 144)
        hlo = sb("hlo", [P, 2, KT, P], FR, 152)
        xs = sb("xs", [P, 2, D], F, 160)
        glu = sb("glu", [P, 2, 512], F, 168)
        sgm = sb("sgm", [P, 2, 512], F, 172)
        hid = sb("hid", [P, 2, FF], F, 176)
        bup = sb("bup", [P, 2 * FF], BF, 184)
        yb = sb("yb", [P, 2, D], F, 189)
        yg = sb("yg", [P, 8, D], F, 0)
        fo = sb("fo", [P, 2, D], F, 32)
        fgb = sb("fgb", [P, D], F, 40)
        sqs = sb("sqs", [P, D], F, 44)
        h3_dram = nc.dram_tensor("h3_scratch", (S, D), F, kind="Internal").ap()
        ys_dram = nc.dram_tensor("ys_scratch", ((NBLK + 1) * P, D), F, kind="Internal").ap()

        s_par = sem("params_loaded")
        s_const = sem("constants_built")
        s_mask = sem("masks_built")
        s_w2z = sem("w2_zeroed")
        s_pvt = sem("vectors_transposed")
        s_pvc = sem("vectors_ready")
        s_ring = [sem(f"chunk_loaded{i}") for i in range(NR)]
        s_xld = [sem(f"x_loaded{i}") for i in range(4)]
        norms = {}
        for n in ("m", "x", "y", "z"):
            norms[n] = {k: sem(f"norm_{n}_{k}") for k in
                        ("stats_by_scalar", "stats_by_vector", "scaled", "turned") + ("drained",) * (n != "z")}
        norms["m"]["loaded"] = sem("memory_loaded")
        s_mm = {k: sem(f"{k}_product") for k in ("mem", "in", "out", "q", "o")}
        s_dr = {k: sem(f"{k}_drained") for k in ("mem", "in", "out", "q", "o")}
        s_pad = sem("margins_zeroed")
        s_u = sem("glu_ready")
        s_cv = sem("conv_tap")
        s_lnp, s_lna, s_lnv = sem("ln_by_tensor"), sem("ln_by_scalar"), sem("ln_by_vector")
        s_z, s_zabs, s_zln, s_zmin, s_la, s_scan, s_tot, s_rb, s_dec = (
            sem(n) for n in ("gate_product", "gate_abs", "gate_softplus", "gate_min", "log_decay", "scanned",
                             "totals", "suffix_ready", "window_decay"))
        s_sub, s_ex, s_kq, s_gram, s_sel = (
            sem(n) for n in ("exponent_ready", "decay_ready", "decayed_kq", "gram_product", "scores_selected"))
        s_ket, s_kev, s_U, s_st, s_st0, s_op, s_oe = (
            sem(n) for n in ("k_turned", "k_token_major", "window_update", "state_ready", "state_zero", "gla_product",
                             "gla_drained"))
        s_axl, s_bld = sem("xout_lo"), sem("expert_biases_loaded")
        s_gxb, s_hh = sem("xattn_gain_loaded"), sem("hidden_states_hi")
        s_gmb, s_xh = sem("mix_gain_loaded"), sem("x_hi")
        s_dhi, s_dlp, s_dlv = (sem(n) for n in ("dense_hi", "dense_lo_by_pool", "dense_lo_by_vector"))
        s_yh, s_yl, s_al = (sem(n) for n in ("y_hi", "y_lo", "a_lo"))
        s_sr, s_osq = sem("r_sigmoid"), sem("o_squares")
        s_ov, s_oa, s_at, s_ae = (sem(n) for n in ("o_norm_by_vector", "o_norm_by_scalar", "a_turned", "a_ready"))
        s_sc, s_sv, s_pe, s_pt, s_pc, s_av, s_ax = (
            sem(n) for n in ("xscores", "softmax_by_vector", "xprob", "xprob_turned", "xprob_T", "xvalue", "xout"))
        s_xre = sem("x_reloaded_and_rows_filled")
        s_out = [sem(f"out_stored{i}") for i in range(2)]
        s_rpar, s_ffg, s_h3s = sem("router_loaded"), sem("final_gain_loaded"), sem("h3_stored")
        s_h3e, s_lgp, s_lg, s_top, s_rt = (
            sem(n) for n in ("h3_turned_out", "logit_product", "logits", "top8", "routing_step"))
        s_gx, s_rk, s_rg, s_oh, s_tm, s_gdt, s_gde, s_bd, s_bdr = (
            sem(n) for n in ("gate_exp", "rank_product", "r_gated", "row_onehot", "token_map_product",
                             "gates_turned", "gates_turned_out", "bias_down_product", "bias_down_added"))
        s_bup, s_tab, s_rmi = sem("bias_parts"), sem("tables_ready"), sem("partition_ids")
        s_raw = [sem(f"expert_chunk_loaded{i}") for i in range(NRAW)]
        s_whi, s_wlv, s_wlp, s_wmm = (sem(n) for n in ("chunk_hi", "chunk_lo_by_vector", "chunk_lo_by_pool",
                                                       "chunk_multiplied"))
        s_idx, s_xsl, s_xt, s_xhi, s_xlo = (sem(n) for n in ("index_column", "tokens_gathered", "tokens_turned",
                                                             "tokens_hi", "tokens_lo"))
        s_bsel, s_g, s_upr, s_sg, s_hid, s_ht, s_hhi, s_hlo = (
            sem(n) for n in ("bias_selector", "glu_clamped", "up_banks_read", "expert_sigmoid", "hidden",
                             "hidden_turned", "hidden_hi", "hidden_lo"))
        s_yev, s_yst = sem("rows_drained"), sem("rows_stored")
        s_yg = [sem(f"rows_gathered{i}") for i in range(8)]
        s_ac, s_fa, s_fv, s_fo = (sem(n) for n in ("row_added", "final_by_scalar", "final_by_vector",
                                                   "final_scaled"))

        w_in, w_out = A["w_in"][0], A["w_out"][0]
        wq, wk, wv, wo = (A[f"xattn_w{c}"][0] for c in "qkvo")
        x_in = A["x"][0].rearrange("(t p) d -> p t d", p=P)
        mem_in = A["mem"][0].rearrange("(t p) d -> p t d", p=P)
        out_v = A["out"][0].rearrange("(t p) d -> p t d", p=P)

        chunks = ([(w_in, G0), (w_in, A0), (w_in, B0), (w_in, A0 + 256), (w_in, B0 + 256),
                     (w_in, Q0), (w_in, K0), (w_in, V0), (w_in, V0 + 256), (w_in, R0), (w_in, R0 + 256)]
                  + [(wk, 256 * c) for c in range(4)] + [(wv, 256 * c) for c in range(4)]
                  + [(w_out, 256 * c) for c in range(4)] + [(wq, 256 * c) for c in range(4)]
                  + [(wo, 256 * c) for c in range(4)])
        used = ([("in", n) for n in (2, 6, 10, 14, 18, 22, 26, 34, 42, 50, 58)]
                + [("mem", 2 * (c + 1)) for c in range(8)]
                + [("out", 8 * (c + 1)) for c in range(4)] + [("q", 4 * (c + 1)) for c in range(4)]
                + [("o", 8 * (c + 1)) for c in range(4)])
        N_IN, g_out = 11, 19
        slot_of = [g % 2 if g < N_IN else g % NR for g in range(len(chunks))]
        fills = [slot_of[:g + 1].count(slot_of[g]) for g in range(len(chunks))]
        def scaled_max(n):
            h, t = n // TT, n % TT
            return 4 * TT * h + (4 * t if t else 2)

        def normalised(n):
            h, t = n // TT, n % TT
            return 4 * TT * h + min(4 * t + 6, 4 * TT)

        def score_bank(n):
            return PS[:, n % 3, 0:256]

        GM, ZB, CB, LG_, LB = 0, 8, 12, 16, 20
        NPV = 24

        def bank_groups(n, width=512):
            return PS[:, n % 8, 0:width]

        w_up, w_dn = A["exp_w_up"][0], A["exp_w_down"][0]

        UPCOL = [0, FF, 512, FF + 512]

        def chunk_slot(c, n):
            return (c - 4) % n

        def wait_lo(eng, t, c):
            if c % 3 == 0:
                eng.wait_ge(s_wlp, 4 * t + (c - 3) // 3)
            else:
                eng.wait_ge(s_wlv, 8 * t + (c - 3) - (c - 3) // 3)

        def wait_raw(eng, t, c):
            eng.wait_ge(s_raw[chunk_slot(c, NRAW)], 16 * 12 // NRAW * t + 16 * ((c - 4) // NRAW + 1))

        def wait_multiplied(eng, t, c):
            eng.wait_ge(s_wmm, 12 * t + c - 3)

        block = ctx.enter_context(nc.Block())

        @block.sync
        def _(sp):
            sp.dma_start(mem_tm[:], mem_in).then_inc(norms["m"]["loaded"], 16)
            for i in range(4):
                sp.dma_start(xres[:, 2 * i:2 * i + 2, :], x_in[:, 2 * i:2 * i + 2, :]).then_inc(s_xld[i], 16)
            for g, (w, c0) in enumerate(chunks):
                if 2 <= g < N_IN + NR:
                    last = used[min(g, N_IN + 1) - 2]
                    sp.wait_ge(s_mm[last[0]], last[1])
                elif g >= NR:
                    sp.wait_ge(s_mm[used[g - NR][0]], used[g - NR][1])
                sp.dma_start(ring[:, slot_of[g]], w[:, c0:c0 + 256].rearrange("(k p) n -> p k n", p=P)
                             ).then_inc(s_ring[slot_of[g]], 16)
                if g == 18 + NR:
                    sp.wait_ge(s_const, 1)
                    fresh_rows = ys_dram[S * TOPK:(NBLK + 1) * P, :].rearrange("(p b) (r c) -> p (b r) c", p=P, c=P)
                    sp.dma_start(fresh_rows, ones[:].unsqueeze(1).broadcast_to(
                        [P, fresh_rows.shape[1], P])).then_inc(s_xre, 16)
                    sp.wait_ge(s_oe, 2 * 16)
                    sp.dma_start(xres[:], x_in).then_inc(s_xre, 16)
            for t in range(TT):
                sp.wait_ge(norms["z"]["scaled"], t + 1)
                sp.dma_start(h3_dram[P * t:P * (t + 1), :], h3[:, t, :]).then_inc(s_h3s, 16)
            def load_chunk(t, c, e_up, e_dn, fresh=False):
                if not fresh:
                    wait_lo(sp, t, c - NRAW)
                if e_dn is None or c < 8:
                    j = c - 4 if e_dn is None and c >= 4 else c
                    w, e, col = w_up, e_up, UPCOL[j // 2]
                else:
                    j = c - 8
                    w, e, col = w_dn, e_dn, 512 * (j // 2)
                src = w[bass.ds(e, 1), 512 * (j % 2):512 * (j % 2 + 1), col:col + 512]
                sp.dma_start(raw[:, chunk_slot(c, NRAW)], src.rearrange("e (k p) n -> p (e k) n", p=P)
                             ).then_inc(s_raw[chunk_slot(c, NRAW)], 16)

            def expert(t):
                return sp.value_load(VT[0:1, 0, bass.ds(t, 1)], min_val=0, max_val=E - 1)

            sp.wait_ge(s_tab, 1)
            used_ = sp.value_load(usedb[0:1, 0:1], min_val=1, max_val=NVIS)
            e0, e1 = expert(0), expert(1)
            for c in range(4, 12):
                load_chunk(0, c, e0, None, fresh=c < 4 + NRAW)
            for c in range(3):
                load_chunk(1, c, e1, None)
            with sp.Fori(1, NVIS + 1) as t:
                with sp.If(t <= used_):
                    eu, ed, en = expert(t), expert(t - 1), expert(t + 1)
                    for c in range(3, 12):
                        load_chunk(t, c, eu, ed)
                    for c in range(3):
                        load_chunk(t + 1, c, en, ed)
            wait_lo(sp, used_ + 1, 1)
            wait_lo(sp, used_ + 1, 2)
            wait_lo(sp, used_ + 1, 0)
            sp.dma_start(fgb[:], A["final_norm_g"].partition_broadcast(P)).then_inc(s_ffg, 16)
            for t in range(TT):
                sp.wait_ge(s_fo, t + 1)
                sp.dma_start(out_v[:, t, :], fo[:, t % 2, :]).then_inc(s_out[t % 2], 16)
            for i in range(2):
                sp.wait_ge(s_out[i], 16 * TT // 2)

        @block.gpsimd
        def _(pool):
            nc.gpsimd.memset(ones[:], 1.0).then_inc(s_const, 1)
            nc.gpsimd.memset(W2[:], 0.0).then_inc(s_w2z, 1)
            pool.wait_ge(s_const, 1)
            nc.gpsimd.affine_select(out=ident[:], in_=ones[:], compare_op=ALU.is_equal, fill=0.0, base=0,
                                    pattern=[[-1, P]], channel_multiplier=1).then_inc(s_const, 1)
            nc.gpsimd.affine_select(out=before[:], in_=ones[:], compare_op=ALU.is_gt, fill=0.0, base=0,
                                    pattern=[[1, P]], channel_multiplier=-1).then_inc(s_const, 1)
            nc.gpsimd.iota(xor[:], pattern=[[1, P]], base=0, channel_multiplier=0).then_inc(s_const, 1)
            nc.gpsimd.iota(mtmp[:].bitcast(I32), pattern=[[0, P]], base=0, channel_multiplier=1).then_inc(s_const, 1)
            nc.gpsimd.iota(pid[:], pattern=[[P, 8]], base=0, channel_multiplier=1,
                           allow_small_or_imprecise_dtypes=True).then_inc(s_const, 1)
            nc.gpsimd.iota(iot[:], pattern=[[1, P]], base=0, channel_multiplier=0,
                           allow_small_or_imprecise_dtypes=True).then_inc(s_const, 1)
            for c in range(CT):
                nc.gpsimd.memset(u_pad[:, c, 0:PAD], 0.0).then_inc(s_pad, 1)
                nc.gpsimd.memset(u_pad[:, c, PAD + S:UW], 0.0).then_inc(s_pad, 1)
            def w_in_lo(c):
                pool.wait_ge(s_dhi, c + 1)
                nc.gpsimd.tensor_tensor(wiL[:, slot_of[c]], ring[:, slot_of[c]], wiH[c % 2][:].bitcast(F),
                                        ALU.subtract).then_inc(s_dlp, 1)

            def w_out_lo(c):
                pool.wait_ge(s_dhi, N_IN + c + 1)
                slot = slot_of[g_out + c]
                nc.gpsimd.tensor_tensor(ringL[:, slot], ring[:, slot], wuH[c % 2][:].bitcast(F), ALU.subtract
                                        ).then_inc(s_dlp, 1)

            def glu_tile(c):
                pool.wait_ge(s_dr["in"], 2 + 8 * (c // 2) + 4 + 2 * (c % 2 + 1))
                uc = u_pad[:, c, PAD:PAD + S]
                nc.gpsimd.tensor_tensor(uc, uc, sig[:], ALU.mult).then_inc(s_u, 1)

            for c in range(N_IN):
                w_in_lo(c)
                if c in (3, 5):
                    glu_tile(c - 3)
                    glu_tile(c - 2)

            pool.wait_ge(s_sr, 1)
            pool.wait_ge(s_dr["in"], 58)
            pool.wait_ge(s_par, 10 * 16)
            nc.gpsimd.tensor_tensor(r_tm[:], r_tm[:], SR[:], ALU.mult).then_inc(s_rg, 1)
            pool.wait_ge(s_rg, 1)
            rg = r_tm[:].rearrange("p w (h c) -> p (w h) c", h=GH)
            nc.gpsimd.tensor_tensor(rg, rg, ngb[:].unsqueeze(1).broadcast_to([P, TT * GH, GDV]), ALU.mult
                                    ).then_inc(s_rg, 1)
            for i in (1, 0):
                pool.wait_ge(s_yh, 2 - i)
                two = slice(2 * i, 2 * i + 2)
                nc.gpsimd.tensor_tensor(yL[:, two, :], yT[:, two, :], yH[i][:].bitcast(F), ALU.subtract
                                        ).then_inc(s_yl, 1)
                if i:
                    w_out_lo(0)
            for c in range(1, 4):
                w_out_lo(c)
            pool.wait_ge(s_mm["o"], 32)
            nc.gpsimd.memset(onesb[:], 1.0).then_inc(s_rmi, 1)
            nc.gpsimd.tensor_copy(beforeb[:], before[:]).then_inc(s_rmi, 1)
            pool.wait_ge(s_bld, 4 * 16)
            b0, b1, b2 = (slice(E * i, E * (i + 1)) for i in range(3))
            bp = 0

            def part(ins):
                nonlocal bp
                bp += 1
                ins.then_inc(s_bup, 1)
                pool.wait_ge(s_bup, bp)

            part(nc.gpsimd.memset(bup[:], 0.0))
            part(nc.gpsimd.tensor_copy(bup[0:3 * E, :], bstage[0:3 * E, :]))
            for rows in (b1, b2):
                part(nc.gpsimd.tensor_tensor(bstage[rows, :], bstage[rows, :], bup[rows, :], ALU.subtract))
            for rows in (b1, b2):
                part(nc.gpsimd.tensor_copy(bup[rows, :], bstage[rows, :]))
            part(nc.gpsimd.tensor_tensor(bstage[b2, :], bstage[b2, :], bup[b2, :], ALU.subtract))
            part(nc.gpsimd.tensor_copy(bup[b2, :], bstage[b2, :]))

            pool.wait_ge(s_rt, 1)
            nc.gpsimd.iota(pmi[:], pattern=[[0, 2]], base=0, channel_multiplier=1).then_inc(s_rmi, 1)

            def index_columns(t):
                b0 = pool.value_load(VT[0:1, 1, bass.ds(t, 1)], min_val=0, max_val=NBLK - 1)
                nc.gpsimd.tensor_copy(idxc[:], TM[:, bass.ds(b0, 2)]).then_inc(s_idx, 1)
                pool.wait_ge(s_idx, t + 1)

            def gather():
                for b in range(2):
                    nc.gpsimd.indirect_dma_start(xs[:, b, :], None, h3_dram,
                                                 bass.IndirectOffsetOnAxis(ap=idxc[:, b:b + 1], axis=0)
                                                 ).then_inc(s_xsl, 16)

            def lo_by_pool(t, c):
                pool.wait_ge(s_whi, 12 * t + c - 3)
                nc.gpsimd.tensor_tensor(wlo[:, chunk_slot(c, NSPL), :], raw[:, chunk_slot(c, NRAW), :],
                                        whi[:, chunk_slot(c, NSPL), :].bitcast(F), ALU.subtract
                                        ).then_inc(s_wlp, 1)

            pool.wait_ge(s_tab, 1)
            pool.wait_ge(s_h3s, 16 * TT)
            used_ = pool.value_load(usedb[0:1, 0:1], min_val=1, max_val=NVIS)
            nc.gpsimd.memset(yb[:], 0.0).then_inc(s_yst, 1)
            index_columns(0)
            gather()
            lo_by_pool(0, 6)
            pool.wait_ge(s_xt, 1)
            index_columns(1)
            gather()
            lo_by_pool(0, 9)
            pool.wait_ge(s_xt, 2)
            index_columns(2)
            lo_by_pool(1, 0)
            gather()
            with pool.Fori(1, NVIS + 1) as t:
                with pool.If(t <= used_):
                    for c in (3, 6, 9):
                        lo_by_pool(t, c)
                    pool.wait_ge(s_xt, t + 2)
                    index_columns(t + 2)
                    lo_by_pool(t + 1, 0)
                    gather()
            pool.wait_ge(s_yst, 16 * used_ + 1)
            wait_lo(pool, used_ + 1, 0)
            wait_lo(pool, used_ + 1, 2)
            nc.gpsimd.tensor_tensor(pmod[:, 0:1], pmod[:, 0:1], pmod[:, 1:2], ALU.mult)
            for i in range(TT * TOPK):
                if i >= 8:
                    pool.wait_ge(s_ac, i - 7)
                nc.gpsimd.indirect_dma_start(yg[:, i % 8, :], None, ys_dram[0:NBLK * P, :],
                                             bass.IndirectOffsetOnAxis(ap=rowof[:, i:i + 1], axis=0)
                                             ).then_inc(s_yg[i % 8], 16)

        @block.scalar
        def _(act):
            act.wait_ge(s_w2z, 1)
            act.dma_start(gmb[:], A["norm_mix_g"][0].partition_broadcast(P)).then_inc(s_gmb, 16)
            act.dma_start(W2[0:RANK, 0, :], A["gate_w2_fwd"][0]).then_inc(s_par, 16)
            act.dma_start(W2[RANK:2 * RANK, 1, :], A["gate_w2_bwd"][0]).then_inc(s_par, 16)
            for row, name, n in ((GM, "norm_mem_g", 8),
                                 (ZB, "gate_b_fwd", 2), (ZB + 2, "gate_b_bwd", 2), (CB, "conv_b", 4),
                                 (LG_, "conv_ln_g", 4), (LB, "conv_ln_b", 4)):
                act.dma_start(PVr[row:row + n, :], A[name][0].rearrange("(k p) -> k p", p=P)).then_inc(s_par, 16)
            act.dma_start(CWr[:], A["conv_w"][0].rearrange("j (c p) -> (j c) p", p=P)).then_inc(s_par, 16)
            act.dma_start(ngb[:], A["gla_norm_g"][0].partition_broadcast(P)).then_inc(s_par, 16)

            def norm_stats(n, src, tiles):
                N = norms[n]
                for t in range(tiles):
                    if n == "m":
                        act.wait_ge(N["loaded"], 16)
                    elif n == "x":
                        act.wait_ge(s_xld[t // 2], 16)
                    elif n == "y":
                        act.wait_ge(s_dr["out"], 24 + t + 1)
                    else:
                        act.wait_ge(s_dr["o"], 24 + t + 1)
                    if t:
                        act.wait_ge(N["stats_by_scalar"], t)
                    nc.scalar.activation(sig[:], src[:, t, :], ACT.Square,
                                         accum_out=st8[:, 0, t:t + 1]).then_inc(N["stats_by_scalar"], 1)
                act.wait_ge(N["stats_by_vector"], 1)
                nc.scalar.activation(st8[:, 2, 0:tiles], st8[:, 1, 0:tiles], ACT.Sqrt).then_inc(N["stats_by_scalar"], 1)

            norm_stats("m", mem_tm, MT)
            act.wait_ge(norms["m"]["stats_by_vector"], 2)
            act.wait_ge(norms["m"]["scaled"], MT)
            norm_stats("x", xres, TT)

            def drain(seg, n):
                act.wait_ge(s_mm[seg], n + 1)
                return s_dr[seg]

            def drain_memory(groups):
                for n in groups:
                    d = drain("mem", n)
                    dst = kx[:, n, :] if n < 8 else vx[:, n % 2, 256 * ((n - 8) // 2):256 * ((n - 8) // 2 + 1)]
                    nc.scalar.copy(dst, PS[:, 4 + n % 4, 0:256]).then_inc(d, 1)

            for n in range(2 * TT):
                t, b = n // 2, n % 2
                act.wait_ge(norms["x"]["turned"], n + 1)
                nc.scalar.copy(xH[:, 4 * b:4 * b + 4, P * t:P * (t + 1)],
                               PS[:, 2 * (t % 4) + b, :].rearrange("p (k c) -> p k c", k=4)).then_inc(s_xh, 1)

            def split_w_in(c):
                act.wait_ge(s_ring[slot_of[c]], 16 * fills[c])
                if c >= 2:
                    act.wait_ge(s_mm["in"], used[c - 2][1])
                nc.scalar.copy(wiH[c % 2][:], ring[:, slot_of[c]]).then_inc(s_dhi, 1)

            def next_split():
                for c in range(N_IN - 2):
                    if used[c][1] == n:
                        split_w_in(c + 2)

            split_w_in(0)
            split_w_in(1)
            n = 0
            for th in range(2):
                d = drain("in", n)
                if n == 0:
                    act.wait_ge(norms["x"]["turned"], 2 * TT)
                nc.scalar.copy(gT[:, 512 * th:512 * (th + 1)], PS[0:2 * RANK, n % 8, :]).then_inc(d, 1)
                n += 1
                next_split()
            for c2 in range(2):
                for ft in range(2):
                    for th in range(2):
                        d = drain("in", n)
                        nc.scalar.copy(u_pad[:, 2 * c2 + ft, PAD + 512 * th:PAD + 512 * (th + 1)],
                                       bank_groups(n)).then_inc(d, 1)
                        n += 1
                        next_split()
                for ft in range(2):
                    for th in range(2):
                        d = drain("in", n)
                        c = 2 * c2 + ft
                        if th == 0 and c:
                            act.wait_ge(s_u, c)
                        nc.scalar.activation(sig[:, 512 * th:512 * (th + 1)], bank_groups(n),
                                             ACT.Sigmoid).then_inc(d, 1)
                        n += 1
                        next_split()
            for dst, sc in ((qT, GDK ** -0.5), (kT, 1.0)):
                for ft in range(2):
                    for th in range(2):
                        d = drain("in", n)
                        if n == 18:
                            act.wait_ge(norms["x"]["scaled"], TT)
                        nc.scalar.mul(dst[:, ft, 512 * th:512 * (th + 1)], bank_groups(n), sc).then_inc(d, 1)
                        n += 1
                        next_split()
            for dst in (v_tm, r_tm):
                for c2 in range(2):
                    for t in range(TT):
                        d = drain("in", n)
                        cols = slice(256 * c2, 256 * (c2 + 1))
                        nc.scalar.copy(dst[:, t, cols], bank_groups(n, 256)).then_inc(d, 1)
                        n += 1
                        next_split()

            for c in range(CT):
                act.wait_ge(s_lnv, 2 * (c + 1))
                if c == 0:
                    act.wait_ge(s_mm["in"], 58)
                nc.scalar.activation(o_gla[:, 2 * c:2 * c + 2, :], yT[:, c, :].rearrange("p (a b) -> p a b", a=2),
                                     ACT.Square).then_inc(s_lna, 1)
            act.wait_ge(s_lnv, 10)
            nc.scalar.activation(sig[:], sig[:], ACT.Sqrt).then_inc(s_lna, 1)
            for c in range(CT):
                act.wait_ge(s_lnv, 12 + c)
                act.wait_ge(s_lnp, 4)
                nc.scalar.activation(o_gla[:, 2 * c:2 * c + 2, :], yT[:, c, :].rearrange("p (a b) -> p a b", a=2),
                                     ACT.Identity, bias=PV[:, LB + c:LB + c + 1],
                                     scale=PV[:, LG_ + c:LG_ + c + 1]).then_inc(s_lna, 1)
            for c in range(CT):
                act.wait_ge(s_lna, 6 + c)
                nc.scalar.activation(yT[:, c, :], yT[:, c, :], ACT.Sigmoid, bias=PV[:, LB + c:LB + c + 1],
                                     scale=PV[:, LG_ + c:LG_ + c + 1]).then_inc(s_lna, 1)

            def split_w_out(c):
                g = g_out + c
                act.wait_ge(s_ring[slot_of[g]], 16 * fills[g])
                if c == 1:
                    act.wait_ge(s_ov, 6)
                if c >= 2:
                    act.wait_ge(s_mm["out"], TT * (c - 1))
                nc.scalar.copy(wuH[c % 2][:], ring[:, slot_of[g]]).then_inc(s_dhi, 1)

            def split_y(i):
                nc.scalar.copy(yH[i][:], yT[:, 2 * i:2 * i + 2, :]).then_inc(s_yh, 1)

            for p in range(2):
                for n in range(4):
                    d, th = n // 2, n % 2
                    act.wait_ge(s_z, 4 * p + n + 1)
                    nc.scalar.activation(KQ[:, d, 512 * th:512 * (th + 1)], PS[:, n, :], ACT.Abs,
                                         bias=PV[:, ZB + 2 * d + p:ZB + 2 * d + p + 1]).then_inc(s_zabs, 1)
                act.wait_ge(s_zabs, 4 * (p + 1))
                nc.scalar.activation(KQ[:], KQ[:], ACT.Exp, scale=-1.0).then_inc(s_zln, 1)
                act.wait_ge(s_zln, 2 * p + 1)
                nc.scalar.activation(KQ[:], KQ[:], ACT.Ln, bias=1.0).then_inc(s_zln, 1)
                drain_memory(range(8 * p, 8 * p + 4))
                if p == 0:
                    nc.scalar.activation(SR[:], r_tm[:], ACT.Sigmoid).then_inc(s_sr, 1)
                act.wait_ge(s_tot, 2 * (p + 1))
                nc.scalar.activation(TTd[:, 1], TTd[:, 0], ACT.Exp, scale=1.0 / TAU).then_inc(s_dec, 1)
                for l in range(8):
                    act.wait_ge(s_sub, 8 * p + l + 1)
                    nc.scalar.activation(EX[:], EX[:], ACT.Exp, scale=1.0 / TAU).then_inc(s_ex, 1)
                    if l == 0:
                        drain_memory(range(8 * p + 4, 8 * p + 8))
                    if l == 7:
                        for b in range(4):
                            act.wait_ge(s_ket, 4 * p + b + 1)
                            nc.scalar.copy(KEt[:, b, :], PS[:, b, :]).then_inc(s_kev, 1)
                act.wait_ge(s_U, 14 * (p + 1))
                nc.scalar.activation(EX[:, 0, :], Bf[:], ACT.Exp, scale=1.0 / TAU)
                nc.scalar.activation(EX[:, 1, :], Rb[:], ACT.Exp, scale=1.0 / TAU).then_inc(s_ex, 1)
                if p:
                    act.wait_ge(s_lnv, 19)
                    split_y(1)
                    split_w_out(0)
                for n in range(16):
                    act.wait_ge(s_op, 16 * p + n + 1)
                    w, hh = n // 2, n % 2
                    h = 2 * p + hh
                    nc.scalar.activation(sig[:, P * (n % 8):P * (n % 8 + 1)], PS[:, n % 4, 0:P], ACT.Square,
                                         accum_out=st8[:, 0, GH * w + h:GH * w + h + 1]).then_inc(s_osq, 1)
                    nc.scalar.copy(o_gla[:, w, GDV * h:GDV * (h + 1)], PS[:, n % 4, 0:P]).then_inc(s_oe, 1)
            act.wait_ge(s_ov, 1)
            nc.scalar.activation(st8[:, 2, :], st8[:, 1, :], ACT.Sqrt).then_inc(s_oa, 1)
            split_y(0)
            for b in range(2):
                for c in range(CT):
                    n = 2 * c + b
                    act.wait_ge(s_at, CT * b + c + 1)
                    nc.scalar.copy(aH[:, c, 512 * b:512 * (b + 1)], PS[:, n, :]).then_inc(s_ae, 1)
            for c in range(1, 4):
                split_w_out(c)
            act.wait_ge(s_mm["mem"], 16)
            act.dma_start(gxb[:], A["norm_xattn_g"][0].partition_broadcast(P)).then_inc(s_gxb, 16)
            g_q = len(chunks) - 8

            def split_wq(c):
                act.wait_ge(s_ring[slot_of[g_q + c]], 16 * fills[g_q + c])
                if c == 1:
                    act.wait_ge(norms["y"]["turned"], 2 * TT)
                if c >= 2:
                    act.wait_ge(s_mm["q"], 4 * (c - 1))
                nc.scalar.copy(wqH[c % 2][:], ring[:, slot_of[g_q + c]]).then_inc(s_dhi, 1)

            act.wait_ge(s_mm["out"], 3 * TT)
            split_wq(0)
            norm_stats("y", xres, TT)
            for n in range(2 * TT):
                t, b = n // 2, n % 2
                act.wait_ge(norms["y"]["turned"], n + 1)
                nc.scalar.copy(hH[:, 4 * b:4 * b + 4, P * t:P * (t + 1)],
                               PS[:, 2 * (t % 4) + b, :].rearrange("p (k c) -> p k c", k=4)).then_inc(s_hh, 1)
            split_wq(1)
            for n in range(16):
                d = drain("q", n)
                nc.scalar.copy(qxT[:, n // 2, 512 * (n % 2):512 * (n % 2 + 1)], bank_groups(n)).then_inc(d, 1)
                if n in (3, 7):
                    split_wq(n // 4 + 2)
            def xprob_drain(h, t):
                i = TT * h + t
                act.wait_ge(s_pt, i + 1)
                nc.scalar.copy(pT[:, h % 2, :, P * t:P * (t + 1)],
                               PS[:, 3, 0:256].rearrange("p (m c) -> p m c", m=MT)).then_inc(s_pc, 1)

            g_o = len(chunks) - 4

            def split_wo(c):
                act.wait_ge(s_ring[slot_of[g_o + c]], 16 * fills[g_o + c])
                if c >= 2:
                    act.wait_ge(s_mm["o"], TT * (c - 1))
                nc.scalar.copy(woH[c % 2][:], ring[:, slot_of[g_o + c]]).then_inc(s_dhi, 1)

            split_wo(0)
            for h in range(XH):
                for t in range(TT):
                    n = TT * h + t
                    act.wait_ge(s_sv, scaled_max(n))
                    if n >= 4:
                        act.wait_ge(s_pt, n - 3)
                    nc.scalar.activation(pr[:, n % 4, :], score_bank(n), ACT.Exp, bias=smx[:, n % 4, 1:2],
                                         scale=XDH ** -0.5, accum_out=smx[:, n % 4, 2:3]).then_inc(s_pe, 1)
                    if t >= 2:
                        xprob_drain(h, t - 2)
                xprob_drain(h, TT - 2)
                xprob_drain(h, TT - 1)
                for b in range(4):
                    m = 4 * h + b
                    act.wait_ge(s_av, m + 1)
                    nc.scalar.copy(oxH[:, 2 * h + b // 2, 512 * (b % 2):512 * (b % 2 + 1)],
                                   PS[:, 4 + b, :]).then_inc(s_ax, 1)
            for c in range(1, 4):
                split_wo(c)
            act.wait_ge(s_mm["o"], 24)
            act.dma_start(gfb[:], A["norm_ffn_g"][0].partition_broadcast(P)).then_inc(s_rpar, 16)
            act.dma_start(rw[:], A["router_w"][0].rearrange("(k p) e -> p k e", p=P)).then_inc(s_rpar, 16)
            act.dma_start(rbb[:], A["router_b"][0].partition_broadcast(P)).then_inc(s_rpar, 16)
            norm_stats("z", xres, TT)
            act.wait_ge(s_mm["o"], 32)
            act.dma_start(bdn[:], A["exp_b_down"][0]).then_inc(s_bld, 16)
            for i in range(3):
                act.dma_start(bstage[E * i:E * (i + 1), :], A["exp_b_up"][0]).then_inc(s_bld, 16)
            for t in range(TT):
                for b in range(2):
                    act.wait_ge(norms["z"]["turned"], 2 * t + b + 1)
                    if t >= 2:
                        act.wait_ge(s_lgp, t - 1)
                    nc.scalar.copy(h3T[:, t % 2, 4 * b:4 * b + 4, :].rearrange("p k c -> p (k c)"),
                                   PS[:, 2 * (t % 2) + b, :]).then_inc(s_h3e, 1)
            act.wait_ge(s_rt, 2)
            nc.scalar.activation(Gt[:], Gt[:], ACT.Exp).then_inc(s_gx, 1)
            for b in range(2):
                act.wait_ge(s_gdt, b + 1)
                nc.scalar.copy(GDT[:, 512 * b:512 * (b + 1)], PS[0:E, b, :]).then_inc(s_gde, 1)

            def split_hi(t, c, first=False):
                wait_raw(act, t, c)
                if not first:
                    wait_multiplied(act, t, c - NSPL)
                nc.scalar.copy(whi[:, chunk_slot(c, NSPL), :], raw[:, chunk_slot(c, NRAW), :]).then_inc(s_whi, 1)

            def two_blocks(t):
                return act.value_load(VT[0:1, 2, bass.ds(t, 1)], min_val=0, max_val=1)

            def turned_hi(turned, t, hi, blocks, done):
                act.wait_ge(turned, t + 1)
                for b in range(blocks):
                    for i in range(2):
                        ins = nc.scalar.copy(hi[:, b, 4 * i:4 * i + 4, :].rearrange("p k c -> p (k c)"),
                                             PS[:, 4 + 2 * b + i, :])
                ins.then_inc(done, 1)

            def tokens_hi(t):
                both = two_blocks(t)
                with act.If(both >= 1):
                    turned_hi(s_xt, t, xhi, 2, s_xhi)
                with act.Else():
                    turned_hi(s_xt, t, xhi, 1, s_xhi)

            def hidden_hi(t, both):
                with act.If(both >= 1):
                    turned_hi(s_ht, t, hhi, 2, s_hhi)
                with act.Else():
                    turned_hi(s_ht, t, hhi, 1, s_hhi)

            def expert_sigmoid(t, i, both):
                def one(blocks):
                    act.wait_ge(s_g, 2 * t + i + 1)
                    nc.scalar.activation(sgm[:, 0:blocks, :], glu[:, 0:blocks, :], ACT.Sigmoid, scale=ALPHA
                                         ).then_inc(s_sg, 1)
                with act.If(both >= 1):
                    one(2)
                with act.Else():
                    one(1)

            def drain_rows(t, i, both):
                def one(blocks):
                    wait_multiplied(act, t, 9 + 2 * i)
                    act.wait_ge(s_yst, 16 * t - 15)
                    for b in range(blocks):
                        ins = nc.scalar.copy(yb[:, b, 512 * i:512 * (i + 1)], PS[:, 2 * i + b, :])
                    ins.then_inc(s_yev, 1)
                with act.If(both >= 1):
                    one(2)
                with act.Else():
                    one(1)

            def store_rows(t):
                b0 = act.value_load(VT[0:1, 1, bass.ds(t, 1)], min_val=0, max_val=NBLK - 1)
                act.dma_start(ys_dram[bass.ds(b0 * P, 2 * P), :].rearrange("(b p) d -> p b d", p=P), yb[:]
                              ).then_inc(s_yst, 16)

            act.wait_ge(s_tab, 1)
            used_ = act.value_load(usedb[0:1, 0:1], min_val=1, max_val=NVIS)
            nc.scalar.copy(smx[:, 0, 0:1], st8[:, 0, 0:1]).then_inc(s_yev, 1)
            nc.scalar.copy(smx[:, 0, 1:2], st8[:, 0, 0:1]).then_inc(s_yev, 1)
            tokens_hi(0)
            both0 = two_blocks(0)
            for c in range(4, 9):
                split_hi(0, c, first=c < 4 + NSPL)
            expert_sigmoid(0, 0, both0)
            for c in (9, 10, 11):
                split_hi(0, c)
            split_hi(1, 0)
            expert_sigmoid(0, 1, both0)
            split_hi(1, 1)
            split_hi(1, 2)
            tokens_hi(1)
            hidden_hi(0, both0)
            with act.Fori(1, NVIS + 1) as t:
                with act.If(t <= used_):
                    both, both_last = two_blocks(t), two_blocks(t - 1)
                    split_hi(t, 3)
                    split_hi(t, 4)
                    split_hi(t, 5)
                    expert_sigmoid(t, 0, both)
                    split_hi(t, 6)
                    split_hi(t, 7)
                    split_hi(t, 8)
                    split_hi(t, 9)
                    expert_sigmoid(t, 1, both)
                    split_hi(t, 10)
                    split_hi(t, 11)
                    tokens_hi(t + 1)
                    split_hi(t + 1, 0)
                    drain_rows(t, 0, both_last)
                    split_hi(t + 1, 1)
                    drain_rows(t, 1, both_last)
                    hidden_hi(t, both)
                    split_hi(t + 1, 2)
                    act.wait_ge(s_yev, 2 * t + 2)
                    store_rows(t - 1)
            for t in range(TT):
                act.wait_ge(s_ac, TOPK * (t + 1))
                nc.scalar.activation(sqs[:], xres[:, t, :], ACT.Square, accum_out=st8[:, 0, t:t + 1]
                                     ).then_inc(s_fa, 1)
                act.wait_ge(s_fv, 2 * t + 1)
                nc.scalar.activation(st8[:, 2, t:t + 1], st8[:, 1, t:t + 1], ACT.Sqrt).then_inc(s_fa, 1)

        @block.vector
        def _(dve):
            dve.wait_ge(s_const, 5)
            nc.vector.tensor_tensor(xor[:], xor[:], mtmp[:].bitcast(I32), ALU.bitwise_xor).then_inc(s_mask, 1)
            for l, s in enumerate(LEVELS):
                dve.wait_ge(s_mask, 2 * l + 1)
                nc.vector.tensor_scalar(mtmp[:], xor[:], float(2 * s), None, ALU.is_lt).then_inc(s_mask, 1)
                dve.wait_ge(s_mask, 2 * l + 2)
                nc.vector.scalar_tensor_tensor(out=masks[:, l, :], in0=xor[:], scalar=float(s), in1=mtmp[:],
                                               op0=ALU.is_ge, op1=ALU.mult).then_inc(s_mask, 1)
            dve.wait_ge(s_pvt, 2)
            nc.vector.tensor_copy(PV[:, 0:NPV], PS[:, 6, 0:NPV]).then_inc(s_pvc, 1)
            nc.vector.tensor_copy(CWT[:], PS[:, 7, 0:TAPS * CT]).then_inc(s_pvc, 1)
            dve.wait_ge(s_pvc, 2)

            def norm_scale(n, src, tiles, g, dst):
                N = norms[n]
                dve.wait_ge(N["stats_by_scalar"], tiles)
                nc.vector.tensor_scalar(st8[:, 1, 0:tiles], st8[:, 0, 0:tiles], 1.0 / D, RMS_EPS,
                                        ALU.mult, ALU.add).then_inc(N["stats_by_vector"], 1)
                dve.wait_ge(N["stats_by_scalar"], tiles + 1)
                nc.vector.reciprocal(st8[:, 3, 0:tiles], st8[:, 2, 0:tiles]).then_inc(N["stats_by_vector"], 1)
                dve.wait_ge(N["stats_by_vector"], 2)

                def evac(t):
                    for b in range(2):
                        dve.wait_ge(N["turned"], 2 * t + b + 1)
                        bank = 2 * (t % 4) + b
                        nc.vector.tensor_tensor(
                            dst[:, 4 * b:4 * b + 4, P * t:P * (t + 1)],
                            PS[:, bank, :].rearrange("p (k c) -> p k c", k=4),
                            PV[:, g + 4 * b:g + 4 * b + 4].unsqueeze(2).broadcast_to([P, 4, P]),
                            ALU.mult).then_inc(N["drained"], 1)

                for t in range(tiles):
                    if t >= 2:
                        dve.wait_ge(N["turned"], 2 * (t - 1))
                    nc.vector.tensor_scalar(XN[:, t % 2, :], src[:, t, :], st8[:, 3, t:t + 1], None,
                                            ALU.mult).then_inc(N["scaled"], 1)
                    if t >= 1:
                        evac(t - 1)
                evac(tiles - 1)

            def split_norm(n, gain, gain_loaded, low_part):
                N = norms[n]
                dve.wait_ge(N["stats_by_scalar"], TT)
                nc.vector.tensor_scalar(st8[:, 1, 0:TT], st8[:, 0, 0:TT], 1.0 / D, RMS_EPS, ALU.mult, ALU.add
                                        ).then_inc(N["stats_by_vector"], 1)
                dve.wait_ge(N["stats_by_scalar"], TT + 1)
                nc.vector.reciprocal(st8[:, 3, 0:TT], st8[:, 2, 0:TT]).then_inc(N["stats_by_vector"], 1)
                dve.wait_ge(N["stats_by_vector"], 2)
                dve.wait_ge(gain_loaded, 16)
                for t in range(TT):
                    if t >= 2:
                        dve.wait_ge(N["turned"], 2 * (t - 1))
                    nc.vector.scalar_tensor_tensor(out=XN[:, t % 2, :], in0=xres[:, t, :],
                                                   scalar=st8[:, 3, t:t + 1], in1=gain[:], op0=ALU.mult,
                                                   op1=ALU.mult).then_inc(N["scaled"], 1)
                    if t:
                        low_part(t - 1)
                low_part(TT - 1)

            def x_lo(t):
                cols = slice(P * t, P * (t + 1))
                for b in range(2):
                    dve.wait_ge(s_xh, 2 * t + b + 1)
                    pieces = ((0, 4),) if b == 0 else ((4, 6), (6, 8))
                    for k0, k1 in pieces:
                        dst = xL[0][:, k0:k1, cols] if k0 < 6 else xL[1][:, :, cols]
                        turned = PS[:, 2 * (t % 4) + b, P * (k0 - 4 * b):P * (k1 - 4 * b)]
                        ins = nc.vector.tensor_tensor(dst, turned.rearrange("p (k c) -> p k c", c=P),
                                                      xH[:, k0:k1, cols].bitcast(F), ALU.subtract)
                    ins.then_inc(norms["x"]["drained"], 1)

            norm_scale("m", mem_tm, MT, GM, mT)
            split_norm("x", gmb, s_gmb, x_lo)

            dve.wait_ge(s_pad, 2 * CT)
            cv = 0
            for c2 in range(2):
                dve.wait_ge(s_u, 2 * c2 + 2)
                for j in range(TAPS):
                    for c in (2 * c2, 2 * c2 + 1):
                        uc = u_pad[:, c, j:j + S]
                        w = CWT[:, j * CT + c:j * CT + c + 1]
                        if j == 0:
                            if c == 0:
                                dve.wait_ge(norms["m"]["scaled"], MT)
                            ins = nc.vector.tensor_scalar(yT[:, c, :], uc, w, PV[:, CB + c:CB + c + 1],
                                                          ALU.mult, ALU.add)
                        else:
                            dve.wait_ge(s_cv, cv - 1)
                            ins = nc.vector.scalar_tensor_tensor(out=yT[:, c, :], in0=uc, scalar=w,
                                                                 in1=yT[:, c, :], op0=ALU.mult, op1=ALU.add)
                        ins.then_inc(s_cv, 1)
                        cv += 1
            for th in range(2):
                dve.wait_ge(s_lnp, th + 1)
            for c in range(CT):
                for th in range(2):
                    yh = yT[:, c, 512 * th:512 * (th + 1)]
                    nc.vector.scalar_tensor_tensor(out=yh, in0=PS[:, th, :], scalar=-1.0 / CW_, in1=yh,
                                                   op0=ALU.mult, op1=ALU.add).then_inc(s_lnv, 1)
            for th in range(2):
                dve.wait_ge(s_lnp, th + 3)
                nc.vector.tensor_scalar(sig[:, 512 * th:512 * (th + 1)], PS[:, 2 + th, :], 1.0 / CW_, LN_EPS,
                                        ALU.mult, ALU.add).then_inc(s_lnv, 1)
            dve.wait_ge(s_lna, 5)
            nc.vector.reciprocal(sig[:], sig[:]).then_inc(s_lnv, 1)
            dve.wait_ge(s_lnv, 11)
            for c in range(CT):
                nc.vector.tensor_tensor(yT[:, c, :], yT[:, c, :], sig[:], ALU.mult).then_inc(s_lnv, 1)
            for c in range(CT):
                dve.wait_ge(s_lna, 10 + c)
                nc.vector.tensor_tensor(yT[:, c, :].rearrange("p (a b) -> p a b", a=2),
                                        yT[:, c, :].rearrange("p (a b) -> p a b", a=2),
                                        o_gla[:, 2 * c:2 * c + 2, :], ALU.mult).then_inc(s_lnv, 1)

            dve.wait_ge(s_par, 10 * 16)
            for p in range(2):
                if p:
                    dve.wait_ge(s_kq, 9 * p)
                for n in range(4):
                    d, th = n // 2, n % 2
                    dve.wait_ge(s_z, 4 * p + n + 1)
                    dve.wait_ge(s_zabs, 4 * p + n + 1)
                    nc.vector.tensor_scalar(EX[:, d, 512 * th:512 * (th + 1)], PS[:, n, :],
                                            PV[:, ZB + 2 * d + p:ZB + 2 * d + p + 1], 0.0,
                                            ALU.add, ALU.min).then_inc(s_zmin, 1)
                dve.wait_ge(s_zmin, 4 * (p + 1))
                dve.wait_ge(s_zln, 2 * (p + 1))
                nc.vector.tensor_tensor(EX[:], EX[:], KQ[:], ALU.subtract).then_inc(s_la, 1)
                dve.wait_ge(s_la, p + 1)
                for d, dst in ((0, Bf), (1, Rb)):
                    for w in range(TT):
                        nc.vector.tensor_tensor_scan(out=dst[:, P * w:P * (w + 1)], data0=ones[:],
                                                     data1=EX[:, d, P * w:P * (w + 1)], initial=0.0,
                                                     op0=ALU.mult, op1=ALU.add).then_inc(s_scan, 1)
                dve.wait_ge(s_scan, 16 * (p + 1))
                wins = lambda ap: ap.rearrange("p (w c) -> p w c", w=TT)
                ends = lambda ap: wins(ap)[:, :, P - 1:P].rearrange("p w c -> p (w c)")
                if p:
                    dve.wait_ge(s_st, 14 * p)
                nc.vector.tensor_copy(TTd[:, 0, 0, :], ends(Bf[:])).then_inc(s_tot, 1)
                nc.vector.tensor_copy(TTd[:, 0, 1, :], ends(Rb[:])).then_inc(s_tot, 1)
                dve.wait_ge(s_tot, 2 * (p + 1))
                nc.vector.tensor_tensor(Rb[:], EX[:, 1, :], Rb[:], ALU.subtract).then_inc(s_rb, 1)
                dve.wait_ge(s_rb, 2 * p + 1)
                tot = lambda d: TTd[:, 0, d, :].unsqueeze(2).broadcast_to([P, TT, P])
                nc.vector.tensor_tensor(wins(Rb[:]), wins(Rb[:]), tot(1), ALU.add).then_inc(s_rb, 1)
                dve.wait_ge(s_rb, 2 * p + 2)

                def exponents(l):
                    s = LEVELS[l]
                    v3 = lambda ap: ap.rearrange("p (g h c) -> p g h c", h=2, c=s)
                    bref = v3(Bf[:])[:, :, 0, s - 1:s].broadcast_to([P, S // (2 * s), s])
                    rref = v3(Rb[:])[:, :, 1, 0:1].broadcast_to([P, S // (2 * s), s])
                    B_, R_, K_, Q_ = v3(Bf[:]), v3(Rb[:]), v3(EX[:, 0, :]), v3(EX[:, 1, :])
                    nc.vector.tensor_tensor(K_[:, :, 0, :], bref, B_[:, :, 0, :], ALU.subtract)
                    nc.vector.tensor_tensor(K_[:, :, 1, :], rref, R_[:, :, 1, :], ALU.subtract)
                    nc.vector.tensor_tensor(Q_[:, :, 0, :], R_[:, :, 0, :], rref, ALU.subtract)
                    nc.vector.tensor_tensor(Q_[:, :, 1, :], B_[:, :, 1, :], bref, ALU.subtract).then_inc(s_sub, 1)

                def select(l):
                    for b in range(4):
                        hh, half = b // 2, b % 2
                        L = 8 * p + l
                        dve.wait_ge(s_gram, 4 * L + b + 1)
                        if l and b == 0:
                            dve.wait_ge(s_sel, 4 * L)
                        scores = Ssc[:, hh, 4 * half:4 * half + 4, :]
                        products = PS[:, 4 * (L % 2) + b, :].rearrange("p (w c) -> p w c", w=4)
                        if l == 0:
                            ins = nc.vector.tensor_copy(scores, products)
                        else:
                            ins = nc.vector.copy_predicated(
                                scores, masks[:, l - 1:l, :].broadcast_to([P, 4, P]), products)
                        ins.then_inc(s_sel, 1)

                exponents(0)
                dve.wait_ge(s_rg, 1)
                for l in range(7):
                    dve.wait_ge(s_ex, 9 * p + l + 1)
                    if l >= 2:
                        dve.wait_ge(s_gram, 32 * p + 4 * l)
                    dst = (KQ, KQ2)[l % 2]
                    nc.vector.tensor_tensor(dst[:, 0, :], EX[:, 0, :], kT[:, p, :], ALU.mult)
                    nc.vector.tensor_tensor(dst[:, 1, :], EX[:, 1, :], qT[:, p, :], ALU.mult).then_inc(s_kq, 1)
                    dve.wait_ge(s_kq, 9 * p + l + 1)
                    if l < 6:
                        exponents(l + 1)
                    else:
                        nc.vector.tensor_tensor(wins(EX[:, 0, :]), tot(0), wins(Bf[:]), ALU.subtract)
                        nc.vector.tensor_tensor(wins(EX[:, 1, :]), tot(1), wins(Rb[:]),
                                                ALU.subtract).then_inc(s_sub, 1)
                    select(l)
                dve.wait_ge(s_ex, 9 * p + 8)
                nc.vector.tensor_tensor(KQ2[:, 0, :], EX[:, 0, :], kT[:, p, :], ALU.mult)
                nc.vector.tensor_tensor(KQ2[:, 1, :], EX[:, 1, :], kT[:, p, :], ALU.mult).then_inc(s_kq, 1)
                select(7)
                nc.vector.memset(ST[:, 0, 0, :], 0.0).then_inc(s_st0, 1)
                nc.vector.memset(ST[:, 1, TT - 1, :], 0.0).then_inc(s_st0, 1)
                dve.wait_ge(s_st0, 2 * (p + 1))
                dve.wait_ge(s_dec, p + 1)
                for n in range(14):
                    d = n % 2
                    w = n // 2 if d == 0 else TT - 1 - n // 2
                    to = w + 1 if d == 0 else w - 1
                    dve.wait_ge(s_U, 14 * p + n + 1)
                    if n >= 2:
                        dve.wait_ge(s_st, 14 * p + n - 1)
                    for hh in range(2):
                        a, b = GDK * hh, GDK * (hh + 1)
                        ins = nc.vector.scalar_tensor_tensor(
                            out=ST[a:b, d, to, :], in0=ST[a:b, d, w, :], scalar=TTd[a:b, 1, d, w:w + 1],
                            in1=PS[a:b, 4 + n % 4, P * hh:P * (hh + 1)], op0=ALU.mult, op1=ALU.add)
                    ins.then_inc(s_st, 1)
                dve.wait_ge(s_ex, 9 * p + 9)
                nc.vector.tensor_tensor(KQ[:, 0, :], EX[:, 0, :], qT[:, p, :], ALU.mult)
                nc.vector.tensor_tensor(KQ[:, 1, :], EX[:, 1, :], qT[:, p, :], ALU.mult).then_inc(s_kq, 1)
            og = o_gla[:].rearrange("p w (h c) -> p (w h) c", h=GH)
            dve.wait_ge(s_oe, 32)
            dve.wait_ge(s_osq, 32)
            nc.vector.tensor_scalar(st8[:, 1, :], st8[:, 0, :], 1.0 / GDV, RMS_EPS, ALU.mult, ALU.add
                                    ).then_inc(s_ov, 1)
            dve.wait_ge(s_oa, 1)
            nc.vector.reciprocal(st8[:, 3, :], st8[:, 2, :]).then_inc(s_ov, 1)
            dve.wait_ge(s_ov, 2)
            dve.wait_ge(s_rg, 2)
            rg = r_tm[:].rearrange("p w (h c) -> p (w h) c", h=GH)
            half = TT * GH // 2
            for b in range(2):
                hs = slice(half * b, half * (b + 1))
                nc.vector.tensor_tensor(og[:, hs], og[:, hs], st8[:, 3, hs].unsqueeze(2).broadcast_to([P, half, P]),
                                        ALU.mult).then_inc(s_ov, 1)
                dve.wait_ge(s_ov, 3 + 2 * b)
                nc.vector.tensor_tensor(og[:, hs], og[:, hs], rg[:, hs], ALU.mult).then_inc(s_ov, 1)

            def add_residual(seg, then=lambda c: None):
                for c in range(4):
                    for t in range(TT):
                        n = TT * c + t
                        dve.wait_ge(s_mm[seg], n + 1)
                        xs = xres[:, t, 256 * c:256 * (c + 1)]
                        nc.vector.tensor_tensor(xs, xs, bank_groups(n, 256), ALU.add).then_inc(s_dr[seg], 1)
                    then(c)

            for b in range(2):
                for c in range(CT):
                    dve.wait_ge(s_ae, CT * b + c + 1)
                    cols = slice(512 * b, 512 * (b + 1))
                    nc.vector.tensor_tensor(aL[:, c, cols], PS[:, 2 * c + b, :], aH[:, c, cols].bitcast(F),
                                            ALU.subtract).then_inc(s_al, 1)

            dve.wait_ge(s_xre, 32)
            add_residual("out")
            def wq_lo(c):
                slot = slot_of[len(chunks) - 8 + c]
                dve.wait_ge(s_dhi, N_IN + 4 + c + 1)
                nc.vector.tensor_tensor(ringL[:, slot], ring[:, slot], wqH[c % 2][:].bitcast(F), ALU.subtract
                                        ).then_inc(s_dlv, 1)

            def hidden_states_lo(t):
                for b in range(2):
                    dve.wait_ge(s_hh, 2 * t + b + 1)
                    cols = slice(P * t, P * (t + 1))
                    nc.vector.tensor_tensor(hL[b][:, :, cols],
                                            PS[:, 2 * (t % 4) + b, :].rearrange("p (k c) -> p k c", k=4),
                                            hH[:, 4 * b:4 * b + 4, cols].bitcast(F), ALU.subtract
                                            ).then_inc(norms["y"]["drained"], 1)

            wq_lo(0)
            split_norm("y", gxb, s_gxb, hidden_states_lo)
            for c in range(1, 4):
                wq_lo(c)
            def wo_lo(c):
                dve.wait_ge(s_dhi, N_IN + 8 + c + 1)
                nc.vector.tensor_tensor(woL[c % 2][:], ring[:, slot_of[len(chunks) - 4 + c]], woH[c % 2][:].bitcast(F),
                                        ALU.subtract).then_inc(s_dlv, 1)

            def xout_lo(h):
                for b in range(4):
                    dve.wait_ge(s_ax, 4 * h + b + 1)
                    k, cols = 2 * h + b // 2, slice(512 * (b % 2), 512 * (b % 2 + 1))
                    nc.vector.tensor_tensor(oxL[:, k, cols], PS[:, 4 + b, :], oxH[:, k, cols].bitcast(F),
                                            ALU.subtract).then_inc(s_axl, 1)

            wo_lo(0)
            def normalise(n):
                m = smx[:, n % 4, :]
                dve.wait_ge(s_pe, n + 1)
                nc.vector.reciprocal(m[:, 3:4], m[:, 2:3]).then_inc(s_sv, 1)
                dve.wait_ge(s_sv, normalised(n) - 1)
                nc.vector.tensor_scalar(pr[:, n % 4, :], pr[:, n % 4, :], m[:, 3:4], None,
                                        ALU.mult).then_inc(s_sv, 1)

            for h in range(XH):
                for t in range(TT):
                    n = TT * h + t
                    dve.wait_ge(s_sc, n + 1)
                    if n >= 4:
                        dve.wait_ge(s_sv, normalised(n - 4))
                    m = smx[:, n % 4, :]
                    nc.vector.reduce_max(m[:, 0:1], score_bank(n), X).then_inc(s_sv, 1)
                    dve.wait_ge(s_sv, scaled_max(n) - 1)
                    nc.vector.tensor_scalar(m[:, 1:2], m[:, 0:1], -(XDH ** -0.5), None, ALU.mult).then_inc(s_sv, 1)
                    if t:
                        normalise(n - 1)
                    if t == TT - 1:
                        normalise(n)
                    if h and t == 3:
                        xout_lo(h - 1)
            xout_lo(XH - 1)
            wo_lo(1)
            add_residual("o", lambda c: wo_lo(c + 2) if c < 2 else None)

            N = norms["z"]
            dve.wait_ge(N["stats_by_scalar"], TT)
            nc.vector.tensor_scalar(st8[:, 1, 0:TT], st8[:, 0, 0:TT], 1.0 / D, RMS_EPS, ALU.mult, ALU.add
                                    ).then_inc(N["stats_by_vector"], 1)
            dve.wait_ge(N["stats_by_scalar"], TT + 1)
            nc.vector.reciprocal(st8[:, 3, 0:TT], st8[:, 2, 0:TT]).then_inc(N["stats_by_vector"], 1)
            dve.wait_ge(N["stats_by_vector"], 2)
            dve.wait_ge(s_rpar, 3 * 16)

            def logits(t):
                dve.wait_ge(s_lgp, t + 1)
                nc.vector.tensor_tensor(LG[:, t, :], PS[:, 4 + t % 2, 0:E], rbb[:], ALU.add).then_inc(s_lg, 1)
                dve.wait_ge(s_lg, t + 1)
                nc.vector.max(MX[:, t, :], LG[:, t, :]).then_inc(s_top, 1)
                dve.wait_ge(s_top, 2 * t + 1)
                nc.vector.max_index(IX[:, t, :], MX[:, t, :], LG[:, t, :]).then_inc(s_top, 1)

            for t in range(TT):
                if t == 0:
                    dve.wait_ge(s_mm["o"], 32)
                nc.vector.scalar_tensor_tensor(out=h3[:, t, :], in0=xres[:, t, :], scalar=st8[:, 3, t:t + 1],
                                               in1=gfb[:], op0=ALU.mult, op1=ALU.mult).then_inc(N["scaled"], 1)
                if t >= 2:
                    logits(t - 2)
            logits(TT - 2)
            logits(TT - 1)
            dve.wait_ge(s_top, 2 * TT)

            rt = 0

            def step(ins):
                nonlocal rt
                rt += 1
                ins.then_inc(s_rt, 1)
                dve.wait_ge(s_rt, rt)

            step(nc.vector.tensor_copy(IXf[:], IX[:]))
            step(nc.vector.tensor_tensor(Gt[:], MX[:, :, 0:TOPK], MX[:, :, 0:1].broadcast_to([P, TT, TOPK]),
                                         ALU.subtract))
            for k in range(TOPK):
                step(nc.vector.tensor_tensor(OH[:, :, k, :], iot[:, 0:E].unsqueeze(1).broadcast_to([P, TT, E]),
                                             IXf[:, :, k:k + 1].broadcast_to([P, TT, E]), ALU.is_equal))
            step(nc.vector.tensor_tensor(M[:], OH[:, :, 0, :], OH[:, :, 1, :], ALU.add))
            step(nc.vector.tensor_tensor(M[:], M[:], OH[:, :, 2, :], ALU.add))
            step(nc.vector.tensor_tensor(Mb[:], M[:], OH[:, :, 3, :], ALU.add))
            assert rt == RT_M
            dve.wait_ge(s_gx, 1)
            step(nc.vector.tensor_reduce(gsum[:, 0, :], Gt[:], X, ALU.add))
            step(nc.vector.reciprocal(gsum[:, 1, :], gsum[:, 0, :]))
            step(nc.vector.tensor_tensor(Gt[:], Gt[:], gsum[:, 1, :].unsqueeze(2).broadcast_to([P, TT, TOPK]),
                                         ALU.mult))
            tA = tmpA[:, 0:TT * TOPK * E].rearrange("p (t k e) -> p t k e", t=TT, k=TOPK)
            for k in range(TOPK):
                step(nc.vector.tensor_tensor(tA[:, :, k, :], OH[:, :, k, :],
                                             Gt[:, :, k:k + 1].broadcast_to([P, TT, E]), ALU.mult))
            step(nc.vector.tensor_reduce(GD[:], tA.rearrange("p t k e -> p t e k"), X, ALU.add))
            assert rt == RT_GD
            dve.wait_ge(s_rk, 2)
            nblk, pend, pstb, pst, nvis, vend, vst, first = (ex1[:, i, :] for i in range(8))
            step(nc.vector.tensor_scalar(exi[:, 0, :], PS[:, 7, 0:E], float(P - 1), None, ALU.add))
            step(nc.vector.tensor_scalar(exi[:, 1, :], exi[:, 0, :], 7, None, ALU.arith_shift_right))
            step(nc.vector.tensor_copy(nblk, exi[:, 1, :]))
            step(nc.vector.tensor_tensor_scan(out=pend, data0=ones[:, 0:E], data1=nblk, initial=0.0,
                                              op0=ALU.mult, op1=ALU.add))
            step(nc.vector.tensor_tensor(pstb, pend, nblk, ALU.subtract))
            step(nc.vector.tensor_scalar(pst, pstb, float(P), None, ALU.mult))
            step(nc.vector.tensor_scalar(exi[:, 0, :], exi[:, 1, :], 1.0, None, ALU.add))
            step(nc.vector.tensor_scalar(exi[:, 1, :], exi[:, 0, :], 1, None, ALU.arith_shift_right))
            step(nc.vector.tensor_copy(nvis, exi[:, 1, :]))
            step(nc.vector.tensor_tensor_scan(out=vend, data0=ones[:, 0:E], data1=nvis, initial=0.0,
                                              op0=ALU.mult, op1=ALU.add))
            step(nc.vector.tensor_tensor(vst, vend, nvis, ALU.subtract))
            step(nc.vector.scalar_tensor_tensor(out=first, in0=vst, scalar=-2.0, in1=pstb, op0=ALU.mult,
                                                op1=ALU.add))
            step(nc.vector.tensor_tensor(slot0[:], PS[:, 6, 0:TT * E].rearrange("p (t e) -> p t e", e=E),
                                         pst.unsqueeze(1).broadcast_to([P, TT, E]), ALU.add))
            for k in range(TOPK):
                step(nc.vector.tensor_tensor(tA[:, :, k, :], OH[:, :, k, :], slot0[:], ALU.mult))
            step(nc.vector.tensor_reduce(df[:, 0, :], tA.rearrange("p t k e -> p (t k) e"), X, ALU.add))
            step(nc.vector.tensor_copy(rowof[:], df[:, 0, :]))
            step(nc.vector.tensor_copy(di[:, 0, :], df[:, 0, :]))
            step(nc.vector.tensor_scalar(di[:, 1, :], di[:, 0, :], 7, None, ALU.arith_shift_right))
            step(nc.vector.tensor_scalar(di[:, 2, :], di[:, 0, :], P - 1, None, ALU.bitwise_and))
            step(nc.vector.tensor_copy(df[:, 1:3, :], di[:, 1:3, :]))
            step(nc.vector.tensor_tensor(blkhot[:], iot[:, 0:NB].unsqueeze(1).broadcast_to([P, TT * TOPK, NB]),
                                         df[:, 1, :].unsqueeze(2).broadcast_to([P, TT * TOPK, NB]), ALU.is_equal))
            nc.vector.tensor_tensor(blkhot[:].rearrange("p (t k) b -> p t (k b)", t=TT),
                                    blkhot[:].rearrange("p (t k) b -> p t (k b)", t=TT),
                                    pid[:].unsqueeze(2).broadcast_to([P, TT, TOPK * NB]), ALU.mult
                                    ).then_inc(s_oh, 1)
            for t in range(TT):
                ks = slice(TOPK * t, TOPK * (t + 1))
                if t >= 2:
                    dve.wait_ge(s_tm, t - 1)
                nc.vector.tensor_tensor(rowhot[:, t % 2], iot[:].unsqueeze(1).broadcast_to([P, TOPK, P]),
                                        df[:, 2, ks].unsqueeze(2).broadcast_to([P, TOPK, P]),
                                        ALU.is_equal).then_inc(s_oh, 1)
            tB = tmpA[:, 0:NV * E].rearrange("p (v e) -> p v e", e=E)
            visit = iot[:, 0:NV]
            over_v = lambda ap: ap.unsqueeze(1).broadcast_to([P, NV, E])
            over_e = lambda ap: ap.unsqueeze(2).broadcast_to([P, NV, E])
            ve, vb, vp, v2 = (vt[:, i, :] for i in range(4))
            step(nc.vector.tensor_tensor(tB, over_v(vend), over_e(visit), ALU.is_le))
            step(nc.vector.tensor_reduce(ve, tB, X, ALU.add))
            step(nc.vector.tensor_scalar(ve, ve, float(E - 1), None, ALU.min))
            tC = tmpC[:, 0:NV * E].rearrange("p (v e) -> p v e", e=E)
            step(nc.vector.tensor_tensor(tC, over_v(iot[:, 0:E]), over_e(ve), ALU.is_equal))
            for src, dst_ in ((first, vb), (pend, vp)):
                step(nc.vector.tensor_tensor(tB, tC, over_v(src), ALU.mult))
                step(nc.vector.tensor_reduce(dst_, tB, X, ALU.add))
            step(nc.vector.scalar_tensor_tensor(out=vb, in0=visit, scalar=2.0, in1=vb, op0=ALU.mult, op1=ALU.add))
            step(nc.vector.scalar_tensor_tensor(out=v2, in0=vb, scalar=1.0, in1=vp, op0=ALU.add, op1=ALU.is_lt))
            step(nc.vector.tensor_scalar(vb, vb, float(NBLK - 1), None, ALU.min))
            step(nc.vector.tensor_copy(VT[:, 0:2, :], vt[:, 0:2, :]))
            step(nc.vector.tensor_copy(VT[:, 2, :], v2))
            step(nc.vector.tensor_copy(usedb[:], vend[:, E - 1:E]))
            dve.wait_ge(s_rmi, 3)
            step(nc.vector.tensor_scalar(pmi[:, 0:1], pmi[:, 0:1], E - 1, None, ALU.bitwise_and))
            step(nc.vector.tensor_copy(pmod[:, 0:1], pmi[:, 0:1]))
            step(nc.vector.tensor_scalar(EB[:], ve, pmod[:, 0:1], None, ALU.is_equal))
            dve.wait_ge(s_tm, TT)
            step(nc.vector.tensor_copy(TM[:], PS[:, 4, 0:NB]))

            def bias_selector(t):
                nc.vector.tensor_scalar(SEL[:], ones[:], EB[:, bass.ds(t, 1)], None, ALU.mult).then_inc(s_bsel, 1)

            nc.vector.tensor_copy(pmod[:, 1:2], pmod[:, 0:1]).then_inc(s_tab, 1)
            for t in range(TT):
                for b in range(2):
                    n = 2 * t + b
                    dve.wait_ge(s_bd, n + 1)
                    xh = xres[:, t, 512 * b:512 * (b + 1)]
                    nc.vector.tensor_tensor(xh, xh, PS[:, n % 4, :], ALU.add).then_inc(s_bdr, 1)
            dve.wait_ge(s_bdr, 2 * TT)

            def lo_by_vector(t, c):
                dve.wait_ge(s_whi, 12 * t + c - 3)
                nc.vector.tensor_tensor(wlo[:, chunk_slot(c, NSPL), :], raw[:, chunk_slot(c, NRAW), :],
                                        whi[:, chunk_slot(c, NSPL), :].bitcast(F), ALU.subtract
                                        ).then_inc(s_wlv, 1)

            def two_blocks(t):
                return dve.value_load(VT[0:1, 2, bass.ds(t, 1)], min_val=0, max_val=1)

            def turned_lo(t, split, hi, lo, blocks, done):
                dve.wait_ge(split, t + 1)
                flat = lambda ap, b, i: ap[:, b, 4 * i:4 * i + 4, :].rearrange("p k c -> p (k c)")
                for b in range(blocks):
                    for i in range(2):
                        ins = nc.vector.tensor_tensor(flat(lo, b, i), PS[:, 4 + 2 * b + i, :],
                                                      flat(hi, b, i).bitcast(F), ALU.subtract)
                ins.then_inc(done, 1)

            def tokens_lo(t):
                both = two_blocks(t)
                with dve.If(both >= 1):
                    turned_lo(t, s_xhi, xhi, xlo, 2, s_xlo)
                with dve.Else():
                    turned_lo(t, s_xhi, xhi, xlo, 1, s_xlo)

            def hidden_lo(t, both):
                with dve.If(both >= 1):
                    turned_lo(t, s_hhi, hhi, hlo, 2, s_hlo)
                with dve.Else():
                    turned_lo(t, s_hhi, hhi, hlo, 1, s_hlo)

            def clamp_glu(t, c, i, both, first=False):
                def one(blocks):
                    wait_multiplied(dve, t, c)
                    if not first:
                        dve.wait_ge(s_hid, 4 * t + 2 * i)
                    for b in range(blocks):
                        ins = nc.vector.tensor_scalar(glu[:, b, :], PS[:, b, :], LIMIT, None, ALU.min)
                    ins.then_inc(s_g, 1)
                with dve.If(both >= 1):
                    one(2)
                with dve.Else():
                    one(1)

            def hidden(t, c, i, both):
                cols = slice(512 * i, 512 * (i + 1))

                def one(blocks):
                    wait_multiplied(dve, t, c)
                    if not (isinstance(t, int) and t == 0):
                        dve.wait_ge(s_ht, t)
                    for b in range(blocks):
                        ins = nc.vector.tensor_scalar(hid[:, b, cols], PS[:, 2 + b, :], LIMIT, -LIMIT,
                                                      ALU.min, ALU.max)
                    ins.then_inc(s_upr, 1)
                    dve.wait_ge(s_sg, 2 * t + i + 1)
                    nc.vector.tensor_tensor(glu[:, 0:blocks, :], glu[:, 0:blocks, :], sgm[:, 0:blocks, :],
                                            ALU.mult).then_inc(s_hid, 1)
                    dve.wait_ge(s_hid, 4 * t + 2 * i + 1)
                    dve.wait_ge(s_upr, 2 * t + i + 1)
                    nc.vector.scalar_tensor_tensor(out=hid[:, 0:blocks, cols], in0=hid[:, 0:blocks, cols],
                                                   scalar=1.0, in1=glu[:, 0:blocks, :], op0=ALU.add,
                                                   op1=ALU.mult).then_inc(s_hid, 1)
                with dve.If(both >= 1):
                    one(2)
                with dve.Else():
                    one(1)

            used_ = dve.value_load(usedb[0:1, 0:1], min_val=1, max_val=NVIS)
            bias_selector(0)
            nc.vector.memset(glu[:, 1, 0:1], 0.0)
            tokens_lo(0)
            both0 = two_blocks(0)
            for c in (4, 5, 7, 8):
                lo_by_vector(0, c)
            clamp_glu(0, 5, 0, both0, first=True)
            lo_by_vector(0, 10)
            hidden(0, 7, 0, both0)
            lo_by_vector(0, 11)
            clamp_glu(0, 9, 1, both0)
            lo_by_vector(1, 1)
            lo_by_vector(1, 2)
            wait_multiplied(dve, 0, 11)
            bias_selector(1)
            hidden(0, 11, 1, both0)
            tokens_lo(1)
            hidden_lo(0, both0)
            with dve.Fori(1, NVIS + 1) as t:
                with dve.If(t <= used_):
                    both = two_blocks(t)
                    lo_by_vector(t, 4)
                    clamp_glu(t, 1, 0, both)
                    lo_by_vector(t, 5)
                    hidden(t, 3, 0, both)
                    lo_by_vector(t, 7)
                    lo_by_vector(t, 8)
                    clamp_glu(t, 5, 1, both)
                    lo_by_vector(t, 10)
                    wait_multiplied(dve, t, 7)
                    bias_selector(t + 1)
                    hidden(t, 7, 1, both)
                    lo_by_vector(t, 11)
                    tokens_lo(t + 1)
                    lo_by_vector(t + 1, 1)
                    hidden_lo(t, both)
                    lo_by_vector(t + 1, 2)
            def final(t):
                dve.wait_ge(s_fv, 2 * t + 2)
                if t >= 2:
                    dve.wait_ge(s_out[t % 2], 16 * (t // 2))
                nc.vector.scalar_tensor_tensor(out=fo[:, t % 2, :], in0=xres[:, t, :], scalar=st8[:, 3, t:t + 1],
                                               in1=fgb[:], op0=ALU.mult, op1=ALU.mult).then_inc(s_fo, 1)

            def root(t):
                dve.wait_ge(s_fa, 2 * t + 1)
                nc.vector.tensor_scalar(st8[:, 1, t:t + 1], st8[:, 0, t:t + 1], 1.0 / D, RMS_EPS, ALU.mult,
                                        ALU.add).then_inc(s_fv, 1)
                dve.wait_ge(s_fa, 2 * t + 2)
                nc.vector.reciprocal(st8[:, 3, t:t + 1], st8[:, 2, t:t + 1]).then_inc(s_fv, 1)

            dve.wait_ge(s_ffg, 16)
            for t in range(TT):
                for k in range(TOPK):
                    i = TOPK * t + k
                    dve.wait_ge(s_yg[i % 8], 16 * (i // 8 + 1))
                    if k:
                        dve.wait_ge(s_ac, i)
                    nc.vector.scalar_tensor_tensor(out=xres[:, t, :], in0=yg[:, i % 8, :], scalar=Gt[:, t, k:k + 1],
                                                   in1=xres[:, t, :], op0=ALU.mult, op1=ALU.add).then_inc(s_ac, 1)
                if t:
                    root(t - 1)
                    final(t - 1)
            root(TT - 1)
            final(TT - 1)

        @block.tensor
        def _(pe):
            pe.wait_ge(s_const, 2)
            pe.wait_ge(s_par, 10 * 16)
            pe.transpose(PS[:, 6, 0:NPV], PVr[0:NPV, :], ident[0:NPV, 0:NPV]).then_inc(s_pvt, 1)
            pe.transpose(PS[:, 7, 0:TAPS * CT], CWr[:], ident[0:TAPS * CT, 0:TAPS * CT]).then_inc(s_pvt, 1)
            pe.wait_ge(s_pvc, 2)

            def norm_turn(n, tiles):
                N = norms[n]
                for t in range(tiles):
                    pe.wait_ge(N["scaled"], t + 1)
                    if t >= 4:
                        pe.wait_ge(N["drained"], 2 * (t - 3))
                    for b in range(2):
                        for k in range(4):
                            ins = pe.transpose(PS[:, 2 * (t % 4) + b, P * k:P * (k + 1)],
                                               XN[:, t % 2, P * (4 * b + k):P * (4 * b + k + 1)], ident[:])
                        ins.then_inc(N["turned"], 1)
                pe.wait_ge(N["drained"], 2 * tiles)

            g = 0
            n = 0

            def split_group(n, out, weights_move, w, rows):
                if n >= 8:
                    pe.wait_ge(s_dr["in"], n - 7)
                for k in range(KT):
                    wh, wl = wiH[g % 2][:, k, w], wiL[:, slot_of[g], k, w]
                    xh, xl = xH[:, k, rows], (xL[0][:, k, rows] if k < 6 else xL[1][:, k - 6, rows])
                    for i, (a, b) in enumerate(((wh, xh), (wh, xl), (wl, xh))):
                        lhs, rhs = (b, a) if weights_move else (a, b)
                        ins = pe.matmul(out, lhs, rhs, start=(k == 0 and i == 0), stop=(k == KT - 1 and i == 2))
                ins.then_inc(s_mm["in"], 1)

            def chunk_T(fts=2):
                nonlocal g, n
                pe.wait_ge(s_dlp, g + 1)
                for ft in range(fts):
                    for th in range(2):
                        split_group(n, bank_groups(n), False, slice(P * ft, P * (ft + 1)),
                                    slice(512 * th, 512 * (th + 1)))
                        n += 1
                g += 1

            def chunk_rows():
                nonlocal g, n
                pe.wait_ge(s_dlp, g + 1)
                for t in range(TT):
                    split_group(n, bank_groups(n, 256), True, slice(0, 256), slice(P * t, P * (t + 1)))
                    n += 1
                g += 1

            norm_turn("m", MT)
            norm_turn("x", TT)

            def memory_chunk(c):
                nonlocal g
                pe.wait_ge(s_ring[slot_of[g]], 16 * fills[g])
                for i in range(2):
                    m = 2 * c + i
                    if m >= 4:
                        pe.wait_ge(s_dr["mem"], m - 3)
                    for k in range(KT):
                        w = ring[:, slot_of[g], k, :]
                        if c < 4:
                            lhs, rhs = w[:, P * i:P * (i + 1)], mT[:, k, :]
                        else:
                            lhs, rhs = mT[:, k, P * i:P * (i + 1)], w
                        ins = pe.matmul(PS[:, 4 + m % 4, 0:256], lhs, rhs, start=(k == 0), stop=(k == KT - 1))
                    ins.then_inc(s_mm["mem"], 1)
                g += 1

            n = 0
            chunk_T(fts=1)
            for c in range(6):
                chunk_T()
            for c in range(4):
                chunk_rows()
            pe.wait_ge(s_dr["in"], 58)

            pe.wait_ge(s_cv, TAPS * CT)
            for th in range(2):
                for c in range(CT):
                    ins = pe.matmul(PS[:, th, :], ones[:], yT[:, c, 512 * th:512 * (th + 1)],
                                    start=(c == 0), stop=(c == CT - 1))
                ins.then_inc(s_lnp, 1)
            pe.wait_ge(s_lna, CT)
            for th in range(2):
                for c in range(CT):
                    ins = pe.matmul(PS[:, 2 + th, :], ones[:], o_gla[:, 2 * c + th, :],
                                    start=(c == 0), stop=(c == CT - 1))
                ins.then_inc(s_lnp, 1)
            pe.wait_ge(s_lnv, 10)

            for p in range(2):
                if p:
                    pe.wait_ge(s_oe, 16 * p)
                for i in range(4):
                    d, th = i // 2, i % 2
                    pe.matmul(PS[:, i, :], W2[:, d, P * p:P * (p + 1)], gT[:, 512 * th:512 * (th + 1)],
                              start=True, stop=True).then_inc(s_z, 1)
                if p:
                    pe.wait_ge(s_st, 14 * p)
                memory_chunk(4 * p)
                memory_chunk(4 * p + 1)
                for l in range(8):
                    L = 8 * p + l
                    if l == 0:
                        pe.wait_ge(s_zmin, 4 * (p + 1))
                        pe.wait_ge(s_zabs, 4 * (p + 1))
                    else:
                        pe.wait_ge(s_kq, 9 * p + l)
                        if l >= 2:
                            pe.wait_ge(s_sel, 4 * (L - 1))
                    K_, Q_ = (kT[:, p, :], qT[:, p, :]) if l == 0 else (
                        (KQ, KQ2)[(l - 1) % 2][:, i, :] for i in range(2))
                    for b in range(4):
                        hh, half = b // 2, b % 2
                        for w in range(4):
                            a = slice(P * (4 * half + w), P * (4 * half + w + 1))
                            hp = slice(GDK * hh, GDK * (hh + 1))
                            ins = pe.matmul(PS[:, 4 * (L % 2) + b, P * w:P * (w + 1)], K_[hp, a], Q_[hp, a],
                                            start=True, stop=True)
                        ins.then_inc(s_gram, 1)
                    if l == 0:
                        memory_chunk(4 * p + 2)
                        memory_chunk(4 * p + 3)
                        pe.wait_ge(s_dr["mem"], 8 * (p + 1))
                pe.wait_ge(s_kq, 9 * p + 8)
                pe.wait_ge(s_sel, 32 * (p + 1))
                for b in range(4):
                    for i in range(4):
                        m = 4 * b + i
                        ins = pe.transpose(PS[:, b, P * i:P * (i + 1)],
                                           KQ2[:, m // TT, P * (m % TT):P * (m % TT + 1)], ident[:])
                    ins.then_inc(s_ket, 1)
                pe.wait_ge(s_kev, 4 * (p + 1))
                for i in range(14):
                    d = i % 2
                    w = i // 2 if d == 0 else TT - 1 - i // 2
                    if i >= 4:
                        pe.wait_ge(s_st, 14 * p + i - 3)
                    m = TT * d + w
                    pe.matmul(PS[:, 4 + i % 4, 0:256], KEt[:, m // 4, P * (m % 4):P * (m % 4 + 1)],
                              v_tm[:, w, 256 * p:256 * (p + 1)], start=True, stop=True).then_inc(s_U, 1)
                pe.wait_ge(s_kq, 9 * p + 9)
                pe.wait_ge(s_st, 14 * (p + 1))
                for i in range(16):
                    w, hh = i // 2, i % 2
                    h = 2 * p + hh
                    if i >= 4:
                        pe.wait_ge(s_oe, 16 * p + i - 3)
                    o = PS[:, i % 4, 0:P]
                    hp = slice(GDK * hh, GDK * (hh + 1))
                    tw = slice(P * w, P * (w + 1))
                    pe.matmul(o, Ssc[:, hh, w, :], v_tm[:, w, P * h:P * (h + 1)], start=True, stop=False)
                    pe.matmul(o, KQ[hp, 0, tw], ST[hp, 0, w, :], start=False, stop=False)
                    pe.matmul(o, KQ[hp, 1, tw], ST[hp, 1, w, :], start=False, stop=True).then_inc(s_op, 1)
            pe.wait_ge(s_oe, 32)
            for b in range(2):
                pe.wait_ge(s_ov, 4 + 2 * b)
                for c in range(CT):
                    for i in range(4):
                        ins = pe.transpose(PS[:, 2 * c + b, P * i:P * (i + 1)],
                                           o_gla[:, 4 * b + i, P * c:P * (c + 1)], ident[:])
                    ins.then_inc(s_at, 1)
            pe.wait_ge(s_al, 8)
            pe.wait_ge(s_yl, 2)
            for c in range(4):
                pe.wait_ge(s_dlp, N_IN + c + 1)
                for t in range(TT):
                    n = TT * c + t
                    if n >= 8:
                        pe.wait_ge(s_dr["out"], n - 7)
                    tile = slice(P * t, P * (t + 1))
                    for k in range(KT):
                        hi = aH[:, k, tile] if k < CT else yH[k // 2 - 2][:, k % 2, tile]
                        lo = aL[:, k, tile] if k < CT else yL[:, k - CT, tile]
                        wh, wl = wuH[c % 2][:, k, :], ringL[:, slot_of[g], k, :]
                        for i, (a, b) in enumerate(((hi, wh), (hi, wl), (lo, wh))):
                            ins = pe.matmul(bank_groups(n, 256), a, b, start=(k == 0 and i == 0),
                                            stop=(k == KT - 1 and i == 2))
                    ins.then_inc(s_mm["out"], 1)
                g += 1
            pe.wait_ge(s_dr["out"], 32)
            norm_turn("y", TT)
            for c in range(4):
                pe.wait_ge(s_dlv, c + 1)
                slot = slot_of[g]
                for i in range(4):
                    n = 4 * c + i
                    ft, th = i // 2, i % 2
                    if n >= 8:
                        pe.wait_ge(s_dr["q"], n - 7)
                    w, rows = slice(P * ft, P * (ft + 1)), slice(512 * th, 512 * (th + 1))
                    for k in range(KT):
                        wh, wl = wqH[c % 2][:, k, w], ringL[:, slot, k, w]
                        xh, xl = hH[:, k, rows], hL[k // 4][:, k % 4, rows]
                        pe.matmul(bank_groups(n), wh, xh, start=(k == 0), stop=False)
                        pe.matmul(bank_groups(n), wh, xl, start=False, stop=False)
                        ins = pe.matmul(bank_groups(n), wl, xh, start=False, stop=(k == KT - 1))
                    ins.then_inc(s_mm["q"], 1)
                g += 1
            pe.wait_ge(s_dr["q"], 16)
            for h in range(XH):
                def turn(t):
                    i = TT * h + t
                    pe.wait_ge(s_sv, normalised(i))
                    if i >= 1:
                        pe.wait_ge(s_pc, i)
                    for m in range(MT):
                        ins = pe.transpose(PS[:, 3, P * m:P * (m + 1)], pr[:, i % 4, P * m:P * (m + 1)],
                                           ident[:])
                    ins.then_inc(s_pt, 1)

                for t in range(TT):
                    i = TT * h + t
                    if i >= 3:
                        pe.wait_ge(s_pe, i - 2)
                    for k in range(2):
                        ins = pe.matmul(score_bank(i), qxT[:, 2 * h + k, P * t:P * (t + 1)],
                                        kx[:, 2 * h + k, :], start=(k == 0), stop=(k == 1))
                    ins.then_inc(s_sc, 1)
                    if t >= 2:
                        turn(t - 2)
                turn(TT - 2)
                turn(TT - 1)
                pe.wait_ge(s_pc, TT * (h + 1))
                if h:
                    pe.wait_ge(s_axl, 4 * h)
                for b in range(4):
                    ft, th = b // 2, b % 2
                    for m in range(MT):
                        ins = pe.matmul(PS[:, 4 + b, :], vx[:, m, XDH * h + P * ft:XDH * h + P * (ft + 1)],
                                        pT[:, h % 2, m, 512 * th:512 * (th + 1)], start=(m == 0), stop=(m == 1))
                    ins.then_inc(s_av, 1)
            pe.wait_ge(s_axl, 16)
            for c in range(4):
                pe.wait_ge(s_dlv, 4 + c + 1)
                for t in range(TT):
                    n = TT * c + t
                    if n >= 8:
                        pe.wait_ge(s_dr["o"], n - 7)
                    tile = slice(P * t, P * (t + 1))
                    for k in range(KT):
                        for i, (a, b) in enumerate(((oxH, woH), (oxH, woL), (oxL, woH))):
                            ins = pe.matmul(bank_groups(n, 256), a[:, k, tile], b[c % 2][:, k, :],
                                            start=(k == 0 and i == 0), stop=(k == KT - 1 and i == 2))
                    ins.then_inc(s_mm["o"], 1)
            pe.wait_ge(s_dr["o"], 32)

            def router(t):
                pe.wait_ge(s_h3e, 2 * (t + 1))
                if t >= 2:
                    pe.wait_ge(s_lg, t - 1)
                if t == 0:
                    pe.wait_ge(s_rpar, 3 * 16)
                for k in range(KT):
                    ins = pe.matmul(PS[:, 4 + t % 2, 0:E], h3T[:, t % 2, k, :], rw[:, k, :],
                                    start=(k == 0), stop=(k == KT - 1))
                ins.then_inc(s_lgp, 1)

            for t in range(TT):
                pe.wait_ge(norms["z"]["scaled"], t + 1)
                if t >= 2:
                    pe.wait_ge(s_h3e, 2 * (t - 1))
                for b in range(2):
                    for k in range(4):
                        ins = pe.transpose(PS[:, 2 * (t % 2) + b, P * k:P * (k + 1)],
                                           h3[:, t, P * (4 * b + k):P * (4 * b + k + 1)], ident[:])
                    ins.then_inc(norms["z"]["turned"], 1)
                if t:
                    router(t - 1)
            router(TT - 1)
            pe.wait_ge(s_rt, RT_M)
            pe.wait_ge(s_rmi, 2)
            for t in range(TT):
                o = PS[:, 6, E * t:E * (t + 1)]
                ins = pe.matmul(o, beforeb[:], Mb[:, t, :], start=True, stop=(t == 0))
                for j in range(t):
                    ins = pe.matmul(o, onesb[:], Mb[:, j, :], start=False, stop=(j == t - 1))
            ins.then_inc(s_rk, 1)
            for t in range(TT):
                ins = pe.matmul(PS[:, 7, 0:E], onesb[:], Mb[:, t, :], start=(t == 0), stop=(t == TT - 1))
            ins.then_inc(s_rk, 1)
            pe.wait_ge(s_rt, RT_GD)
            pe.wait_ge(s_h3e, 2 * TT)
            for b in range(2):
                for i in range(4):
                    ins = pe.transpose(PS[0:E, b, P * i:P * (i + 1)], GD[:, 4 * b + i, :], ident[:])
                ins.then_inc(s_gdt, 1)
            def down_bias(i):
                if i >= 4:
                    pe.wait_ge(s_bdr, i - 3)
                t, b = i // 2, i % 2
                pe.matmul(PS[:, i % 4, :], GDT[:, P * t:P * (t + 1)], bdn[:, 512 * b:512 * (b + 1)],
                          start=True, stop=True).then_inc(s_bd, 1)

            pe.wait_ge(s_gde, 2)
            pe.wait_ge(s_bld, 4 * 16)
            for i in range(4):
                down_bias(i)
            pe.wait_ge(s_lg, TT)
            for t in range(TT):
                pe.wait_ge(s_oh, t + 2)
                for k in range(TOPK):
                    ins = pe.matmul(PS[:, 4, 0:NB], rowhot[:, t % 2, k, :], blkhot[:, TOPK * t + k, :],
                                    start=(t == 0 and k == 0), stop=(t == TT - 1 and k == TOPK - 1))
                ins.then_inc(s_tm, 1)
            for i in range(4, 2 * TT):
                down_bias(i)
            pe.wait_ge(s_tab, 1)
            pe.wait_ge(s_bup, 8)

            def two_blocks(t):
                return pe.value_load(VT[0:1, 2, bass.ds(t, 1)], min_val=0, max_val=1)

            def turn(src, blocks, done):
                for b in range(blocks):
                    for k in range(KT):
                        ins = pe.transpose(PS[:, 4 + 2 * b + k // 4, P * (k % 4):P * (k % 4 + 1)],
                                           src[:, b, P * k:P * (k + 1)], ident[:])
                ins.then_inc(done, 1)

            def turn_tokens(t, both):
                pe.wait_ge(s_xsl, 32 * (t + 1))
                with pe.If(both >= 1):
                    turn(xs, 2, s_xt)
                with pe.Else():
                    turn(xs, 1, s_xt)

            def turn_hidden(t, both):
                pe.wait_ge(s_hid, 4 * t + 4)
                pe.wait_ge(s_xlo, t + 2)
                with pe.If(both >= 1):
                    turn(hid, 2, s_ht)
                with pe.Else():
                    turn(hid, 1, s_ht)

            def products(i, blocks, hi, lo, k0, slot, start, stop):
                for kk in range(4):
                    k = k0 + kk
                    for b in range(blocks):
                        o = PS[:, 2 * (i % 2) + b, :]
                        pe.matmul(o, hi[:, b, k, :], whi[:, slot, kk, :], start=start and kk == 0, stop=False)
                        pe.matmul(o, hi[:, b, k, :], wlo[:, slot, kk, :], start=False, stop=False)
                        ins = pe.matmul(o, lo[:, b, k, :], whi[:, slot, kk, :], start=False,
                                        stop=stop and kk == 3)
                ins.then_inc(s_wmm, 1)

            def up(t, both, c0):
                def all_groups(blocks):
                    for i in range(4):
                        if i < 2:
                            if c0 == 0:
                                pe.wait_ge(s_yev, 2 * t - 1 + i)
                        elif i == 2:
                            pe.wait_ge(s_g, 2 * t + 1)
                        else:
                            pe.wait_ge(s_upr, 2 * t + 1)
                        for b in range(blocks):
                            pe.matmul(PS[:, 2 * (i % 2) + b, :], SEL[:], bup[:, UPCOL[i]:UPCOL[i] + 512],
                                      start=True, stop=False)
                        for half in range(2):
                            c = c0 + 2 * i + half
                            wait_lo(pe, t, c)
                            products(i, blocks, xhi, xlo, 4 * half, chunk_slot(c, NSPL), False, half == 1)
                pe.wait_ge(s_xlo, t + 1)
                pe.wait_ge(s_bsel, t + 1)
                with pe.If(both >= 1):
                    all_groups(2)
                with pe.Else():
                    all_groups(1)

            def down(t, both):
                def all_groups(blocks):
                    for i in range(2):
                        pe.wait_ge(s_g if i == 0 else s_upr, 2 * t + 2)
                        for half in range(2):
                            c = 8 + 2 * i + half
                            wait_lo(pe, t, c)
                            products(i, blocks, hhi, hlo, 4 * half, chunk_slot(c, NSPL), half == 0, half == 1)
                pe.wait_ge(s_hlo, t)
                with pe.If(both >= 1):
                    all_groups(2)
                with pe.Else():
                    all_groups(1)

            used_ = pe.value_load(usedb[0:1, 0:1], min_val=1, max_val=NVIS)
            both0 = two_blocks(0)
            turn_tokens(0, both0)
            up(0, both0, 4)
            pe.wait_ge(s_xlo, 1)
            turn_tokens(1, two_blocks(1))
            turn_hidden(0, both0)
            with pe.Fori(1, NVIS + 1) as t:
                with pe.If(t <= used_):
                    both, both_last, both_next = two_blocks(t), two_blocks(t - 1), two_blocks(t + 1)
                    up(t, both, 0)
                    pe.wait_ge(s_hlo, t)
                    turn_tokens(t + 1, both_next)
                    down(t, both_last)
                    turn_hidden(t, both)
                    pe.wait_ge(s_hlo, t)


_INS = ["x", "mem", "norm_mix_g", "w_in", "gate_w2_fwd", "gate_b_fwd", "gate_w2_bwd", "gate_b_bwd",
        "gla_norm_g", "conv_w", "conv_b", "conv_ln_g", "conv_ln_b", "w_out", "norm_xattn_g", "norm_mem_g",
        "xattn_wq", "xattn_wk", "xattn_wv", "xattn_wo", "norm_ffn_g", "router_w", "router_b", "exp_w_up",
        "exp_b_up", "exp_w_down", "exp_b_down", "final_norm_g"]


def kernel(**inputs):
    import numpy as np
    from concourse import bacc
    from concourse.bass_utils import run_bass_kernel_spmd

    nc = bacc.Bacc("TRN2", target_bir_lowering=False, num_devices=1)
    arrays, aps = {}, {}
    for name in _INS:
        a = np.ascontiguousarray(inputs[name])
        arrays["in_" + name] = a
        aps[name] = nc.dram_tensor("in_" + name, a.shape, mybir.dt.from_np(a.dtype), kind="ExternalInput").ap()
    aps["out"] = nc.dram_tensor("out_y", (1, S, D), F, kind="ExternalOutput").ap()
    build(nc, aps)
    r = run_bass_kernel_spmd(nc, [arrays], core_ids=[0])
    return r.results[0]["out_y"]
```
